# Optimizing a Trainium2 kernel written in Bass

```python
import math
import jax, jax.numpy as jnp
from jax import lax
import numpy as np

D_MODEL = 1024
BATCH = 1
SEQ = 256
DEPTH = 2

CHUNK = 64
BLOCK = 128
N_META = 16
PAD_FRONT = BLOCK - N_META
HEAD_DIM = 64
SB_WIDTH = D_MODEL // 2
SB_HEADS = SB_WIDTH // HEAD_DIM
RWKV_WIDTH = D_MODEL // 2
RWKV_HEADS = RWKV_WIDTH // HEAD_DIM
DECAY_RANK = max(32, round(1.8 * D_MODEL ** 0.5 / 32) * 32)
AAA_RANK = max(32, round(1.8 * D_MODEL ** 0.5 / 32) * 32)
MV_RANK = max(32, round(1.3 * D_MODEL ** 0.5 / 32) * 32)
GATE_RANK = max(32, round(0.6 * D_MODEL ** 0.8 / 32) * 32)
RWKV_COLS = 3 * RWKV_WIDTH + DECAY_RANK + AAA_RANK + GATE_RANK
RWKV_SPLITS = (RWKV_WIDTH, RWKV_WIDTH + DECAY_RANK, 2 * RWKV_WIDTH + DECAY_RANK,
               3 * RWKV_WIDTH + DECAY_RANK, 3 * RWKV_WIDTH + DECAY_RANK + AAA_RANK)
RWKV_GN_EPS = 64e-5
SWA_Q_HEADS = 8
SWA_KV_HEADS = 2
SWA_GROUPS = SWA_Q_HEADS // SWA_KV_HEADS
SWA_WIDTH = SWA_Q_HEADS * HEAD_DIM
SWA_KV_WIDTH = SWA_KV_HEADS * HEAD_DIM
WINDOW = 128
WINDOW_CHUNKS = WINDOW // CHUNK
N_REL_BUCKETS = 32
REL_MAX_DIST = 128
N_BRANCH = 3
IN_SPLITS = (3 * SB_WIDTH, 3 * SB_WIDTH + RWKV_COLS, 3 * SB_WIDTH + RWKV_COLS + SWA_WIDTH + 2 * SWA_KV_WIDTH)
N_IN = IN_SPLITS[2] + N_BRANCH * D_MODEL
D_FF = (D_MODEL * 7) // 2
N_EXPERTS = 8
TOP_K = 2
N_DENSE = (DEPTH + 1) // 2
N_MOE = DEPTH // 2
N_VRES = DEPTH - 1
RMS_EPS = 1e-6
NEG_INF = -1e30

kernel_name = "hybrid_sb_rwkv7_swa_moe_trunk"

def rms_norm(x, g):
    xf = x.astype(jnp.float32)
    y = xf * lax.rsqrt(jnp.mean(xf * xf, axis=-1, keepdims=True) + RMS_EPS)
    return (y * g.astype(jnp.float32)).astype(x.dtype)

def shift_right(t):
    return jnp.pad(t, ((0, 0), (1, 0), (0, 0)))[:, :-1]

def chunk_id(pos):
    return jnp.where(pos >= BLOCK, 1 + (pos - BLOCK) // CHUNK, 0)

def t5_bucket(n):
    n = jnp.maximum(n, 0)
    max_exact = N_REL_BUCKETS // 2
    nf = jnp.maximum(n, 1).astype(jnp.float32)
    large = max_exact + (jnp.log(nf / max_exact) / math.log(REL_MAX_DIST / max_exact)
                         * (N_REL_BUCKETS - max_exact)).astype(jnp.int32)
    large = jnp.minimum(large, N_REL_BUCKETS - 1)
    return jnp.where(n < max_exact, n, large)

def stick_breaking_attention(q, k, v):
    P = q.shape[1]
    scale = HEAD_DIM ** -0.5
    outs = []
    for b in range(P // BLOCK):
        kl = (b + 1) * BLOCK
        z = jnp.einsum('bihd,bjhd->bhij', q[:, b * BLOCK:kl], k[:, :kl]).astype(jnp.float32) * scale
        tpos = b * BLOCK + jnp.arange(BLOCK)
        spos = jnp.arange(kl)
        mask = (spos[None, :] < tpos[:, None]) & (spos[None, :] >= PAD_FRONT)
        log_rest = jnp.where(mask, jax.nn.log_sigmoid(-z), 0.0)
        after = lax.cumsum(log_rest, axis=3, reverse=True) - log_rest
        attn = jnp.where(mask, jnp.exp(jax.nn.log_sigmoid(z) + after), 0.0)
        outs.append(jnp.einsum('bhij,bjhd->bihd', attn.astype(v.dtype), v[:, :kl]))
    return jnp.concatenate(outs, axis=1)

def rwkv7_recurrence(r, w, k, v, kk, a):
    B, L, H, N = r.shape

    def step(S, inp):
        r_t, w_t, k_t, v_t, kk_t, a_t = inp
        sa = jnp.einsum('bhvk,bhk->bhv', S, -kk_t)
        S = (S * w_t[:, :, None, :] + sa[..., None] * (kk_t * a_t)[:, :, None, :]
             + v_t[..., None] * k_t[:, :, None, :])
        return S, jnp.einsum('bhvk,bhk->bhv', S, r_t)

    xs = tuple(jnp.moveaxis(t, 1, 0) for t in (r, w, k, v, kk, a))
    _, ys = lax.scan(step, jnp.zeros((B, H, N, N), jnp.float32), xs)
    return jnp.moveaxis(ys, 0, 1)

def rwkv7_time_mix(pb, xn, v_first, mu, w0, w2, a0, a2, g2, k_k, k_a, r_k, ln_g, ln_b, vres):
    B, L, _ = pb.shape
    f32 = jnp.float32
    pm = pb + (shift_right(pb) - pb) * mu
    r, xw, k, v, xa, xg = jnp.split(pm, RWKV_SPLITS, axis=-1)
    decay = jnp.exp(-jnp.exp(-jax.nn.softplus(-(w0 + jnp.tanh(xw) @ w2).astype(f32)) - 0.5))
    if vres is not None:
        mu_v, vw1, vw2, vb = vres
        xv = xn + (shift_right(xn) - xn) * mu_v
        v = v + (v_first - v) * jax.nn.sigmoid(vb + (xv @ vw1) @ vw2)
    a = jax.nn.sigmoid(a0 + xa @ a2)
    g = jax.nn.sigmoid(xg) @ g2
    heads = lambda t: t.reshape(B, L, RWKV_HEADS, HEAD_DIM).astype(f32)
    kk = heads(k * k_k)
    kk = kk / jnp.maximum(jnp.sqrt(jnp.sum(kk * kk, axis=-1, keepdims=True)), 1e-12)
    k = k * (1 + (a - 1) * k_a)
    rh, kh, vh, ah = heads(r), heads(k), heads(v), heads(a)
    y = rwkv7_recurrence(rh, heads(decay), kh, vh, kk, ah)
    mean = jnp.mean(y, axis=-1, keepdims=True)
    var = jnp.mean(jnp.square(y - mean), axis=-1, keepdims=True)
    y = ((y - mean) * lax.rsqrt(var + RWKV_GN_EPS)).reshape(B, L, RWKV_WIDTH) * ln_g + ln_b
    bonus = jnp.sum(rh * kh * r_k, axis=-1, keepdims=True) * vh
    y = (y + bonus.reshape(B, L, RWKV_WIDTH)) * g
    return y.astype(pb.dtype), v

def swa_sink_attention(q, k, v, k_meta, v_meta, rel_bias, sinks):
    B, P = q.shape[:2]
    nb = P // BLOCK
    scale = HEAD_DIM ** -0.5
    qb = q.reshape(B, nb, BLOCK, SWA_KV_HEADS, SWA_GROUPS, HEAD_DIM)

    def band(t):
        tp = jnp.pad(t, ((0, 0), (BLOCK, 0), (0, 0), (0, 0))).reshape(B, nb + 1, BLOCK, SWA_KV_HEADS, HEAD_DIM)
        return jnp.concatenate([tp[:, :-1], tp[:, 1:]], axis=2)

    kb, vb = band(k), band(v)
    s_band = jnp.einsum('bnikgd,bnjkd->bnkgij', qb, kb).astype(jnp.float32) * scale
    s_meta = jnp.einsum('bnikgd,bmkd->bnkgim', qb, k_meta).astype(jnp.float32) * scale
    qpos = (jnp.arange(nb) * BLOCK)[:, None] + jnp.arange(BLOCK)[None, :]
    kpos = (jnp.arange(nb) * BLOCK - BLOCK)[:, None] + jnp.arange(2 * BLOCK)[None, :]
    mpos = PAD_FRONT + jnp.arange(N_META)
    dc = chunk_id(qpos)[:, :, None] - chunk_id(kpos)[:, None, :]
    mask = (kpos[:, None, :] >= BLOCK) & (dc >= 0) & (dc < WINDOW_CHUNKS)

    def bias(dist):
        bt = rel_bias[t5_bucket(dist)].reshape(dist.shape + (SWA_KV_HEADS, SWA_GROUPS))
        return jnp.transpose(bt, (0, 3, 4, 1, 2)).astype(jnp.float32)

    s_band = jnp.where(mask[None, :, None, None], s_band + bias(qpos[:, :, None] - kpos[:, None, :])[None], NEG_INF)
    s_meta = s_meta + bias(qpos[:, :, None] - mpos[None, None, :])[None]
    sink = jnp.broadcast_to(sinks.reshape(SWA_KV_HEADS, SWA_GROUPS)[None, None, :, :, None, None].astype(jnp.float32),
                            s_band.shape[:-1] + (1,))
    p = jax.nn.softmax(jnp.concatenate([s_band, s_meta, sink], axis=-1), axis=-1)
    p_band = p[..., :2 * BLOCK].astype(v.dtype)
    p_meta = p[..., 2 * BLOCK:2 * BLOCK + N_META].astype(v.dtype)
    o = (jnp.einsum('bnkgij,bnjkd->bnikgd', p_band, vb)
         + jnp.einsum('bnkgim,bmkd->bnikgd', p_meta, v_meta))
    return o.reshape(B, P, SWA_WIDTH)

def swiglu(x, wg, wu, wd):
    return (jax.nn.silu(x @ wg) * (x @ wu)) @ wd

def moe_swiglu(x, router, wg, wu, wd):
    logits = (x @ router).astype(jnp.float32)
    top_val, top_idx = lax.top_k(logits, TOP_K)
    top_w = jax.nn.softmax(top_val, axis=-1)
    gates = jnp.sum(jax.nn.one_hot(top_idx, N_EXPERTS, dtype=jnp.float32) * top_w[..., None], axis=-2)
    y = jnp.zeros_like(x)
    for e in range(N_EXPERTS):
        y = y + gates[..., e:e + 1].astype(x.dtype) * swiglu(x, wg[e], wu[e], wd[e])
    return y

def setup_inputs(seed: int = 0) -> dict:
    key = jax.random.key(seed)
    ks = iter(jax.random.split(key, 48))
    nrm = lambda shape, s: jax.random.normal(next(ks), shape, jnp.float32) * s
    uni = lambda shape, lo, hi: jax.random.uniform(next(ks), shape, jnp.float32, lo, hi)
    gain = lambda shape: 1.0 + nrm(shape, 0.05)
    D, RW = D_MODEL, RWKV_WIDTH
    return {
        "x": nrm((BATCH, SEQ, D), 1.0),
        "meta_tokens": nrm((N_META, D), 1.0),
        "rel_bias": nrm((N_REL_BUCKETS, SWA_Q_HEADS), 0.5),
        "norm_mix": gain((DEPTH, D)),
        "w_in": nrm((DEPTH, D, N_IN), D ** -0.5),
        "tshift_mu": uni((DEPTH, RWKV_COLS), 0.0, 1.0),
        "rwkv_w0": uni((DEPTH, RW), -6.0, 0.0),
        "rwkv_w2": nrm((DEPTH, DECAY_RANK, RW), 0.5 * DECAY_RANK ** -0.5),
        "rwkv_a0": nrm((DEPTH, RW), 0.5),
        "rwkv_a2": nrm((DEPTH, AAA_RANK, RW), AAA_RANK ** -0.5),
        "rwkv_g2": nrm((DEPTH, GATE_RANK, RW), GATE_RANK ** -0.5),
        "rwkv_k_k": 0.85 + nrm((DEPTH, RW), 0.05),
        "rwkv_k_a": gain((DEPTH, RW)),
        "rwkv_r_k": nrm((DEPTH, RWKV_HEADS, HEAD_DIM), 0.1),
        "rwkv_ln_g": gain((DEPTH, RW)),
        "rwkv_ln_b": nrm((DEPTH, RW), 0.02),
        "vres_mu": uni((N_VRES, D), 0.0, 1.0),
        "vres_w1": nrm((N_VRES, D, MV_RANK), D ** -0.5),
        "vres_w2": nrm((N_VRES, MV_RANK, RW), MV_RANK ** -0.5),
        "vres_b": nrm((N_VRES, RW), 0.1),
        "sinks": nrm((DEPTH, SWA_Q_HEADS), 1.0),
        "w_proj_a": nrm((DEPTH, SB_WIDTH, D), SB_WIDTH ** -0.5),
        "w_proj_b": nrm((DEPTH, RW, D), RW ** -0.5),
        "w_proj_c": nrm((DEPTH, SWA_WIDTH, D), SWA_WIDTH ** -0.5),
        "w_out": nrm((DEPTH, D, D), D ** -0.5),
        "norm_ffn": gain((DEPTH, D)),
        "dense_w_gate": nrm((N_DENSE, D, D_FF), D ** -0.5),
        "dense_w_up": nrm((N_DENSE, D, D_FF), D ** -0.5),
        "dense_w_down": nrm((N_DENSE, D_FF, D), D_FF ** -0.5),
        "moe_router": nrm((N_MOE, D, N_EXPERTS), D ** -0.5),
        "moe_w_gate": nrm((N_MOE, N_EXPERTS, D, D_FF), D ** -0.5),
        "moe_w_up": nrm((N_MOE, N_EXPERTS, D, D_FF), D ** -0.5),
        "moe_w_down": nrm((N_MOE, N_EXPERTS, D_FF, D), D_FF ** -0.5),
        "norm_final": gain((D,)),
    }

def reference(x, meta_tokens, rel_bias, norm_mix, w_in, tshift_mu, rwkv_w0, rwkv_w2, rwkv_a0, rwkv_a2,
              rwkv_g2, rwkv_k_k, rwkv_k_a, rwkv_r_k, rwkv_ln_g, rwkv_ln_b, vres_mu, vres_w1, vres_w2, vres_b,
              sinks, w_proj_a, w_proj_b, w_proj_c, w_out, norm_ffn, dense_w_gate, dense_w_up, dense_w_down,
              moe_router, moe_w_gate, moe_w_up, moe_w_down, norm_final):
    B = x.shape[0]
    h = jnp.concatenate([jnp.broadcast_to(meta_tokens[None].astype(x.dtype), (B, N_META, D_MODEL)), x], axis=1)
    L = h.shape[1]
    pad = lambda t: jnp.pad(t, ((0, 0), (PAD_FRONT, 0), (0, 0), (0, 0)))
    v_first = None
    for i in range(DEPTH):
        xn = rms_norm(h, norm_mix[i])
        proj = xn @ w_in[i]
        pa, pb, pc, pg = jnp.split(proj, IN_SPLITS, axis=-1)
        qa, ka, va = [t.reshape(B, L, SB_HEADS, HEAD_DIM) for t in jnp.split(pa, 3, axis=-1)]
        ya = stick_breaking_attention(pad(qa), pad(ka), pad(va))[:, PAD_FRONT:].reshape(B, L, SB_WIDTH)
        vres = None if i == 0 else (vres_mu[i - 1], vres_w1[i - 1], vres_w2[i - 1], vres_b[i - 1])
        yb, v_b = rwkv7_time_mix(pb, xn, v_first, tshift_mu[i], rwkv_w0[i], rwkv_w2[i], rwkv_a0[i], rwkv_a2[i],
                                 rwkv_g2[i], rwkv_k_k[i], rwkv_k_a[i], rwkv_r_k[i], rwkv_ln_g[i], rwkv_ln_b[i], vres)
        if i == 0:
            v_first = v_b
        qc, kc, vc = jnp.split(pc, (SWA_WIDTH, SWA_WIDTH + SWA_KV_WIDTH), axis=-1)
        qc = qc.reshape(B, L, SWA_Q_HEADS, HEAD_DIM)
        kc = kc.reshape(B, L, SWA_KV_HEADS, HEAD_DIM)
        vc = vc.reshape(B, L, SWA_KV_HEADS, HEAD_DIM)
        yc = swa_sink_attention(pad(qc), pad(kc), pad(vc), kc[:, :N_META], vc[:, :N_META],
                                rel_bias, sinks[i])[:, PAD_FRONT:]
        ga, gb, gc = jnp.split(jax.nn.sigmoid(pg), N_BRANCH, axis=-1)
        merged = ga * (ya @ w_proj_a[i]) + gb * (yb @ w_proj_b[i]) + gc * (yc @ w_proj_c[i])
        h = h + merged @ w_out[i]
        hn = rms_norm(h, norm_ffn[i])
        j = i // 2
        if i % 2 == 0:
            h = h + swiglu(hn, dense_w_gate[j], dense_w_up[j], dense_w_down[j])
        else:
            h = h + moe_swiglu(hn, moe_router[j], moe_w_gate[j], moe_w_up[j], moe_w_down[j])
    return rms_norm(h, norm_final)[:, N_META:]


_drawn_inputs = setup_inputs


def setup_inputs(seed=0):
    import zlib

    import numpy as np

    out = dict(_drawn_inputs(seed))
    spreads = {}
    factors = {'rwkv_ln_b': 7.01, 'vres_b': 2.942, 'sinks': 8.0}
    for name, (base, spread) in spreads.items():
        noise = np.random.default_rng([zlib.crc32(name.encode()), seed]).standard_normal(out[name].shape)
        drawn = base * np.exp(spread * noise) if base else spread * noise
        out[name] = __import__('jax').numpy.asarray(drawn.astype(out[name].dtype))
    for name, factor in factors.items():
        out[name] = (out[name] * factor).astype(out[name].dtype)
    return out
```

```python
from contextlib import ExitStack

import numpy as np

import concourse.bass as bass
from concourse import mybir

F32 = mybir.dt.float32
I32 = mybir.dt.int32
U32 = mybir.dt.uint32
ALU = mybir.AluOpType
ACT = mybir.ActivationFunctionType
AX = mybir.AxisListType

P = 128
D = 1024
KT = D // P
SEQ, META = 256, 16
T = SEQ + META
DEPTH = 2
HD = 64
HALF = D // 2
NP_ = HALF // P
CH = 64
PADC = 48
TP = T + PADC
NCH = TP // CH
NXC = SEQ // CH
FF = 3584
FG = FF // 512
NE = 8
SLOTS = 128
N_IN = 7200
COL_R, COL_W, COL_K, COL_V, COL_A, COL_G = 1536, 2048, 2112, 2624, 3136, 3200
COL_CQ, COL_CK, COL_GATE = 3360, 3872, 4128
NBUCKET = 32
LINE = 336
LINE_TOP = T - 1
RING = 3
EPS = 1e-6
GN_EPS = 64e-5
DECAY_SCALE = -float(np.exp(-0.5))
QS = HD ** -0.5

CONST_COLS = {}
_at = 0
for _n, _w in (("ident", P), ("ones", P), ("headones", P), ("negsuffix", P), ("negones", P), ("negmask", P),
               ("before", P), ("sbmask", 432), ("level", 6 * P), ("strict", P), ("bd", P), ("incl", CH),
               ("stack", CH), ("reset", TP), ("iota", 2 * P), ("iota8", NE), ("bucket", LINE)):
    CONST_COLS[_n] = (_at, _w)
    _at += _w
NCONST = _at

PARAM_COLS = {}
_at = 0
for _n, _w in (("norm_mix", KT), ("norm_ffn", KT), ("mu_r", 4), ("mu_k", 4), ("mu_v", 4), ("mu_wa", 1),
               ("mu_g0", 1), ("mu_g1", 1), ("w0", 4), ("a0", 4), ("k_k", 4), ("k_a", 4), ("r_k", 4),
               ("ln_g", 4), ("ln_b", 4), ("vres_mu", KT), ("vres_b", 4), ("sink", 4), ("sink_meta", 2),
               ("norm_final", KT)):
    PARAM_COLS[_n] = (_at, _w)
    _at += _w
NPARAM = _at

PER_LAYER = dict(
    sq_done=2, sum_done=2, rstd_done=2,
    proj_done=32, proj_copied=32,
    z_done=8, sp_done=8, arg_done=8, at_done=8, ya_done=4, ya_copied=4,
    c_z=5, c_s=5, c_m=5, c_e=5, c_r=5, c_p=5, c_t=5, c_tc=5, c_y=5, c_yc=5, c_vt=1, c_vtc=1,
    w_mm=3, w_ev=3, w_in=1, v_mm=2, v_ev=2, k_sq=1, k_sum=1, k_rt=1, k_mul=1, b_pr=1, b_sum=1, b_bn=1,
    g_done=1, e_done=3, e_used=3,
    r_bd=5, r_mm=5, r_tt=5, r_lv=25, r_t=5, r_tc=5, r_p=25, r_pc=25, r_d=25, r_x=5, r_xc=5, r_u=5,
    r_uc=5, r_ust=5, r_ys=5, r_yc=5, r_s=5, r_cp=5, r_tr=5,
    n_m=1, n_d=1, n_sq=1, n_v=1, n_e=1, n_s=1,
    m_g=24, m_p=24, m_s=24, m_acc=24, o_mm=8, o_add=8,
)


def weight_chunks(w_in, w_a, w_b, w_c, w_out, dg, du, dd):
    out = []
    rows = lambda w: w.rearrange("(k p) n -> p k n", p=P)
    for l in range(DEPTH):
        wl = rows(w_in[l])

        def cols(name, c0, n):
            out.append((l, name, "k", [(slice(0, 4), 0, n, wl[:, 0:4, c0:c0 + n]),
                                       (slice(4, 8), 0, n, wl[:, 4:8, c0:c0 + n])]))

        cols("Aq", 0, 512)
        cols("Ak", 512, 512)
        cols("Av", 1024, 512)
        out.append((l, "Cq", "q", [(g, 0, 0, wl[:, :, COL_CQ + 256 * g:COL_CQ + 256 * (g + 1)]
                                    .rearrange("p k (j d) -> p k j d", j=4)) for g in range(2)]))
        cols("Ckv", COL_CK, 256)
        cols("Br", COL_R, 512)
        cols("Bk", COL_K, 512)
        cols("Bv", COL_V, 512)
        out.append((l, "Bx", "k", [(slice(0, 8), 0, 64, wl[:, :, COL_W:COL_W + 64]),
                                   (slice(0, 8), 64, 224, wl[:, :, COL_A:COL_A + 224])]))
        for b, wp in enumerate((w_a, w_b, w_c)):
            if b < 2:
                wr = rows(wp[l])
                out.append((l, f"P{b}", "w", [(slice(0, 2), 0, 0, wr[:, 0:2, :]), (slice(2, 4), 0, 0, wr[:, 2:4, :])]))
            else:
                wc = wp[l].rearrange("(g j d) n -> g d j n", g=2, j=4)
                out.append((l, "P2", "c", [(g, 0, 0, wc[g]) for g in range(2)]))
            for h in range(2):
                cols(f"G{b}{h}", COL_GATE + D * b + 512 * h, 512)
        wo = rows(w_out[l])
        for h in range(2):
            out.append((l, f"O{h}", "k", [(slice(0, 4), 0, 512, wo[:, 0:4, 512 * h:512 * h + 512]),
                                          (slice(4, 8), 0, 512, wo[:, 4:8, 512 * h:512 * h + 512])]))
        if l == 0:
            for f in range(FG):
                for nm, w in (("DG", dg), ("DU", du)):
                    wr = rows(w[0])
                    out.append((l, f"{nm}{f}", "k",
                                [(slice(0, 4), 0, 512, wr[:, 0:4, 512 * f:512 * f + 512]),
                                 (slice(4, 8), 0, 512, wr[:, 4:8, 512 * f:512 * f + 512])]))
            for f in range(FG):
                wr = rows(dd[0, 512 * f:512 * f + 512, :])
                out.append((l, f"DD{f}", "w", [(slice(0, 2), 0, 0, wr[:, 0:2, :]), (slice(2, 4), 0, 0, wr[:, 2:4, :])]))
    return out


def build_trunk(nc, x, meta, w_in, w_a, w_b, w_c, w_out, dg, du, dd, router, mg, mu_, md, w2, a2, g2, vw1, vw2,
                rel_bias, consts, params, out):
    chunks = weight_chunks(w_in, w_a, w_b, w_c, w_out, dg, du, dd)
    position = {(l, n): i for i, (l, n, _, _) in enumerate(chunks)}
    MOE0 = len(chunks)
    line = nc.dram_tensor("bias_line", (NE, CH, LINE), F32, kind="Internal").ap()

    with ExitStack() as ctx:
        def sb(name, shape, dt=F32):
            return ctx.enter_context(nc.sbuf_tensor(name, shape, dt))

        sems = {}

        def S(name):
            if name not in sems:
                sems[name] = ctx.enter_context(nc.semaphore(name))
            return sems[name]

        def at(name, l, i):
            assert 0 <= i < PER_LAYER[name], name
            return l * PER_LAYER[name] + i + 1

        ring = [sb(f"ring{i}", [P, 4096]) for i in range(RING)]
        hT = sb("hT", [P, KT, T])
        xn = sb("xn", [P, KT, T + 1])
        cst = sb("cst", [P, NCONST])
        prm = sb("prm", [P, DEPTH, NPARAM])
        wwa = sb("wwa", [P, HALF])
        wg0 = sb("wg0", [P, HALF])
        wg1 = sb("wg1", [32, HALF])
        vw1_sb = sb("vw1_sb", [P, KT, 32])
        vw2_sb = sb("vw2_sb", [32, HALF])
        router_sb = sb("router_sb", [P, KT, NE])
        relb = sb("relb", [NBUCKET, NE])
        lin = sb("lin", [NE, LINE])
        bias0 = sb("bias0", [P, 4, 80])
        biasb = sb("biasb", [P, 4, P])
        biasm = sb("biasm", [P, 3, 4, META])
        biasq = sb("biasq", [64, 2, META])
        yA = sb("yA", [P, NP_, T])
        yC = sb("yC", [P, NP_, T])
        VF = sb("VF", [P, NP_, TP])
        rstd = sb("rstd", [P, T])
        egc = sb("egc", [P, NP_, NCH])
        state = sb("state", [P, NP_, CH])
        small = sb("small", [P, 64])
        area1 = sb("area1", [P, 9216])
        area2 = sb("area2", [P, 12544])
        PS = ctx.enter_context(nc.psum_tensor("PS", [P, 8, 512], F32))

        def C(name, lo=0, n=None):
            o, w = CONST_COLS[name]
            return cst[:, o + lo:o + (w if n is None else lo + n)]

        def prm_col(l, name, i):
            o, w = PARAM_COLS[name]
            return prm[:, l, o + i:o + i + 1]

        def carve(area, specs):
            got, o = [], 0
            for shape in specs:
                n = int(np.prod(shape))
                v = area[:, o:o + n]
                if len(shape) == 2:
                    v = v.rearrange("p (a b) -> p a b", b=shape[1])
                if len(shape) == 3:
                    v = v.rearrange("p (a b c) -> p a b c", b=shape[1], c=shape[2])
                got.append(v)
                o += n
            assert o <= area.shape[1], (o, area.shape)
            return got

        (xin,) = carve(area1, [(3, D)])
        qA, kA, vA, uA, spA, atA = carve(area1, [(4, T), (4, 384), (3, 512), (2, 432), (2, 432), (2, 432)])
        qCm, qCx, kC, vC, vW, sC, mC, pTC, pTm = carve(
            area1, [(4, META), (NXC, 4, CH), (T,), (T,), (4, P), (4, 144), (32,), (4, P), (4, P)])
        (Bbd, Kbd, Hbd, VTbd, Vbd, Ubd, Sbd, BT, HT, TT, TI, PW, NTb, M2bd) = carve(area1, [(4, P)] * 14)[:14]
        AA, Vst, Xst, Ust = carve(area1[:, 14 * 512:], [(8, CH), (4, CH), (4, CH), (4, CH)])
        R, K, V, LW, G, AI, KK, DD, GT = carve(area2, [(4, TP)] * 9)
        (PX,) = carve(area2[:, 9 * 4 * TP:], [(3, TP)])
        Y, BN = LW, G
        (_, MG, SG, TMP) = carve(area2, [(4, TP), (KT, T), (2, T), (2, T)])
        (_, HF, SF) = carve(area2, [(KT, T), (28, T), (4, T)])
        (SQ,) = carve(area2, [(KT, T)])
        LWG, SV = G, KK
        SQ_v = area2[:, 6 * 4 * TP:6 * 4 * TP + KT * T].rearrange("p (a b) -> p a b", b=T)
        (_, hnT, XG, MS, MH, SEL, SELT, YE, MR) = carve(
            area2, [(KT, T), (2, D), (KT, SLOTS), (2, 512), (2, 512), (4, SLOTS), (SEQ,), (D,), (160,)])
        ostage = area2[:, 0:2 * D].rearrange("p (a n) -> p a n", a=2)

        n_linked = {}

        def link(eng, ins, name):
            n_linked[name] = n_linked.get(name, 0) + 1
            ins.then_inc(S(name), 1)
            eng.wait_ge(S(name), n_linked[name])

        ENGINES = ("pe", "act", "dve")
        stage_no = dict.fromkeys(ENGINES, 0)

        def end_stage(eng, who):
            stage_no[who] += 1
            eng.drain().then_inc(S(f"{who}_stage"), 1)
            for other in ENGINES:
                if other != who:
                    eng.wait_ge(S(f"{other}_stage"), stage_no[who])

        def bc(v, shape, axis):
            return v.unsqueeze(axis).broadcast_to(shape)

        N_SETUP = 13

        block = ctx.enter_context(nc.Block())

        landed_at = []
        total = [0] * RING
        for i, (_, _, kind, _) in enumerate(chunks):
            total[i % RING] += 256 if kind == "q" else 32
            landed_at.append(total[i % RING])
        landed_moe0 = list(total)

        MOE_ORDER = []
        for f in range(FG):
            MOE_ORDER.append(("g", f))
            if f:
                MOE_ORDER.append(("d", f - 1))
            MOE_ORDER.append(("u", f))
        MOE_ORDER.append(("d", FG - 1))
        assert len(MOE_ORDER) % RING == 0
        PER_BUF = len(MOE_ORDER) // RING

        def experts_stream(sp, pos0, again):
            with sp.Fori(0, NE) as e:
                for i, (kind, f) in enumerate(MOE_ORDER):
                    buf = ring[(pos0 + i) % RING]
                    w = {"g": mg, "u": mu_, "d": md}[kind]
                    if kind == "d":
                        src = w[0, e, 512 * f:512 * f + 512, :].rearrange("(k p) n -> p k n", p=P)
                        dst = buf[:, :].rearrange("p (k n) -> p k n", k=4)
                        halves = [(dst[:, 0:2], src[:, 0:2]), (dst[:, 2:4], src[:, 2:4])]
                    else:
                        src = w[0, e, :, 512 * f:512 * f + 512].rearrange("(k p) n -> p k n", p=P)
                        dst = buf[:, :].rearrange("p (k n) -> p k n", k=8)
                        halves = [(dst[:, 0:4], src[:, 0:4]), (dst[:, 4:8], src[:, 4:8])]
                    sp.wait_ge(S("chunk_used"), e * len(MOE_ORDER) + (pos0 + i - RING + 1))
                    for d_, s_ in halves:
                        sp.dma_start(d_, s_).then_inc(S(f"landed{(pos0 + i) % RING}"), 16)

        def overflow_branch(eng):
            eng.wait_ge(S("route_flag"), 1)
            flag = eng.value_load(small[0:1, 40:41].bitcast(I32), min_val=0, max_val=1)
            return eng.If(flag > 0)

        @block.sync
        def _(sp):
            for i, (l, name, kind, parts) in enumerate(chunks):
                buf = ring[i % RING]
                if i >= RING:
                    sp.wait_ge(S("chunk_used"), i - RING + 1)
                for a, c0, n, src in parts:
                    if kind == "k":
                        dst = buf[:, :].rearrange("p (k n) -> p k n", k=8)[:, a, c0:c0 + n]
                    elif kind == "w":
                        dst = buf[:, :].rearrange("p (k n) -> p k n", k=4)[:, a, :]
                    elif kind == "c":
                        dst = buf[64 * a:64 * a + 64, :].rearrange("p (k n) -> p k n", k=4)
                    else:
                        dst = buf[:, :].rearrange("p (k j g d) -> p k j g d", k=8, j=4, g=2)[:, :, :, a, :]
                    if kind == "q":
                        for k in range(KT):
                            sp.dma_start(dst[:, k], src[:, k]).then_inc(S(f"landed{i % RING}"), 16)
                    else:
                        sp.dma_start(dst, src).then_inc(S(f"landed{i % RING}"), 16)
            experts_stream(sp, MOE0, 0)
            with overflow_branch(sp):
                experts_stream(sp, MOE0 + 3 * FG * NE, 1)
            for h in range(2):
                sp.wait_ge(S("out_copied"), 2 * h + 2)
                sp.dma_start(out[0, h * P:(h + 1) * P, :], ostage[:, h, :]).then_inc(S("out_stored"), 16)
            sp.wait_ge(S("out_stored"), 32)

        @block.tensor
        def _(pe):
            used = [0]

            def chunk(l, name):
                i = position[(l, name)]
                assert i == used[0], (l, name, i, used[0])
                pe.wait_ge(S(f"landed{i % RING}"), landed_at[i])
                return ring[i % RING]

            def release(ins):
                ins.then_inc(S("chunk_used"), 1)
                used[0] += 1

            def k8(buf, n=512):
                return buf[:, :].rearrange("p (k n) -> p k n", k=8)[:, :, 0:n]

            def k4(buf):
                return buf[:, :].rearrange("p (k n) -> p k n", k=4)

            def spare():
                return pe.drain()

            def norm(l, which):
                pe.wait_ge(S("sq_done"), at("sq_done", l, which) if l < DEPTH else 2 * DEPTH + 1)
                for k in range(KT):
                    ins = pe.matmul(PS[:, 0, 0:T], C("ones"), SQ[:, k, :], start=(k == 0), stop=(k == KT - 1))
                ins.then_inc(S("sum_done"), 1)

            def project(l, tiles, n0):
                for i, (w, lo) in enumerate(tiles):
                    n = n0 + i
                    if i >= 8:
                        pe.wait_ge(S("proj_copied"), at("proj_copied", l, n - 8))
                    bank = i % 8
                    m = w(0).shape[1]
                    for k in range(KT):
                        ins = pe.matmul(PS[lo:lo + m, bank, 0:T], w(k), xn[:, k, 1:T + 1], start=(k == 0), stop=(k == KT - 1))
                    yield ins

            def column_tiles(l, name, widths, n0, first):
                buf = k8(chunk(l, name))
                c = 0
                for i, m in enumerate(widths):
                    n = n0 + i
                    if n >= 8 and first + i >= 8:
                        pe.wait_ge(S("proj_copied"), at("proj_copied", l, n - 8))
                    bank = (first + i) % 8
                    for k in range(KT):
                        ins = pe.matmul(PS[0:m, bank, 0:T], buf[:, k, c:c + m], xn[:, k, 1:T + 1],
                                        start=(k == 0), stop=(k == KT - 1))
                    c += m
                    ins.then_inc(S("proj_done"), 1)
                release(spare())

            pe.wait_ge(S("setup"), 16 * N_SETUP)
            for k in range(KT):
                pe.transpose(PS[:, k, 0:META], xin[0:META, 0, k * P:(k + 1) * P], C("ident")[0:META, 0:META])
                for t in range(2):
                    ins = pe.transpose(PS[:, k, META + t * P:META + (t + 1) * P], xin[:, 1 + t, k * P:(k + 1) * P], C("ident"))
                ins.then_inc(S("in_turned"), 1)
            pe.wait_ge(S("in_copied"), 1)
            pe.matmul(PS[0:NE, 0, 0:LINE], relb[:, :], C("bucket")[0:NBUCKET, :], start=True, stop=True).then_inc(S("line_done"), 1)
            end_stage(pe, "pe")

            for l in range(DEPTH):
                norm(l, 0)
                end_stage(pe, "pe")
                column_tiles(l, "Aq", [P] * 4, 0, 0)
                column_tiles(l, "Ak", [P] * 4, 4, 4)
                buf = k8(chunk(l, "Av"))
                for t, (t0, n) in enumerate(((0, P), (P, P), (2 * P, T - 2 * P))):
                    pe.wait_ge(S("proj_copied"), at("proj_copied", l, t))
                    for k in range(KT):
                        ins = pe.matmul(PS[0:n, t, :], xn[:, k, 1 + t0:1 + t0 + n], buf[:, k, :], start=(k == 0), stop=(k == KT - 1))
                    ins.then_inc(S("proj_done"), 1)
                release(spare())
                end_stage(pe, "pe")

                def zscores(h):
                    if h >= 2:
                        pe.wait_ge(S("at_done"), at("at_done", l, h - 2))
                    p, r, b = h // 2, 64 * (h % 2), 2 * (h % 2)
                    kh, qh = kA[r:r + 64, p], qA[r:r + 64, p]
                    pe.matmul(PS[:, b, 0:T], kh[:, 0:P], qh[:, 0:T], start=True, stop=False, skip_group_check=True)
                    pe.matmul(PS[:, b + 1, 0:144], kh[:, P:2 * P], qh[:, P:T], start=True, stop=False, skip_group_check=True)
                    pe.matmul(PS[:, b + 1, 144:160], kh[:, 2 * P:3 * P], qh[:, 2 * P:T], start=False, stop=False,
                              skip_group_check=True).then_inc(S("z_done"), 1)

                zscores(0)
                for h in range(8):
                    if h < 7:
                        zscores(h + 1)
                    s, b = h % 2, 2 * (h % 2)
                    pe.wait_ge(S("sp_done"), at("sp_done", l, h))
                    sp_ = spA[:, s, :]
                    mm = lambda o, a, b_: pe.matmul(o, a, b_, start=False, stop=False, skip_group_check=True)
                    mm(PS[:, b, 0:T], C("negsuffix"), sp_[:, 0:T])
                    mm(PS[:, b, P:T], C("negones"), sp_[:, T:T + 144])
                    mm(PS[:, b, 2 * P:T], C("negones"), sp_[:, 416:432])
                    mm(PS[:, b, 0:P], C("ident"), C("negmask"))
                    mm(PS[:, b + 1, 0:160], C("negsuffix"), sp_[:, T:432])
                    mm(PS[:, b + 1, P:144], C("negones"), sp_[:, 416:432])
                    mm(PS[:, b + 1, 0:P], C("ident"), C("negmask"))
                    pe.matmul(PS[:, b + 1, 144:160], C("ident"), C("negmask", 0, 16), start=False, stop=True,
                              skip_group_check=True).then_inc(S("arg_done"), 1)
                    pe.wait_ge(S("at_done"), at("at_done", l, h))
                    p, r, yb = h // 2, 64 * (h % 2), 4 + (h // 2) % 2
                    if r == 0 and p >= 2:
                        pe.wait_ge(S("ya_copied"), at("ya_copied", l, p - 2))
                    vh = lambda J: vA[:, J, h * 64:h * 64 + 64]
                    a_ = atA[:, s, :]
                    pe.matmul(PS[r:r + 64, yb, 0:T], vh(0), a_[:, 0:T], start=True, stop=False, skip_group_check=True)
                    pe.matmul(PS[r:r + 64, yb, P:T], vh(1), a_[:, T:T + 144], start=False, stop=False, skip_group_check=True)
                    ins = pe.matmul(PS[r:r + 64, yb, 2 * P:T], vh(2), a_[:, 416:432], start=False, stop=True, skip_group_check=True)
                    if r:
                        ins.then_inc(S("ya_done"), 1)
                end_stage(pe, "pe")

                column_tiles(l, "Cq", [P] * 4, 11, 0)
                column_tiles(l, "Ckv", [P] * 2, 15, 4)
                pe.wait_ge(S("proj_copied"), at("proj_copied", l, 16))
                for w, (t0, n) in enumerate(((0, 80), (META, P), (META + 64, P), (META + 128, P))):
                    ins = pe.transpose(PS[0:n, 6, w * P:(w + 1) * P], vC[:, t0:t0 + n], C("ident"))
                ins.then_inc(S("c_vt"), 1)
                pe.wait_ge(S("c_vtc"), at("c_vtc", l, 0))
                for u in range(5):
                    meta_q = u == 4
                    if meta_q and l == DEPTH - 1:
                        break
                    for g in range(2):
                        r = 64 * g
                        for jp in range(1 if meta_q else 2):
                            if meta_q:
                                lhs, o, m = qCm[r:r + 64, :, :].rearrange("p a b -> p (a b)"), 0, 64
                            else:
                                lhs = qCx[r:r + 64, u, 2 * jp:2 * jp + 2, :].rearrange("p a b -> p (a b)")
                                o, m = (80 if u == 0 else 144) * jp, P
                            keys = [(0, META)] if meta_q else [(0, 80)] if u == 0 else [(0, META), (META + 64 * (u - 1), P)]
                            for t0, n in keys:
                                ins = pe.matmul(PS[0:m, g, o:o + n], lhs, kC[r:r + 64, t0:t0 + n], start=True, stop=True)
                                o += n
                    ins.then_inc(S("c_z"), 1)
                    pe.wait_ge(S("c_p"), at("c_p", l, u))
                    units, m = (2, 64) if meta_q else (4, P)
                    for v in range(units):
                        if meta_q or u == 0:
                            n = META if meta_q else 80
                            ins = pe.transpose(PS[0:n, 2, v * m:(v + 1) * m], sC[0:m, v, 0:n], C("ident")[0:m, 0:m])
                        else:
                            pe.transpose(PS[:, 2, v * P:(v + 1) * P], sC[:, v, META:144], C("ident"))
                            ins = pe.transpose(PS[0:META, 3, v * P:(v + 1) * P], sC[:, v, 0:META], C("ident"))
                    ins.then_inc(S("c_t"), 1)
                    pe.wait_ge(S("c_tc"), at("c_tc", l, u))
                    for g in range(2):
                        vcols = slice(64 * g, 64 * g + 64)
                        if meta_q:
                            ins = pe.matmul(PS[64 * g:64 * g + 64, 4, 0:64], vW[0:META, 0, vcols],
                                            pTC[0:META, :, :].rearrange("p a b -> p (a b)")[:, 64 * g:64 * g + 64], start=True, stop=True)
                        elif u == 0:
                            ins = pe.matmul(PS[64 * g:64 * g + 64, 4, 0:256], vW[0:80, 0, vcols],
                                            pTC[0:80, 2 * g:2 * g + 2, :], start=True, stop=True)
                        else:
                            pe.matmul(PS[64 * g:64 * g + 64, 4, 0:256], vW[:, u, vcols],
                                      pTC[:, 2 * g:2 * g + 2, :], start=True, stop=False, skip_group_check=True)
                            ins = pe.matmul(PS[64 * g:64 * g + 64, 4, 0:256], vW[0:META, 0, vcols],
                                            pTm[0:META, 2 * g:2 * g + 2, :], start=False, stop=True, skip_group_check=True)
                    ins.then_inc(S("c_y"), 1)
                    pe.wait_ge(S("c_yc"), at("c_yc", l, u))
                end_stage(pe, "pe")

                column_tiles(l, "Br", [P] * 4, 17, 0)
                column_tiles(l, "Bk", [P] * 4, 21, 4)
                column_tiles(l, "Bv", [P] * 4, 25, 8)
                buf = k8(chunk(l, "Bx"))
                for i, (c, m, lo) in enumerate(((0, 64, 0), (64, 64, 64), (128, P, 0), (256, 32, 0))):
                    if i != 1:
                        pe.wait_ge(S("proj_copied"), at("proj_copied", l, 21 + max(i - 1, 0)))
                    bank = 4 + max(i - 1, 0)
                    for k in range(KT):
                        ins = pe.matmul(PS[lo:lo + m, bank, 0:T], buf[:, k, c:c + m], xn[:, k, 1:T + 1],
                                        start=(k == 0), stop=(k == KT - 1))
                    if i:
                        ins.then_inc(S("proj_done"), 1)
                release(spare())
                end_stage(pe, "pe")

                pe.wait_ge(S("w_in"), at("w_in", l, 0))
                for p in range(4):
                    ins = pe.matmul(PS[:, p, 0:T], wwa[0:64, p * P:(p + 1) * P], PX[0:64, 0, PADC:TP], start=True, stop=True)
                ins.then_inc(S("w_mm"), 1)
                for p in range(4):
                    ins = pe.matmul(PS[:, 4 + p, 0:T], wwa[64:P, p * P:(p + 1) * P], PX[64:P, 0, PADC:TP], start=True, stop=True)
                ins.then_inc(S("w_mm"), 1)
                pe.wait_ge(S("w_ev"), at("w_ev", l, 0))
                for p in range(4):
                    pe.matmul(PS[:, p, 0:T], wg0[:, p * P:(p + 1) * P], PX[:, 1, PADC:TP], start=True, stop=False)
                    ins = pe.matmul(PS[:, p, 0:T], wg1[:, p * P:(p + 1) * P], PX[0:32, 2, PADC:TP], start=False, stop=True)
                ins.then_inc(S("w_mm"), 1)
                if l:
                    pe.wait_ge(S("w_ev"), at("w_ev", l, 1))
                    pe.wait_ge(S("xv_done"), 1)
                    for k in range(KT):
                        ins = pe.matmul(PS[0:32, 4, 0:T], vw1_sb[:, k, :], SQ_v[:, k, :], start=(k == 0), stop=(k == KT - 1))
                    ins.then_inc(S("v_mm"), 1)
                    pe.wait_ge(S("v_ev"), 1)
                    for p in range(4):
                        ins = pe.matmul(PS[:, 4 + p, 0:T], vw2_sb[:, p * P:(p + 1) * P], PX[0:32, 1, PADC:TP], start=True, stop=True)
                    ins.then_inc(S("v_mm"), 1)
                end_stage(pe, "pe")
                pe.wait_ge(S("k_sq"), at("k_sq", l, 0))
                for p in range(4):
                    ins = pe.matmul(PS[:, p, 0:T], C("headones"), DD[:, p, PADC:TP], start=True, stop=True)
                ins.then_inc(S("k_sum"), 1)
                pe.wait_ge(S("b_pr"), at("b_pr", l, 0))
                for p in range(4):
                    ins = pe.matmul(PS[:, 4 + p, 0:T], C("headones"), DD[:, p, PADC:TP], start=True, stop=True)
                ins.then_inc(S("b_sum"), 1)
                end_stage(pe, "pe")

                for c in range(NCH):
                    cc = slice(c * CH, (c + 1) * CH)
                    pe.wait_ge(S("r_bd"), at("r_bd", l, c))
                    for p in range(4):
                        for j, (lhs, rhs) in enumerate(((Bbd, KK), (Hbd, KK))):
                            pe.matmul(PS[:, 0, (4 * j + p) * CH:(4 * j + p + 1) * CH], lhs[:, p, :], rhs[:, p, cc], start=True, stop=True)
                        for j, (lhs, rhs) in enumerate(((Bbd, R), (Hbd, R))):
                            pe.matmul(PS[:, 1, (4 * j + p) * CH:(4 * j + p + 1) * CH], lhs[:, p, :], rhs[:, p, cc], start=True, stop=True)
                        pe.matmul(PS[:, 2, p * CH:(p + 1) * CH], VTbd[:, p, :], C("stack"), start=True, stop=True)
                        pe.transpose(PS[:, 3, p * P:(p + 1) * P], Bbd[:, p, :], C("ident"))
                        ins = pe.transpose(PS[:, 4, p * P:(p + 1) * P], Hbd[:, p, :], C("ident"))
                    ins.then_inc(S("r_mm"), 1)
                    pe.wait_ge(S("r_tt"), at("r_tt", l, c))
                    for p in range(4):
                        ins = pe.transpose(PS[:, 5, p * P:(p + 1) * P], TT[:, p, :], C("ident"))
                    ins.then_inc(S("r_t"), 1)
                    pe.wait_ge(S("r_tc"), at("r_tc", l, c))
                    for v in range(5):
                        n = c * 5 + v
                        pe.wait_ge(S("r_lv"), at("r_lv", l, n))
                        for p in range(4):
                            ins = pe.matmul(PS[:, 5, p * P:(p + 1) * P], NTb[:, p, :], TI[:, p, :], start=True, stop=True)
                        ins.then_inc(S("r_p"), 1)
                        pe.wait_ge(S("r_pc"), at("r_pc", l, n))
                        for p in range(4):
                            ins = pe.matmul(PS[:, 6, p * P:(p + 1) * P], PW[:, p, :], TT[:, p, :], start=True, stop=True)
                            if v < 4:
                                ins = pe.matmul(PS[:, 7, p * P:(p + 1) * P], TT[:, p, :], PW[:, p, :], start=True, stop=True)
                        ins.then_inc(S("r_d"), 1)
                    pe.wait_ge(S("r_cp"), at("r_cp", l, c))
                    for p in range(4):
                        o = PS[:, 5, p * CH:(p + 1) * CH]
                        pe.matmul(o, Kbd[:, p, :], state[:, p, :], start=True, stop=False, skip_group_check=True)
                        ins = pe.matmul(o, M2bd[:, p, :], Vst[:, p, :], start=False, stop=True, skip_group_check=True)
                    ins.then_inc(S("r_x"), 1)
                    pe.wait_ge(S("r_xc"), at("r_xc", l, c))
                    pe.wait_ge(S("r_tr"), at("r_tr", l, c))
                    for p in range(4):
                        ins = pe.matmul(PS[:, 6, p * CH:(p + 1) * CH], TT[:, p, :], Xst[:, p, :], start=True, stop=True)
                    ins.then_inc(S("r_u"), 1)
                    pe.wait_ge(S("r_ust"), at("r_ust", l, c))
                    for p in range(4):
                        o = PS[:, 7, p * CH:(p + 1) * CH]
                        pe.matmul(o, Sbd[:, p, :], R[:, p, cc], start=True, stop=False, skip_group_check=True)
                        pe.matmul(o, Vbd[:, p, :], AA[:, 4 + p, :], start=False, stop=False, skip_group_check=True)
                        ins = pe.matmul(o, Ubd[:, p, :], AA[:, p, :], start=False, stop=True, skip_group_check=True)
                    ins.then_inc(S("r_ys"), 1)
                    for p in range(4):
                        o = PS[:, 5, p * CH:(p + 1) * CH]
                        pe.matmul(o, BT[:, p, :], Ust[:, p, :], start=True, stop=False, skip_group_check=True)
                        ins = pe.matmul(o, HT[:, p, :], Vst[:, p, :], start=False, stop=True, skip_group_check=True)
                    ins.then_inc(S("r_s"), 1)
                end_stage(pe, "pe")
                for p in range(4):
                    ins = pe.matmul(PS[:, p, 0:T], C("headones"), Y[:, p, PADC:TP], start=True, stop=True)
                ins.then_inc(S("n_m"), 1)
                pe.wait_ge(S("n_sq"), at("n_sq", l, 0))
                for p in range(4):
                    ins = pe.matmul(PS[:, 4 + p, 0:T], C("headones"), K[:, p, PADC:TP], start=True, stop=True)
                ins.then_inc(S("n_v"), 1)
                end_stage(pe, "pe")

                ycur = [yA[:, :, :], R[:, :, PADC:TP], yC[:, :, :]]
                for b in range(3):
                    wp = k4(chunk(l, f"P{b}"))
                    i_p = used[0]
                    used[0] += 1
                    for h in range(2):
                        i_g = position[(l, f"G{b}{h}")]
                        pe.wait_ge(S(f"landed{i_g % RING}"), landed_at[i_g])
                        gb = k8(ring[i_g % RING])
                        for dt in range(4):
                            n = b * 8 + h * 4 + dt
                            if n >= 4:
                                pe.wait_ge(S("m_acc"), at("m_acc", l, n - 4))
                            bank = n % 4
                            for k in range(KT):
                                ins = pe.matmul(PS[:, bank, 0:T], gb[:, k, dt * P:(dt + 1) * P], xn[:, k, 1:T + 1],
                                                start=(k == 0), stop=(k == KT - 1))
                            ins.then_inc(S("m_g"), 1)
                            for k in range(4):
                                ins = pe.matmul(PS[:, 4 + bank, 0:T], wp[:, k, (4 * h + dt) * P:(4 * h + dt + 1) * P],
                                                ycur[b][:, k, :], start=(k == 0), stop=(k == 3))
                            ins.then_inc(S("m_p"), 1)
                        if h == 1:
                            pe.drain().then_inc(S("chunk_used"), 3)
                            used[0] += 2
                pe.wait_ge(S("m_acc"), at("m_acc", l, 23))
                for h in range(2):
                    ob = k8(chunk(l, f"O{h}"))
                    for dt in range(4):
                        n = 4 * h + dt
                        for k in range(KT):
                            ins = pe.matmul(PS[:, n, 0:T], ob[:, k, dt * P:(dt + 1) * P], MG[:, k, :], start=(k == 0), stop=(k == KT - 1))
                        ins.then_inc(S("o_mm"), 1)
                    release(spare())
                end_stage(pe, "pe")
                norm(l, 1)
                end_stage(pe, "pe")
                if l == 0:
                    for f in range(FG):
                        for j, nm in enumerate(("DG", "DU")):
                            buf = k8(chunk(l, f"{nm}{f}"))
                            for i in range(4):
                                if f:
                                    pe.wait_ge(S("f_h"), 4 * (f - 1) + i + 1)
                                for k in range(KT):
                                    ins = pe.matmul(PS[:, 4 * j + i, 0:T], buf[:, k, i * P:(i + 1) * P], xn[:, k, 1:T + 1],
                                                    start=(k == 0), stop=(k == KT - 1))
                                ins.then_inc(S("f_mm"), 1)
                            release(spare())
                    pe.wait_ge(S("f_h"), 4 * FG)
                    for f in range(FG):
                        buf = k4(chunk(l, f"DD{f}"))
                        for i in range(4):
                            for d in range(KT):
                                ins = pe.matmul(PS[:, d, 0:T], buf[:, i, d * P:(d + 1) * P], HF[:, 4 * f + i, :],
                                                start=(f == 0 and i == 0), stop=(f == FG - 1 and i == 3))
                        release(ins if f < FG - 1 else spare())
                    pe.drain().then_inc(S("f_down"), 1)
                    end_stage(pe, "pe")

            for t in range(2):
                for k in range(KT):
                    ins = pe.matmul(PS[:, 0, 8 * t:8 * t + 8], xn[:, k, 1 + META + t * P:1 + META + (t + 1) * P],
                                    router_sb[:, k, :], start=(k == 0), stop=(k == KT - 1))
            ins.then_inc(S("q_log"), 1)
            for t in range(2):
                for q in range(2):
                    for k in range(4):
                        ins = pe.transpose(PS[:, 1 + 2 * t + q, k * P:(k + 1) * P],
                                           xn[:, 4 * q + k, 1 + META + t * P:1 + META + (t + 1) * P], C("ident"))
            ins.then_inc(S("q_turn"), 1)
            pe.wait_ge(S("q_sel"), 1)
            sel = lambda t: MR[:, 16 + 8 * t:24 + 8 * t]
            pe.matmul(PS[:, 5, 0:8], C("before"), sel(0), start=True, stop=True)
            pe.matmul(PS[:, 5, 8:16], C("ones"), sel(0), start=True, stop=False, skip_group_check=True)
            pe.matmul(PS[:, 5, 8:16], C("before"), sel(1), start=False, stop=True, skip_group_check=True)
            pe.matmul(PS[:, 5, 16:24], C("ones"), sel(0), start=True, stop=False, skip_group_check=True)
            pe.matmul(PS[:, 5, 16:24], C("ones"), sel(1), start=False, stop=True, skip_group_check=True).then_inc(S("q_rank"), 1)
            end_stage(pe, "pe")

            def experts(again):
                base = again * NE
                with pe.Fori(0, NE) as e:
                    pe.wait_ge(S("e_sel"), e + (base + 1))
                    for k in range(KT):
                        for t in range(2):
                            ins = pe.matmul(PS[:, 6 + k // 4, (k % 4) * P:(k % 4 + 1) * P], hnT[:, t, k * P:(k + 1) * P],
                                            SEL[:, t, :], start=(t == 0), stop=(t == 1))
                    ins.then_inc(S("e_xg"), 1)
                    pe.wait_ge(S("e_xgc"), e + (base + 1))
                    for t in range(2):
                        ins = pe.transpose(PS[:, 6, t * P:(t + 1) * P], SEL[:, 2 + t, :], C("ident"))
                    ins.then_inc(S("e_st"), 1)
                    for i, (kind, f) in enumerate(MOE_ORDER):
                        n = MOE0 + i + again * NE * len(MOE_ORDER)
                        b = n % RING
                        pe.wait_ge(S(f"landed{b}"), e * (32 * PER_BUF) + (landed_moe0[b] + again * NE * 32 * PER_BUF + 32 * (i // RING + 1)))
                        if kind in "gu":
                            buf = k8(ring[b])
                            bank = 2 * (f % 2) + (kind == "u")
                            pe.wait_ge(S("e_h"), e * FG + (base * FG + f - 1)) if f >= 2 else pe.wait_ge(S("e_free"), e + (base + 1))
                            for q in range(4):
                                for k in range(KT):
                                    ins = pe.matmul(PS[:, bank, q * P:(q + 1) * P], buf[:, k, q * P:(q + 1) * P], XG[:, k, :],
                                                    start=(k == 0), stop=(k == KT - 1))
                            ins.then_inc(S("e_mm"), 1)
                        else:
                            buf = k4(ring[b])
                            pe.wait_ge(S("e_h"), e * FG + (base * FG + f + 1))
                            for q in range(4):
                                for hf in range(2):
                                    ins = pe.matmul(PS[:, 4 + hf, :], MH[:, f % 2, q * P:(q + 1) * P],
                                                    buf[:, q, 512 * hf:512 * hf + 512], start=(f == 0 and q == 0),
                                                    stop=(f == FG - 1 and q == 3))
                            ins.then_inc(S("e_dn"), 1)
                        pe.drain().then_inc(S("chunk_used"), 1)
                    pe.wait_ge(S("e_y"), e * 2 + (2 * base + 2))
                    for k in range(KT):
                        ins = pe.matmul(PS[:, k // 2, (k % 2) * SEQ:(k % 2 + 1) * SEQ], YE[:, k * P:(k + 1) * P], SELT[:, :],
                                        start=True, stop=True)
                    ins.then_inc(S("e_sc"), 1)

            experts(0)
            with overflow_branch(pe):
                experts(1)
            end_stage(pe, "pe")
            norm(DEPTH, 0)
            pe.wait_ge(S("fin"), 1)
            for t in range(2):
                for q in range(2):
                    for k in range(4):
                        ins = pe.transpose(PS[:, 1 + 2 * t + q, k * P:(k + 1) * P], xn[:, 4 * q + k, 1 + META + t * P:1 + META + (t + 1) * P],
                                           C("ident"))
                    ins.then_inc(S("out_turned"), 1)

        @block.scalar
        def _(act):
            def a(ins):
                link(act, ins, "act_chain")

            n_dma = [0]

            def load(dst, src):
                act.dma_start(dst, src).then_inc(S("setup"), 16)
                n_dma[0] += 1

            load(cst[:, :], consts)
            load(prm[:, :, :], params.rearrange("l p n -> p l n"))
            load(xin[0:META, 0, :], meta)
            for t in range(2):
                load(xin[:, 1 + t, :], x[0, t * P:(t + 1) * P, :])
            load(relb[:, :], rel_bias)

            def low_rank(l, ld):
                ld(wwa[0:64, :], w2[l])
                ld(wwa[64:P, :], a2[l])
                ld(wg0[:, :], g2[l, 0:P, :])
                ld(wg1[:, :], g2[l, P:P + 32, :])

            low_rank(0, load)
            load(vw1_sb[:, :, :], vw1[0].rearrange("(k p) n -> p k n", p=P))
            load(vw2_sb[:, :], vw2[0])
            load(router_sb[:, :, :], router[0].rearrange("(k p) n -> p k n", p=P))
            act.wait_ge(S("setup"), 16 * n_dma[0])
            assert n_dma[0] == N_SETUP, n_dma

            for k in range(KT):
                act.wait_ge(S("in_turned"), k + 1)
                ins = act.activation(hT[:, k, :], PS[:, k, 0:T], ACT.Copy)
                if k == 0:
                    ins.then_inc(S("in_copied"), 1)
            act.wait_ge(S("line_done"), 1)
            link(act, act.activation(lin[:, :], PS[0:NE, 0, 0:LINE], ACT.Copy), "lin_copied")
            act.dma_start(line, bc(lin[:, :], [NE, CH, LINE], 1)).then_inc(S("line_stored"), 16)
            act.wait_ge(S("line_stored"), 16)

            def toeplitz(dst, head0, r0, rows, unit_step, units, n):
                src = bass.AP(tensor=line.tensor, offset=head0 * CH * LINE + r0,
                              ap=[[LINE - 1, rows], [unit_step * CH * LINE, units], [1, n]])
                act.dma_start(dst, src).then_inc(S("bias_ready"), 16)

            for j2 in range(2):
                rows = slice(64 * j2, 64 * j2 + 64)
                toeplitz(bias0[rows, :, :], j2, LINE_TOP - META, 64, 2, 4, 80)
                toeplitz(biasb[rows, :, :], j2, LINE_TOP - 64, 64, 2, 4, P)
                for c in range(1, NXC):
                    toeplitz(biasm[rows, c - 1, :, :], j2, LINE_TOP - META - 64 * c, 64, 2, 4, META)
            for j in range(4):
                toeplitz(biasq[16 * j:16 * j + 16, :, :], j, LINE_TOP, META, 4, 2, META)
            end_stage(act, "act")

            def norm(l, which):
                act.activation(SQ[:, :, :], hT[:, :, :], ACT.Square).then_inc(S("sq_done"), 1)
                act.wait_ge(S("ms_done"), 2 * l + which + 1)
                act.activation(rstd[:, :], rstd[:, :], ACT.Sqrt).then_inc(S("rt_done"), 1)

            def copies(l, n0, dsts, scale=1.0, first=0):
                for i, dst in enumerate(dsts):
                    n = n0 + i
                    act.wait_ge(S("proj_done"), at("proj_done", l, n))
                    src = PS[:, (first + i) % 8, 0:T]
                    ins = None
                    for d_, s_ in dst(src):
                        if ins is not None:
                            a(ins)
                        ins = act.activation(d_, s_, ACT.Copy, scale=scale)
                    ins.then_inc(S("proj_copied"), 1)

            for l in range(DEPTH):
                norm(l, 0)
                end_stage(act, "act")
                copies(l, 0, [lambda s, p=p: [(qA[:, p, :], s)] for p in range(4)], QS)
                copies(l, 4, [lambda s, p=p: [(kA[:, p, 0:T], s)] for p in range(4)], 1.0, 4)
                for t, n in enumerate((P, P, T - 2 * P)):
                    act.wait_ge(S("proj_done"), at("proj_done", l, 8 + t))
                    act.activation(vA[0:n, t, :], PS[0:n, t, :], ACT.Copy).then_inc(S("proj_copied"), 1)
                end_stage(act, "act")
                def soft(h):
                    s, b = h % 2, 2 * (h % 2)
                    act.wait_ge(S("z_done"), at("z_done", l, h))
                    if h >= 2:
                        act.wait_ge(S("sp_done"), at("sp_done", l, h - 2))
                    act.activation(uA[:, s, 0:T], PS[:, b, 0:T], ACT.Abs)
                    a(act.activation(uA[:, s, T:432], PS[:, b + 1, 0:160], ACT.Abs))
                    a(act.activation(uA[:, s, :], uA[:, s, :], ACT.Exp, scale=-1.0))
                    act.activation(uA[:, s, :], uA[:, s, :], ACT.Ln, bias=1.0).then_inc(S("u_done"), 1)

                soft(0)
                for h in range(8):
                    if h < 7:
                        soft(h + 1)
                    s, b = h % 2, 2 * (h % 2)
                    act.wait_ge(S("arg_done"), at("arg_done", l, h))
                    act.activation(atA[:, s, 0:T], PS[:, b, 0:T], ACT.Exp)
                    act.activation(atA[:, s, T:432], PS[:, b + 1, 0:160], ACT.Exp).then_inc(S("at_done"), 1)
                end_stage(act, "act")
                copies(l, 11, [lambda s, j=j: [(qCm[:, j, :], s[:, 0:META]),
                                               (qCx[:, :, j, :], s[:, META:T].rearrange("p (c q) -> p c q", q=CH))]
                               for j in range(4)], QS)
                copies(l, 15, [lambda s: [(kC[:, :], s)], lambda s: [(vC[:, :], s)]], 1.0, 4)
                act.wait_ge(S("c_vt"), at("c_vt", l, 0))
                act.activation(vW[0:80, 0, :], PS[0:80, 6, 0:P], ACT.Copy)
                act.activation(vW[:, 1:4, :], PS[:, 6, P:4 * P].rearrange("p (a b) -> p a b", b=P), ACT.Copy).then_inc(S("c_vtc"), 1)
                for u in range(5):
                    meta_q = u == 4
                    if meta_q and l == DEPTH - 1:
                        break
                    m, v, n = (64, 2, META) if meta_q else (P, 4, 80 if u == 0 else 144)
                    act.wait_ge(S("c_m"), at("c_m", l, u))
                    act.activation(sC[0:m, 0:v, 0:n], sC[0:m, 0:v, 0:n], ACT.Exp)
                    act.activation(mC[0:m, 8:8 + v], mC[0:m, 4:4 + v], ACT.Exp).then_inc(S("c_e"), 1)
                    act.wait_ge(S("c_t"), at("c_t", l, u))
                    if meta_q or u == 0:
                        rows, w = (META, P) if meta_q else (80, 512)
                        act.activation(pTC[0:rows, :, :].rearrange("p a b -> p (a b)")[:, 0:w], PS[0:rows, 2, 0:w], ACT.Copy)\
                            .then_inc(S("c_tc"), 1)
                    else:
                        act.activation(pTC[:, :, :].rearrange("p a b -> p (a b)"), PS[:, 2, :], ACT.Copy)
                        act.activation(pTm[0:META, :, :].rearrange("p a b -> p (a b)"), PS[0:META, 3, :], ACT.Copy)\
                            .then_inc(S("c_tc"), 1)
                    act.wait_ge(S("c_y"), at("c_y", l, u))
                    if meta_q:
                        act.activation(yC[:, :, 0:META], PS[:, 4, 0:64].rearrange("p (a b) -> p a b", b=META), ACT.Copy).then_inc(S("c_yc"), 1)
                    else:
                        t0 = META + CH * u
                        act.activation(yC[:, :, t0:t0 + CH], PS[:, 4, 0:256].rearrange("p (a b) -> p a b", b=CH), ACT.Copy)\
                            .then_inc(S("c_yc"), 1)
                end_stage(act, "act")
                for i, (X_, f0) in enumerate(((R, 0), (K, 4), (V, 8))):
                    copies(l, 17 + 4 * i, [lambda s, p=p, X_=X_: [(X_[:, p, PADC:TP], s)] for p in range(4)], 1.0, f0)
                for i, rows in enumerate((P, P, 32)):
                    act.wait_ge(S("proj_done"), at("proj_done", l, 29 + i))
                    act.activation(PX[0:rows, i, PADC:TP], PS[0:rows, 4 + i, 0:T], ACT.Copy).then_inc(S("proj_copied"), 1)
                end_stage(act, "act")
                act.wait_ge(S("x_mixed"), l + 1)
                act.activation(PX[0:64, 0, PADC:TP], PX[0:64, 0, PADC:TP], ACT.Tanh)
                act.activation(PX[:, 1, PADC:TP], PX[:, 1, PADC:TP], ACT.Sigmoid)
                act.activation(PX[0:32, 2, PADC:TP], PX[0:32, 2, PADC:TP], ACT.Sigmoid).then_inc(S("w_in"), 1)
                act.wait_ge(S("w_mm"), at("w_mm", l, 0))
                for p in range(4):
                    ins = act.activation(LW[:, p, PADC:TP], PS[:, p, 0:T], ACT.Sigmoid, bias=prm_col(l, "w0", p))
                ins.then_inc(S("w_ev"), 1)
                act.wait_ge(S("w_mm"), at("w_mm", l, 1))
                for p in range(4):
                    ins = act.activation(AI[:, p, PADC:TP], PS[:, 4 + p, 0:T], ACT.Sigmoid, bias=prm_col(l, "a0", p))
                ins.then_inc(S("w_ev"), 1)
                act.wait_ge(S("w_mm"), at("w_mm", l, 2))
                act.activation(GT[:, :, PADC:TP], PS[:, 0:4, 0:T], ACT.Copy).then_inc(S("w_ev"), 1)
                if l:
                    act.wait_ge(S("v_mm"), 1)
                    act.activation(PX[0:32, 1, PADC:TP], PS[0:32, 4, 0:T], ACT.Copy).then_inc(S("v_ev"), 1)
                    act.wait_ge(S("v_mm"), 2)
                    for p in range(4):
                        ins = act.activation(DD[:, p, PADC:TP], PS[:, 4 + p, 0:T], ACT.Sigmoid, bias=prm_col(l, "vres_b", p))
                    ins.then_inc(S("v_ev"), 1)
                end_stage(act, "act")
                act.wait_ge(S("k_sum"), at("k_sum", l, 0))
                act.activation(BN[:, :, PADC:TP], PS[:, 0:4, 0:T], ACT.Sqrt).then_inc(S("k_rt"), 1)
                for i in range(3):
                    act.wait_ge(S("g_done"), 3 * l + i + 1)
                    src = (LWG, LWG, LW)[i]
                    act.activation(DD[:, :, :], src[:, :, :], ACT.Exp, scale=-1.0 if i == 1 else 1.0).then_inc(S("e_done"), 1)
                end_stage(act, "act")
                for c in range(NCH):
                    cc = slice(c * CH, (c + 1) * CH)
                    flat = lambda v: v[:, :, :].rearrange("p a b -> p (a b)")
                    act.wait_ge(S("r_mm"), at("r_mm", l, c))
                    act.activation(flat(BT), PS[:, 3, :], ACT.Copy)
                    act.activation(flat(HT), PS[:, 4, :], ACT.Copy)
                    act.activation(flat(Vst), PS[:, 2, 0:256], ACT.Copy).then_inc(S("r_vc"), 1)
                    act.wait_ge(S("r_t"), at("r_t", l, c))
                    act.activation(flat(TI), PS[:, 5, :], ACT.Copy).then_inc(S("r_tc"), 1)
                    for v in range(5):
                        act.wait_ge(S("r_p"), at("r_p", l, 5 * c + v))
                        act.activation(flat(PW), PS[:, 5, :], ACT.Copy).then_inc(S("r_pc"), 1)
                    act.wait_ge(S("r_x"), at("r_x", l, c))
                    act.activation(flat(Xst), PS[:, 5, 0:256], ACT.Copy, scale=-1.0).then_inc(S("r_xc"), 1)
                    act.wait_ge(S("r_u"), at("r_u", l, c))
                    act.activation(flat(Ust), PS[:, 6, 0:256], ACT.Copy).then_inc(S("r_uc"), 1)
                    act.wait_ge(S("r_ys"), at("r_ys", l, c))
                    act.activation(Y[:, :, cc], PS[:, 7, 0:256].rearrange("p (a b) -> p a b", b=CH), ACT.Copy).then_inc(S("r_yc"), 1)
                end_stage(act, "act")
                act.wait_ge(S("n_d"), at("n_d", l, 0))
                act.activation(K[:, :, PADC:TP], Y[:, :, PADC:TP], ACT.Square).then_inc(S("n_sq"), 1)
                act.wait_ge(S("n_e"), at("n_e", l, 0))
                act.activation(K[:, :, PADC:TP], K[:, :, PADC:TP], ACT.Sqrt).then_inc(S("n_s"), 1)
                end_stage(act, "act")
                for n in range(24):
                    act.wait_ge(S("m_g"), at("m_g", l, n))
                    if n >= 2:
                        act.wait_ge(S("m_acc"), at("m_acc", l, n - 2))
                    act.activation(SG[:, n % 2, :], PS[:, n % 4, 0:T], ACT.Sigmoid).then_inc(S("m_s"), 1)
                if l == 0:
                    low_rank(1, lambda d_, s_: act.dma_start(d_, s_).then_inc(S("low_rank1"), 16))
                    act.wait_ge(S("low_rank1"), 64)
                end_stage(act, "act")
                norm(l, 1)
                end_stage(act, "act")
                if l == 0:
                    for f in range(FG):
                        for i in range(4):
                            act.wait_ge(S("f_mm"), 8 * f + i + 1)
                            if f:
                                act.wait_ge(S("f_h"), 4 * (f - 1) + i + 1)
                            act.activation(SF[:, i, :], PS[:, i, 0:T], ACT.Silu).then_inc(S("f_s"), 1)
                    end_stage(act, "act")

            act.wait_ge(S("q_turn"), 1)
            for t in range(2):
                ins = act.activation(hnT[:, t, :].rearrange("p (a b) -> p a b", a=2), PS[:, 1 + 2 * t:3 + 2 * t, :], ACT.Copy)
            a(ins)
            act.wait_ge(S("q_gap"), 1)
            act.activation(MR[:, 80:82], MR[:, 80:82], ACT.Exp).then_inc(S("q_exp"), 1)
            end_stage(act, "act")

            def experts(again):
                base = again * NE
                with act.Fori(0, NE) as e:
                    act.wait_ge(S("e_xg"), e + (base + 1))
                    act.activation(XG[:, :, :].rearrange("p (a b) c -> p a (b c)", a=2), PS[:, 6:8, :], ACT.Copy).then_inc(S("e_xgc"), 1)
                    act.wait_ge(S("e_st"), e + (base + 1))
                    act.activation(SELT[:, :], PS[:, 6, 0:SEQ], ACT.Copy).then_inc(S("e_stc"), 1)
                    for f in range(FG):
                        act.wait_ge(S("e_mm"), e * (2 * FG) + (2 * base * FG + 2 * f + 1))
                        if f >= 2:
                            act.wait_ge(S("e_h"), e * FG + (base * FG + f - 1))
                        act.activation(MS[:, f % 2, :], PS[:, 2 * (f % 2), :], ACT.Silu).then_inc(S("e_s"), 1)
                    act.wait_ge(S("e_dn"), e * FG + (base * FG + FG))
                    act.activation(YE[:, 0:512], PS[:, 4, :], ACT.Copy).then_inc(S("e_y"), 1)
                    act.activation(YE[:, 512:D], PS[:, 5, :], ACT.Copy).then_inc(S("e_y"), 1)

            experts(0)
            with overflow_branch(act):
                experts(1)
            end_stage(act, "act")
            norm(DEPTH, 0)
            for t in range(4):
                act.wait_ge(S("out_turned"), t + 1)
                act.activation(ostage[:, t // 2, 512 * (t % 2):512 * (t % 2) + 512], PS[:, 1 + t, :], ACT.Copy).then_inc(S("out_copied"), 1)

        @block.vector
        def _(dve):
            def v(ins):
                link(dve, ins, "dve_chain")

            tt = lambda o, a_, b_, op: dve.tensor_tensor(o, a_, b_, op)

            dve.memset(xn[:, :, 0:1], 0.0)
            v(dve.memset(egc[:, :, :], 0.0))
            end_stage(dve, "dve")

            def norm(l, which, gain):
                dve.wait_ge(S("sum_done"), 2 * l + which + 1)
                dve.tensor_scalar(rstd[:, :], PS[:, 0, 0:T], 1.0 / D, EPS, ALU.mult, ALU.add).then_inc(S("ms_done"), 1)
                dve.wait_ge(S("rt_done"), 2 * l + which + 1)
                v(dve.reciprocal(rstd[:, :], rstd[:, :]))
                for k in range(KT):
                    ins = dve.scalar_tensor_tensor(xn[:, k, 1:T + 1], hT[:, k, :], prm_col(min(l, DEPTH - 1), gain, k), rstd[:, :],
                                                   ALU.mult, ALU.mult)
                return ins

            for l in range(DEPTH):
                dve.memset(kA[:, :, T:384], 0.0)
                dve.memset(vA[:, 2, :], 0.0)
                v(norm(l, 0, "norm_mix"))
                end_stage(dve, "dve")
                end_stage(dve, "dve")
                for h in range(8):
                    s, b = h % 2, 2 * (h % 2)
                    dve.wait_ge(S("u_done"), 8 * l + h + 1)
                    if h >= 2:
                        dve.wait_ge(S("arg_done"), at("arg_done", l, h - 2))
                    dve.scalar_tensor_tensor(spA[:, s, 0:T], PS[:, b, 0:T], 0.0, uA[:, s, 0:T], ALU.max, ALU.add)
                    v(dve.scalar_tensor_tensor(spA[:, s, T:432], PS[:, b + 1, 0:160], 0.0, uA[:, s, T:432], ALU.max, ALU.add))
                    tt(spA[:, s, :], spA[:, s, :], C("sbmask"), ALU.mult).then_inc(S("sp_done"), 1)
                    if h % 2 == 1:
                        p = h // 2
                        dve.wait_ge(S("ya_done"), at("ya_done", l, p))
                        dve.tensor_copy(yA[:, p, :], PS[:, 4 + p % 2, 0:T]).then_inc(S("ya_copied"), 1)
                end_stage(dve, "dve")
                if l == 0:
                    dve.wait_ge(S("bias_ready"), 16 * 14)
                for u in range(5):
                    meta_q = u == 4
                    if meta_q and l == DEPTH - 1:
                        break
                    m, w, n = (64, 2, META) if meta_q else (P, 4, 80 if u == 0 else 144)
                    dve.wait_ge(S("c_z"), at("c_z", l, u))
                    for g in range(2):
                        if meta_q:
                            tt(sC[0:64, g, 0:META], PS[0:64, g, 0:META], biasq[:, g, :], ALU.add)
                            continue
                        src = PS[:, g, 0:2 * n].rearrange("p (a b) -> p a b", a=2)
                        if u == 0:
                            ins = tt(sC[:, 2 * g:2 * g + 2, 0:80], src, bias0[:, 2 * g:2 * g + 2, :], ALU.add)
                        else:
                            tt(sC[:, 2 * g:2 * g + 2, 0:META], src[:, :, 0:META], biasm[:, u - 1, 2 * g:2 * g + 2, :], ALU.add)
                            ins = tt(sC[:, 2 * g:2 * g + 2, META:144], src[:, :, META:144], biasb[:, 2 * g:2 * g + 2, :], ALU.add)
                    sv = sC[0:m, 0:w, 0:n]
                    o, _ = PARAM_COLS["sink_meta" if meta_q else "sink"]
                    v(dve.memset(small[:, 60:61], 0.0))
                    v(dve.tensor_reduce(mC[0:m, 0:w], sv, AX.X, ALU.max))
                    v(tt(mC[0:m, 0:w], mC[0:m, 0:w], prm[0:m, l, o:o + w], ALU.max))
                    tt(mC[0:m, 4:4 + w], prm[0:m, l, o:o + w], mC[0:m, 0:w], ALU.subtract)
                    tt(sv, sv, bc(mC[0:m, 0:w], [m, w, n], 2), ALU.subtract).then_inc(S("c_m"), 1)
                    dve.wait_ge(S("c_e"), at("c_e", l, u))
                    v(dve.tensor_reduce(mC[0:m, 12:12 + w], sv, AX.X, ALU.add))
                    v(tt(mC[0:m, 12:12 + w], mC[0:m, 12:12 + w], mC[0:m, 8:8 + w], ALU.add))
                    v(dve.reciprocal(mC[0:m, 12:12 + w], mC[0:m, 12:12 + w]))
                    tt(sv, sv, bc(mC[0:m, 12:12 + w], [m, w, n], 2), ALU.mult).then_inc(S("c_p"), 1)
                    dve.wait_ge(S("c_t"), at("c_t", l, u))
                end_stage(dve, "dve")
                for X_ in (R, K, V, LW, AI, KK):
                    dve.memset(X_[:, :, 0:PADC], 0.0)
                v(dve.memset(PX[:, :, 0:PADC], 0.0))
                end_stage(dve, "dve")
                def mix(X_, rows, mus, sem=None):
                    w = X_.shape[1]
                    d_ = DD[0:rows, 0:w, PADC:TP]
                    v(tt(d_, X_[0:rows, :, PADC - 1:TP - 1], X_[0:rows, :, PADC:TP], ALU.subtract))
                    for i in range(w):
                        ins = dve.scalar_tensor_tensor(X_[0:rows, i, PADC:TP], d_[:, i, :], mus(i)[0:rows], X_[0:rows, i, PADC:TP],
                                                       ALU.mult, ALU.add)
                    return ins

                v(mix(PX[:, 0:1, :], P, lambda i: prm_col(l, "mu_wa", 0)))
                v(mix(PX[:, 1:2, :], P, lambda i: prm_col(l, "mu_g0", 0)))
                mix(PX[:, 2:3, :], 32, lambda i: prm_col(l, "mu_g1", 0)).then_inc(S("x_mixed"), 1)
                dve.wait_ge(S("x_mixed"), l + 1)
                v(mix(R, P, lambda i: prm_col(l, "mu_r", i)))
                v(mix(K, P, lambda i: prm_col(l, "mu_k", i)))
                v(mix(V, P, lambda i: prm_col(l, "mu_v", i)))
                if l == 0:
                    v(dve.tensor_copy(VF[:, :, :], V[:, :, :]))
                else:
                    v(tt(SQ_v[:, :, :], xn[:, :, 0:T], xn[:, :, 1:T + 1], ALU.subtract))
                    for k in range(KT):
                        ins = dve.scalar_tensor_tensor(SQ_v[:, k, :], SQ_v[:, k, :], prm_col(l, "vres_mu", k), xn[:, k, 1:T + 1],
                                                       ALU.mult, ALU.add)
                    ins.then_inc(S("xv_done"), 1)
                end_stage(dve, "dve")
                TR = slice(PADC, TP)
                if l:
                    v(tt(SV[:, :, TR], VF[:, :, TR], V[:, :, TR], ALU.subtract))
                    v(tt(SV[:, :, TR], SV[:, :, TR], DD[:, :, TR], ALU.mult))
                    v(tt(V[:, :, TR], V[:, :, TR], SV[:, :, TR], ALU.add))
                    dve.memset(KK[:, :, 0:PADC], 0.0)
                v(dve.tensor_scalar(LW[:, :, TR], LW[:, :, TR], DECAY_SCALE, None, ALU.mult))
                for p in range(4):
                    ins = dve.tensor_scalar(KK[:, p, TR], K[:, p, TR], prm_col(l, "k_k", p), None, ALU.mult)
                v(ins)
                tt(DD[:, :, TR], KK[:, :, TR], KK[:, :, TR], ALU.mult).then_inc(S("k_sq"), 1)
                dve.wait_ge(S("k_sum"), at("k_sum", l, 0))
                for p in range(4):
                    ins = dve.tensor_scalar(DD[:, p, TR], AI[:, p, TR], -1.0, prm_col(l, "k_a", p), ALU.add, ALU.mult)
                v(ins)
                v(dve.scalar_tensor_tensor(K[:, :, TR], DD[:, :, TR], 1.0, K[:, :, TR], ALU.add, ALU.mult))
                v(tt(DD[:, :, TR], R[:, :, TR], K[:, :, TR], ALU.mult))
                for p in range(4):
                    ins = dve.tensor_scalar(DD[:, p, TR], DD[:, p, TR], prm_col(l, "r_k", p), None, ALU.mult)
                ins.then_inc(S("b_pr"), 1)
                dve.wait_ge(S("k_rt"), at("k_rt", l, 0))
                v(dve.tensor_scalar(BN[:, :, TR], BN[:, :, TR], 1e-12, None, ALU.max))
                v(dve.reciprocal(BN[:, :, TR], BN[:, :, TR]))
                v(tt(KK[:, :, TR], KK[:, :, TR], BN[:, :, TR], ALU.mult))
                v(tt(AI[:, :, TR], AI[:, :, TR], KK[:, :, TR], ALU.mult))
                dve.wait_ge(S("b_sum"), at("b_sum", l, 0))
                for p in range(4):
                    ins = dve.tensor_tensor_scan(LWG[:, p, :], C("reset"), LW[:, p, :], 0.0, ALU.mult, ALU.add)
                ins.then_inc(S("g_done"), 1)
                dve.wait_ge(S("e_done"), at("e_done", l, 0))
                dve.tensor_copy(egc[:, :, :], DD[:, :, :].rearrange("p a (c q) -> p a c q", q=CH)[:, :, :, CH - 1])
                v(tt(R[:, :, :], R[:, :, :], DD[:, :, :], ALU.mult))
                tt(LW[:, :, :], LWG[:, :, :], LW[:, :, :], ALU.subtract).then_inc(S("g_done"), 1)
                dve.wait_ge(S("e_done"), at("e_done", l, 1))
                tt(AI[:, :, :], AI[:, :, :], DD[:, :, :], ALU.mult)
                v(tt(K[:, :, :], K[:, :, :], DD[:, :, :], ALU.mult))
                dve.memset(small[:, 61:62], 0.0).then_inc(S("g_done"), 1)
                dve.wait_ge(S("e_done"), at("e_done", l, 2))
                v(tt(KK[:, :, :], KK[:, :, :], DD[:, :, :], ALU.mult))
                v(tt(BN[:, :, TR], V[:, :, TR], PS[:, 4:8, 0:T], ALU.mult))
                dve.memset(state[:, :, :], 0.0)
                v(dve.memset(Sbd[:, :, :], 0.0))
                end_stage(dve, "dve")

                bd4 = [P, 4, 2, CH]
                mask4 = lambda m_: bc(m_.rearrange("p (a b) -> p a b", a=2), bd4, 1)
                wide = lambda s_: bc(s_, bd4, 2)
                q4 = lambda x_: x_[:, :, :].rearrange("p a (b c) -> p a b c", b=2)
                for c in range(NCH):
                    cc = slice(c * CH, (c + 1) * CH)
                    if c:
                        dve.wait_ge(S("r_yc"), at("r_yc", l, c - 1))
                    for o, src in ((Bbd, AI), (Kbd, KK), (Hbd, K), (VTbd, V)):
                        ins = tt(q4(o), wide(src[:, :, cc]), mask4(C("bd")), ALU.mult)
                    ins.then_inc(S("r_bd"), 1)
                    dve.wait_ge(S("r_mm"), at("r_mm", l, c))
                    M1T = PS[:, 0, 0:256].rearrange("p (a b) -> p a b", b=CH)
                    M2T = PS[:, 0, 256:512].rearrange("p (a b) -> p a b", b=CH)
                    v(tt(q4(TT), wide(M1T), mask4(C("level", 0, P)), ALU.mult))
                    v(tt(TT[:, :, :], bc(C("ident"), [P, 4, P], 1), TT[:, :, :], ALU.subtract))
                    dve.memset(small[:, 62:63], 0.0).then_inc(S("r_tt"), 1)
                    for w in range(5):
                        tt(q4(NTb), wide(M1T), mask4(C("level", (w + 1) * P, P)), ALU.mult).then_inc(S("r_lv"), 1)
                        if w == 0:
                            tt(q4(M2bd), wide(M2T), mask4(C("strict")), ALU.mult)
                            tt(AA[:, :, :], PS[:, 1, :].rearrange("p (a b) -> p a b", b=CH), bc(C("incl"), [P, 8, CH], 1), ALU.mult)
                            dve.wait_ge(S("r_vc"), NCH * l + c + 1)
                            tt(q4(Vbd), wide(Vst), mask4(C("bd")), ALU.mult).then_inc(S("r_cp"), 1)
                        dve.wait_ge(S("r_d"), at("r_d", l, 5 * c + w))
                        ins = tt(TT[:, :, :].rearrange("p a b -> p (a b)"), TT[:, :, :].rearrange("p a b -> p (a b)"), PS[:, 6, :], ALU.subtract)
                        if w < 4:
                            ins = tt(TI[:, :, :].rearrange("p a b -> p (a b)"), TI[:, :, :].rearrange("p a b -> p (a b)"), PS[:, 7, :], ALU.subtract)
                            v(ins)
                        else:
                            ins.then_inc(S("r_tr"), 1)
                    dve.wait_ge(S("r_uc"), at("r_uc", l, c))
                    tt(q4(Ubd), wide(Ust), mask4(C("bd")), ALU.mult).then_inc(S("r_ust"), 1)
                    dve.wait_ge(S("r_s"), at("r_s", l, c))
                    v(tt(state[:, :, :], state[:, :, :], PS[:, 5, 0:256].rearrange("p (a b) -> p a b", b=CH), ALU.add))
                    v(tt(state[:, :, :], state[:, :, :], bc(egc[:, :, c], [P, 4, CH], 2), ALU.mult))
                    v(tt(q4(Sbd), wide(state[:, :, :]), mask4(C("bd")), ALU.mult))
                end_stage(dve, "dve")
                dve.wait_ge(S("n_m"), at("n_m", l, 0))
                dve.scalar_tensor_tensor(Y[:, :, TR], PS[:, 0:4, 0:T], -1.0 / HD, Y[:, :, TR], ALU.mult, ALU.add).then_inc(S("n_d"), 1)
                dve.wait_ge(S("n_v"), at("n_v", l, 0))
                dve.tensor_scalar(K[:, :, TR], PS[:, 4:8, 0:T], 1.0 / HD, GN_EPS, ALU.mult, ALU.add).then_inc(S("n_e"), 1)
                dve.wait_ge(S("n_s"), at("n_s", l, 0))
                v(dve.reciprocal(K[:, :, TR], K[:, :, TR]))
                v(tt(Y[:, :, TR], Y[:, :, TR], K[:, :, TR], ALU.mult))
                for p in range(4):
                    ins = dve.tensor_scalar(Y[:, p, TR], Y[:, p, TR], prm_col(l, "ln_g", p), prm_col(l, "ln_b", p), ALU.mult, ALU.add)
                v(ins)
                v(tt(Y[:, :, TR], Y[:, :, TR], BN[:, :, TR], ALU.add))
                v(tt(R[:, :, TR], Y[:, :, TR], GT[:, :, TR], ALU.mult))
                end_stage(dve, "dve")
                for n in range(24):
                    d_ = n % 8
                    dve.wait_ge(S("m_p"), at("m_p", l, n))
                    dve.wait_ge(S("m_s"), at("m_s", l, n))
                    if n < 8:
                        tt(MG[:, d_, :], SG[:, n % 2, :], PS[:, 4 + n % 4, 0:T], ALU.mult).then_inc(S("m_acc"), 1)
                    else:
                        v(tt(TMP[:, n % 2, :], SG[:, n % 2, :], PS[:, 4 + n % 4, 0:T], ALU.mult))
                        tt(MG[:, d_, :], MG[:, d_, :], TMP[:, n % 2, :], ALU.add).then_inc(S("m_acc"), 1)
                for n in range(8):
                    dve.wait_ge(S("o_mm"), at("o_mm", l, n))
                    ins = tt(hT[:, n, :], hT[:, n, :], PS[:, n, 0:T], ALU.add)
                v(ins)
                end_stage(dve, "dve")
                v(norm(l, 1, "norm_ffn"))
                end_stage(dve, "dve")
                if l == 0:
                    for f in range(FG):
                        for i in range(4):
                            dve.wait_ge(S("f_mm"), 8 * f + 4 + i + 1)
                            dve.wait_ge(S("f_s"), 4 * f + i + 1)
                            tt(HF[:, 4 * f + i, :], SF[:, i, :], PS[:, 4 + i, 0:T], ALU.mult).then_inc(S("f_h"), 1)
                    dve.wait_ge(S("f_down"), 1)
                    v(tt(hT[:, :, :], hT[:, :, :], PS[:, :, 0:T], ALU.add))
                    end_stage(dve, "dve")

            dve.wait_ge(S("q_log"), 1)
            idx = MR[:, 96:112].bitcast(U32)
            v(dve.tensor_copy(MR[:, 0:16], PS[:, 0, 0:16]))
            for t in range(2):
                v(dve.max(MR[:, 112 + 8 * t:120 + 8 * t], MR[:, 8 * t:8 * t + 8]))
                v(dve.max_index(idx[:, 8 * t:8 * t + 8], MR[:, 112 + 8 * t:120 + 8 * t], MR[:, 8 * t:8 * t + 8]))
            v(dve.tensor_copy(MR[:, 128:144], idx))
            for t in range(2):
                v(tt(MR[:, 80 + t:81 + t], MR[:, 113 + 8 * t:114 + 8 * t], MR[:, 112 + 8 * t:113 + 8 * t], ALU.subtract))
            dve.memset(small[:, 63:64], 0.0).then_inc(S("q_gap"), 1)
            dve.wait_ge(S("q_exp"), 1)
            v(dve.tensor_scalar(MR[:, 82:84], MR[:, 80:82], 1.0, None, ALU.add))
            v(dve.reciprocal(MR[:, 82:84], MR[:, 82:84]))
            v(tt(MR[:, 84:86], MR[:, 80:82], MR[:, 82:84], ALU.mult))
            for t in range(2):
                sel, gate = MR[:, 16 + 8 * t:24 + 8 * t], MR[:, 32 + 8 * t:40 + 8 * t]
                one, two = MR[:, 48:56], MR[:, 56:64]
                v(dve.tensor_scalar(one, C("iota8"), MR[:, 128 + 8 * t:129 + 8 * t], None, ALU.is_equal))
                v(dve.tensor_scalar(two, C("iota8"), MR[:, 129 + 8 * t:130 + 8 * t], None, ALU.is_equal))
                v(tt(sel, one, two, ALU.add))
                v(dve.tensor_scalar(one, one, MR[:, 82 + t:83 + t], None, ALU.mult))
                v(dve.scalar_tensor_tensor(gate, two, MR[:, 84 + t:85 + t], one, ALU.mult, ALU.add))
            dve.memset(small[:, 63:64], 0.0).then_inc(S("q_sel"), 1)
            dve.wait_ge(S("q_rank"), 1)
            for t in range(2):
                slot = MR[:, 64 + 8 * t:72 + 8 * t]
                v(dve.scalar_tensor_tensor(slot, PS[:, 5, 8 * t:8 * t + 8], 1.0, MR[:, 16 + 8 * t:24 + 8 * t], ALU.add, ALU.mult))
                v(dve.tensor_scalar(slot, slot, -1.0, None, ALU.add))
            v(dve.tensor_reduce(small[:, 41:42], PS[:, 5, 16:24], AX.X, ALU.max))
            dve.tensor_scalar(small[:, 40:41].bitcast(I32), small[:, 41:42], float(SLOTS), None, ALU.is_gt).then_inc(S("route_flag"), 1)
            dve.wait_ge(S("route_flag"), 1)
            end_stage(dve, "dve")

            def experts(again):
                base = again * NE
                with dve.Fori(0, NE) as e:
                    if again == 0:
                        pass
                    for t in range(2):
                        slot = MR[:, 64 + 8 * t:72 + 8 * t][:, bass.ds(e, 1)]
                        gate = MR[:, 32 + 8 * t:40 + 8 * t][:, bass.ds(e, 1)]
                        v_e(e, base, 4 * t, dve.tensor_copy(MR[:, 144:145], slot))
                        v_e(e, base, 4 * t + 1, dve.tensor_copy(MR[:, 145:146], gate))
                        v_e(e, base, 4 * t + 2, dve.tensor_scalar(SEL[:, t, :], C("iota", again * SLOTS, SLOTS), MR[:, 144:145], None, ALU.is_equal))
                        v_e(e, base, 4 * t + 3, dve.tensor_scalar(SEL[:, 2 + t, :], SEL[:, t, :], MR[:, 145:146], None, ALU.mult))
                    dve.memset(small[:, 63:64], 0.0).then_inc(S("e_sel"), 1)
                    dve.memset(small[:, 59:60], 0.0).then_inc(S("e_free"), 1)
                    for f in range(FG):
                        dve.wait_ge(S("e_mm"), e * (2 * FG) + (2 * base * FG + 2 * f + 2))
                        dve.wait_ge(S("e_s"), e * FG + (base * FG + f + 1))
                        if f >= 2:
                            dve.wait_ge(S("e_dn"), e * FG + (base * FG + f - 1))
                        tt(MH[:, f % 2, :], MS[:, f % 2, :], PS[:, 2 * (f % 2) + 1, :], ALU.mult).then_inc(S("e_h"), 1)
                    dve.wait_ge(S("e_sc"), e + (base + 1))
                    ins = tt(hT[:, :, META:T].rearrange("p (a b) n -> p a b n", b=2), hT[:, :, META:T].rearrange("p (a b) n -> p a b n", b=2),
                             PS[:, 0:4, :].rearrange("p a (b n) -> p a b n", b=2), ALU.add)
                    v_e(e, base, 8, ins)

            def v_e(e, base, i, ins):
                ins.then_inc(S("e_chain"), 1)
                dve.wait_ge(S("e_chain"), e * 9 + (base * 9 + i + 1))

            experts(0)
            with overflow_branch(dve):
                experts(1)
            end_stage(dve, "dve")
            norm(DEPTH, 0, "norm_final").then_inc(S("fin"), 1)

    return nc


def constant_array():
    c = np.zeros((P, NCONST), np.float32)

    def put(name, v):
        o, w = CONST_COLS[name]
        assert v.shape[1] == w
        c[:v.shape[0], o:o + w] = v

    i = np.arange(P)
    row, col = i[:, None], i[None, :]
    head = (row // HD) == (col // HD)
    put("ident", row == col)
    put("ones", np.ones((P, P)))
    put("headones", head)
    put("negsuffix", -1.0 * (row >= col))
    put("negones", -np.ones((P, P)))
    put("negmask", -1e30 * (row >= col))
    put("before", row < col)
    sb = np.ones((P, 432))
    sb[:, 0:P] = row < col
    sb[:, T:T + P] = row < col
    sb[:, 416:432] = (row < col)[:, 0:16]
    put("sbmask", sb)
    rs, cs = row % CH, col % CH
    level = []
    for v in range(6):
        b = 1 << v
        level.append(head & (rs // (2 * b) == cs // (2 * b)) & (rs // b % 2 == 0) & (cs // b % 2 == 1))
    put("level", np.concatenate(level, 1))
    put("strict", head & (rs < cs))
    put("bd", head)
    put("incl", (row % CH) <= np.arange(CH)[None, :])
    put("stack", (row % CH) == np.arange(CH)[None, :])
    put("reset", np.tile((np.arange(TP) % CH != 0)[None], (P, 1)))
    put("iota", np.tile(np.arange(2 * P)[None], (P, 1)))
    put("iota8", np.tile(np.arange(NE)[None], (P, 1)))
    n = np.maximum(LINE_TOP - np.arange(LINE), 0)
    large = 16 + (np.log(np.maximum(n, 1).astype(np.float32) / np.float32(16)) / np.float32(np.log(8.0)) * np.float32(16)).astype(np.int32)
    bucket = np.where(n < 16, n, np.minimum(large, NBUCKET - 1))
    put("bucket", np.arange(NBUCKET)[:, None] == bucket[None])
    return c


def parameter_array(a):
    out = np.zeros((DEPTH, P, NPARAM), np.float32)
    for l in range(DEPTH):
        def put(name, v):
            o, w = PARAM_COLS[name]
            out[l, :v.shape[0], o:o + w] = v

        tiles = lambda v: np.asarray(v).reshape(-1, P).T
        mu = np.asarray(a["tshift_mu"][l])
        b = COL_R
        put("norm_mix", tiles(a["norm_mix"][l]))
        put("norm_ffn", tiles(a["norm_ffn"][l]))
        put("mu_r", tiles(mu[0:512]))
        put("mu_k", tiles(mu[COL_K - b:COL_K - b + 512]))
        put("mu_v", tiles(mu[COL_V - b:COL_V - b + 512]))
        put("mu_wa", np.concatenate([mu[COL_W - b:COL_W - b + 64], mu[COL_A - b:COL_A - b + 64]])[:, None])
        put("mu_g0", mu[COL_G - b:COL_G - b + P][:, None])
        put("mu_g1", mu[COL_G - b + P:COL_G - b + P + 32][:, None])
        for n, k in (("w0", "rwkv_w0"), ("a0", "rwkv_a0"), ("k_k", "rwkv_k_k"), ("k_a", "rwkv_k_a"), ("r_k", "rwkv_r_k"),
                     ("ln_g", "rwkv_ln_g"), ("ln_b", "rwkv_ln_b")):
            put(n, tiles(np.asarray(a[k][l]).reshape(-1)))
        if l:
            put("vres_mu", tiles(a["vres_mu"][l - 1]))
            put("vres_b", tiles(a["vres_b"][l - 1]))
        sinks = np.asarray(a["sinks"][l])
        put("sink", np.repeat(sinks.reshape(4, 2).T, 64, axis=0))
        put("sink_meta", np.repeat(sinks.reshape(2, 4).T, META, axis=0))
        put("norm_final", tiles(a["norm_final"]))
    return out


_PLAIN = ["x", "meta_tokens", "w_in", "w_proj_a", "w_proj_b", "w_proj_c", "w_out", "dense_w_gate", "dense_w_up", "dense_w_down",
          "moe_router", "moe_w_gate", "moe_w_up", "moe_w_down", "rwkv_w2", "rwkv_a2", "rwkv_g2", "vres_w1", "vres_w2", "rel_bias"]


def kernel(**inputs):
    import concourse.bacc as bacc
    from concourse.bass_utils import run_bass_kernel_spmd

    nc = bacc.Bacc("TRN2", target_bir_lowering=False, num_devices=1)
    arrays, args = {}, []
    given = [(n, np.ascontiguousarray(inputs[n])) for n in _PLAIN]
    given += [("consts", constant_array()), ("params", parameter_array(inputs))]
    for name, a in given:
        arrays[f"in_{name}"] = a
        args.append(nc.dram_tensor(f"in_{name}", a.shape, mybir.dt.from_np(a.dtype), kind="ExternalInput").ap())
    args.append(nc.dram_tensor("out_0", (1, SEQ, D), F32, kind="ExternalOutput").ap())
    build_trunk(nc, *args)
    r = run_bass_kernel_spmd(nc, [arrays], core_ids=[0])
    return r.results[0]["out_0"]
```

```python
from contextlib import ExitStack

import numpy as np

import concourse.bass as bass
from concourse import mybir

F32 = mybir.dt.float32
F32R = mybir.dt.float32r
I32 = mybir.dt.int32
U32 = mybir.dt.uint32
ALU = mybir.AluOpType
ACT = mybir.ActivationFunctionType
AX = mybir.AxisListType

P = 128
D = 1024
KT = D // P
SEQ, META = 256, 16
T = SEQ + META
DEPTH = 2
HD = 64
HALF = D // 2
NP_ = HALF // P
CH = 64
PADC = 48
TP = T + PADC
NCH = TP // CH
NXC = SEQ // CH
FF = 3584
FG = FF // 512
NE = 8
SLOTS = 128
PASSES = -(-SEQ // SLOTS)
N_IN = 7200
COL_R, COL_W, COL_K, COL_V, COL_A, COL_G = 1536, 2048, 2112, 2624, 3136, 3200
COL_CQ, COL_CK, COL_GATE = 3360, 3872, 4128
NBUCKET = 32
LINE = 336
LINE_TOP = T - 1
RING = 3
EPS = 1e-6
GN_EPS = 64e-5
DECAY_SCALE = -float(np.exp(-0.5))
QS = HD ** -0.5

CONST_COLS = {}
_at = 0
for _n, _w in (("ident", P), ("ones", P), ("headones", P), ("negsuffix", P), ("negones", P), ("negmask", P),
               ("before", P), ("sbmask", 432), ("level", 6 * P), ("strict", P), ("bd", P), ("incl", CH),
               ("stack", CH), ("reset", TP), ("iota", 2 * P), ("iota8", NE), ("bucket", LINE)):
    CONST_COLS[_n] = (_at, _w)
    _at += _w
NCONST = _at

PARAM_COLS = {}
_at = 0
for _n, _w in (("norm_mix", KT), ("norm_ffn", KT), ("mu_r", 4), ("mu_k", 4), ("mu_v", 4), ("mu_wa", 1),
               ("mu_g0", 1), ("mu_g1", 1), ("w0", 4), ("a0", 4), ("k_k", 4), ("k_a", 4), ("r_k", 4),
               ("ln_g", 4), ("ln_b", 4), ("vres_mu", KT), ("vres_b", 4), ("sink", 4), ("sink_meta", 2),
               ("norm_final", KT)):
    PARAM_COLS[_n] = (_at, _w)
    _at += _w
NPARAM = _at

PER_LAYER = dict(
    sq_done=2, sum_done=2, rstd_done=2,
    proj_done=32, proj_copied=32,
    z_done=8, sp_done=8, arg_done=8, at_done=8, ya_done=4, ya_copied=4,
    c_z=5, c_s=5, c_m=5, c_e=5, c_r=5, c_p=5, c_t=5, c_tc=5, c_y=5, c_yc=5, c_vt=1, c_vtc=1,
    w_mm=3, w_ev=3, w_in=1, v_mm=2, v_ev=2, k_sq=1, k_sum=1, k_rt=1, k_mul=1, b_pr=1, b_sum=1, b_bn=1,
    g_done=1, e_done=3, e_used=3,
    r_bd=5, r_kbd=5, r_kr=5, r_open=1,
    n_m=1, n_d=1, n_sq=1, n_v=1, n_e=1, n_s=1,
    m_g=24, m_p=24, m_s=24, m_acc=24, o_mm=8, o_add=8,
)


def weight_chunks(w_in, w_a, w_b, w_c, w_out, dg, du, dd):
    out = []
    rows = lambda w: w.rearrange("(k p) n -> p k n", p=P)
    for l in range(DEPTH):
        wl = rows(w_in[l])

        def cols(name, c0, n):
            out.append((l, name, "k", [(slice(0, 4), 0, n, wl[:, 0:4, c0:c0 + n]),
                                       (slice(4, 8), 0, n, wl[:, 4:8, c0:c0 + n])]))

        cols("Aq", 0, 512)
        cols("Ak", 512, 512)
        cols("Av", 1024, 512)
        out.append((l, "Cq", "q", [(g, 0, 0, wl[:, :, COL_CQ + 256 * g:COL_CQ + 256 * (g + 1)]
                                    .rearrange("p k (j d) -> p k j d", j=4)) for g in range(2)]))
        cols("Ckv", COL_CK, 256)
        cols("Br", COL_R, 512)
        cols("Bk", COL_K, 512)
        cols("Bv", COL_V, 512)
        out.append((l, "Bx", "k", [(slice(0, 8), 0, 64, wl[:, :, COL_W:COL_W + 64]),
                                   (slice(0, 8), 64, 224, wl[:, :, COL_A:COL_A + 224])]))
        for b, wp in enumerate((w_a, w_b, w_c)):
            if b < 2:
                wr = rows(wp[l])
                out.append((l, f"P{b}", "w", [(slice(0, 2), 0, 0, wr[:, 0:2, :]), (slice(2, 4), 0, 0, wr[:, 2:4, :])]))
            else:
                wc = wp[l].rearrange("(g j d) n -> g d j n", g=2, j=4)
                out.append((l, "P2", "c", [(g, 0, 0, wc[g]) for g in range(2)]))
            for h in range(2):
                cols(f"G{b}{h}", COL_GATE + D * b + 512 * h, 512)
        wo = rows(w_out[l])
        for h in range(2):
            out.append((l, f"O{h}", "k", [(slice(0, 4), 0, 512, wo[:, 0:4, 512 * h:512 * h + 512]),
                                          (slice(4, 8), 0, 512, wo[:, 4:8, 512 * h:512 * h + 512])]))
        if l == 0:
            for f in range(FG):
                for nm, w in (("DG", dg), ("DU", du)):
                    wr = rows(w[0])
                    out.append((l, f"{nm}{f}", "k",
                                [(slice(0, 4), 0, 512, wr[:, 0:4, 512 * f:512 * f + 512]),
                                 (slice(4, 8), 0, 512, wr[:, 4:8, 512 * f:512 * f + 512])]))
            for f in range(FG):
                wr = rows(dd[0, 512 * f:512 * f + 512, :])
                out.append((l, f"DD{f}", "w", [(slice(0, 2), 0, 0, wr[:, 0:2, :]), (slice(2, 4), 0, 0, wr[:, 2:4, :])]))
    return out


def build_trunk(nc, x, meta, w_in, w_a, w_b, w_c, w_out, dg, du, dd, router, mg, mu_, md, w2, a2, g2, vw1, vw2,
                rel_bias, consts, params, out):
    chunks = weight_chunks(w_in, w_a, w_b, w_c, w_out, dg, du, dd)
    position = {(l, n): i for i, (l, n, _, _) in enumerate(chunks)}
    MOE0 = len(chunks)
    line = nc.dram_tensor("bias_line", (NE, CH, LINE), F32, kind="Internal").ap()

    with ExitStack() as ctx:
        def sb(name, shape, dt=F32):
            return ctx.enter_context(nc.sbuf_tensor(name, shape, dt))

        sems = {}

        def S(name):
            if name not in sems:
                sems[name] = ctx.enter_context(nc.semaphore(name))
            return sems[name]

        def at(name, l, i):
            assert 0 <= i < PER_LAYER[name], name
            return l * PER_LAYER[name] + i + 1

        ring = [sb(f"ring{i}", [P, 4096]) for i in range(RING)]
        hT = sb("hT", [P, KT, T])
        xn = sb("xn", [P, KT, T + 1])
        cst = sb("cst", [P, NCONST])
        prm = sb("prm", [P, DEPTH, NPARAM])
        wwa = sb("wwa", [P, HALF])
        wg0 = sb("wg0", [P, HALF])
        wg1 = sb("wg1", [32, HALF])
        vw1_sb = sb("vw1_sb", [P, KT, 32])
        vw2_sb = sb("vw2_sb", [32, HALF])
        router_sb = sb("router_sb", [P, KT, NE])
        relb = sb("relb", [NBUCKET, NE])
        lin = sb("lin", [NE, LINE])
        bias0 = sb("bias0", [P, 4, 80])
        biasb = sb("biasb", [P, 4, P])
        biasm = sb("biasm", [P, 3, 4, META])
        biasq = sb("biasq", [64, 2, META])
        yA = sb("yA", [P, NP_, T])
        yC = sb("yC", [P, NP_, T])
        VF = sb("VF", [P, NP_, TP])
        rstd = sb("rstd", [P, T])
        egc = sb("egc", [P, NP_, NCH])
        state = sb("state", [P, NP_, CH])
        small = sb("small", [P, 64])
        def pinned(name, shape, offset):
            return nc.alloc_sbuf_tensor_at(name, shape, F32R, offset=offset)

        at1 = -(-nc.sbuf_base // 32) * 32
        area1 = sb("area1", [P, 2 * 3 * 2048])
        at2 = -(-nc.sbuf_base // 32) * 32
        area2 = sb("area2", [P, 12544])
        WH = [pinned(f"WH{i}", [P, 2048], at1 + 4 * 2048 * 2 * i) for i in range(3)]
        WL = [pinned(f"WL{i}", [P, 2048], at1 + 4 * 2048 * (2 * i + 1)) for i in range(3)]
        XGH, XGL, HTH, HTL = [pinned(nm, [P, 1024 if i < 2 else 512], at2 + 4 * o)
                              for i, (nm, o) in enumerate((("XGH", 8448), ("XGL", 9472), ("HTH", 10496), ("HTL", 11008)))]
        PS = ctx.enter_context(nc.psum_tensor("PS", [P, 8, 512], F32))

        def C(name, lo=0, n=None):
            o, w = CONST_COLS[name]
            return cst[:, o + lo:o + (w if n is None else lo + n)]

        def prm_col(l, name, i):
            o, w = PARAM_COLS[name]
            return prm[:, l, o + i:o + i + 1]

        def carve(area, specs):
            got, o = [], 0
            for shape in specs:
                n = int(np.prod(shape))
                v = area[:, o:o + n]
                if len(shape) == 2:
                    v = v.rearrange("p (a b) -> p a b", b=shape[1])
                if len(shape) == 3:
                    v = v.rearrange("p (a b c) -> p a b c", b=shape[1], c=shape[2])
                got.append(v)
                o += n
            assert o <= area.shape[1], (o, area.shape)
            return got

        (xin,) = carve(area1, [(3, D)])
        qA, kA, vA, uA, spA, atA = carve(area1, [(4, T), (4, 384), (3, 512), (2, 432), (2, 432), (2, 432)])
        qCm, qCx, kC, vC, vW, sC, mC, pTC, pTm = carve(
            area1, [(4, META), (NXC, 4, CH), (T,), (T,), (4, P), (4, 144), (32,), (4, P), (4, P)])
        (Bbd, Kbd, Hbd, VTbd, Vbd, Ubd, Sbd, BT, HT, TT, TI, PW, NTb, M2bd) = carve(area1, [(4, P)] * 14)[:14]
        AA, Vst, Xst, Ust, KR = carve(area1[:, 14 * 512:], [(8, CH), (4, CH), (4, CH), (4, CH), (8, CH)])
        R, K, V, LW, G, AI, KK, DD, GT = carve(area2, [(4, TP)] * 9)
        (PX,) = carve(area2[:, 9 * 4 * TP:], [(3, TP)])
        Y, BN = LW, G
        (_, MG, SG, TMP) = carve(area2, [(4, TP), (KT, T), (2, T), (2, T)])
        (_, HF, SF) = carve(area2, [(KT, T), (28, T), (4, T)])
        (SQ,) = carve(area2, [(KT, T)])
        LWG, SV = G, KK
        SQ_v = area2[:, 6 * 4 * TP:6 * 4 * TP + KT * T].rearrange("p (a b) -> p a b", b=T)
        (_, hnT, MS, MH, SEL, SELT, YE, MR) = carve(
            area2, [(KT, T), (2, D), (512,), (512,), (4, SLOTS), (SEQ,), (D,), (192,)])
        ostage = area2[:, 0:2 * D].rearrange("p (a n) -> p a n", a=2)

        STREAM = dict(mm=1, tt=1, t=1, ti=5, ttc=5, lv=5, cp=1, p=5, pw=5, d=5, x=1, xc=1, u=1, uc=1, ubd=1,
                      y=1, yc=1, s=1, st=1, tr=1, vc=1)

        def W(name, s_, l, c, i=0):
            return S(f"r{s_}_{name}"), (l * NCH + c) * STREAM[name] + i + 1

        n_linked = {}

        def link(eng, ins, name):
            n_linked[name] = n_linked.get(name, 0) + 1
            ins.then_inc(S(name), 1)
            eng.wait_ge(S(name), n_linked[name])

        ENGINES = ("pe", "act", "dve")
        stage_no = dict.fromkeys(ENGINES, 0)

        def end_stage(eng, who):
            stage_no[who] += 1
            eng.drain().then_inc(S(f"{who}_stage"), 1)
            for other in ENGINES:
                if other != who:
                    eng.wait_ge(S(f"{other}_stage"), stage_no[who])

        def bc(v, shape, axis):
            return v.unsqueeze(axis).broadcast_to(shape)

        N_SETUP = 13

        block = ctx.enter_context(nc.Block())

        landed_at = []
        total = [0] * RING
        for i, (_, _, kind, _) in enumerate(chunks):
            total[i % RING] += 256 if kind == "q" else 32
            landed_at.append(total[i % RING])
        landed_moe0 = list(total)

        MOE_ORDER = []
        for f in range(FG):
            MOE_ORDER.append(("g", f))
            if f:
                MOE_ORDER.append(("d", f - 1))
            MOE_ORDER.append(("u", f))
        MOE_ORDER.append(("d", FG - 1))
        assert len(MOE_ORDER) % RING == 0
        PER_BUF = len(MOE_ORDER) // RING
        HALVES = 2 * len(MOE_ORDER)
        AHEAD = 6
        POOL_COLS = 768
        assert HALVES % 3 == 0
        first_half = {key: 2 * i for i, key in enumerate(MOE_ORDER)}

        def used(n, kind, f, half=1):
            return n * HALVES + (first_half[(kind, f)] + half + 1 + 3)

        def at_half(events, kind, f, half, later):
            events.setdefault(min(first_half[(kind, f)] + half + later, HALVES - 1), [])
            return events[min(first_half[(kind, f)] + half + later, HALVES - 1)]

        def expert_loads(sp, e, n, run):
            for i, (kind, f) in enumerate(MOE_ORDER):
                b = (MOE0 + i) % RING
                w = {"g": mg, "u": mu_, "d": md}[kind]
                if kind == "d":
                    src = w[0, e, 512 * f:512 * f + 512, :].rearrange("(k p) n -> p k n", p=P)
                    dst = ring[b][:, :].rearrange("p (k n) -> p k n", k=4)
                    halves = [(dst[:, 0:2], src[:, 0:2]), (dst[:, 2:4], src[:, 2:4])]
                else:
                    src = w[0, e, :, 512 * f:512 * f + 512].rearrange("(k p) n -> p k n", p=P)
                    dst = ring[b][:, :].rearrange("p (k n) -> p k n", k=8)
                    halves = [(dst[:, 0:4], src[:, 0:4]), (dst[:, 4:8], src[:, 4:8])]
                for lo in ("w_lo_dve", "w_lo_pool"):
                    sp.wait_ge(S(lo), n * HALVES + (2 * i - 2 * RING + 2 + AHEAD))
                for d_, s_ in halves:
                    sp.dma_start(d_, s_).then_inc(S(f"landed{b}"), 16)

        def for_all_experts(eng, body, before=None):
            if before:
                before(eng, 0)
            with eng.Fori(0, NE) as e:
                body(eng, e, e, 0)
            with overflow_branch(eng):
                with eng.Fori(0, PASSES - 1) as again:
                    if before:
                        before(eng, again + 1)
                    with eng.Fori(0, NE) as e:
                        body(eng, e, again * NE + e + NE, again + 1)

        def overflow_branch(eng):
            eng.wait_ge(S("route_flag"), 1)
            flag = eng.value_load(small[0:1, 40:41].bitcast(I32), min_val=0, max_val=1)
            return eng.If(flag > 0)

        @block.sync
        def _(sp):
            for i, (l, name, kind, parts) in enumerate(chunks):
                buf = ring[i % RING]
                if i >= RING:
                    sp.wait_ge(S("chunk_used"), i - RING + 1)
                for a, c0, n, src in parts:
                    if kind == "k":
                        dst = buf[:, :].rearrange("p (k n) -> p k n", k=8)[:, a, c0:c0 + n]
                    elif kind == "w":
                        dst = buf[:, :].rearrange("p (k n) -> p k n", k=4)[:, a, :]
                    elif kind == "c":
                        dst = buf[64 * a:64 * a + 64, :].rearrange("p (k n) -> p k n", k=4)
                    else:
                        dst = buf[:, :].rearrange("p (k j g d) -> p k j g d", k=8, j=4, g=2)[:, :, :, a, :]
                    if kind == "q":
                        for k in range(KT):
                            sp.dma_start(dst[:, k], src[:, k]).then_inc(S(f"landed{i % RING}"), 16)
                    else:
                        sp.dma_start(dst, src).then_inc(S(f"landed{i % RING}"), 16)
            for_all_experts(sp, expert_loads)
            for h in range(2):
                sp.wait_ge(S("out_copied"), 2 * h + 2)
                sp.dma_start(out[0, h * P:(h + 1) * P, :], ostage[:, h, :]).then_inc(S("out_stored"), 16)
            sp.wait_ge(S("out_stored"), 32)

        @block.tensor
        def _(pe):
            used = [0]

            def chunk(l, name):
                i = position[(l, name)]
                assert i == used[0], (l, name, i, used[0])
                pe.wait_ge(S(f"landed{i % RING}"), landed_at[i])
                return ring[i % RING]

            def release(ins):
                ins.then_inc(S("chunk_used"), 1)
                used[0] += 1

            def k8(buf, n=512):
                return buf[:, :].rearrange("p (k n) -> p k n", k=8)[:, :, 0:n]

            def k4(buf):
                return buf[:, :].rearrange("p (k n) -> p k n", k=4)

            def spare():
                return pe.drain()

            def norm(l, which):
                pe.wait_ge(S("sq_done"), at("sq_done", l, which) if l < DEPTH else 2 * DEPTH + 1)
                for k in range(KT):
                    ins = pe.matmul(PS[:, 0, 0:T], C("ones"), SQ[:, k, :], start=(k == 0), stop=(k == KT - 1))
                ins.then_inc(S("sum_done"), 1)

            def project(l, tiles, n0):
                for i, (w, lo) in enumerate(tiles):
                    n = n0 + i
                    if i >= 8:
                        pe.wait_ge(S("proj_copied"), at("proj_copied", l, n - 8))
                    bank = i % 8
                    m = w(0).shape[1]
                    for k in range(KT):
                        ins = pe.matmul(PS[lo:lo + m, bank, 0:T], w(k), xn[:, k, 1:T + 1], start=(k == 0), stop=(k == KT - 1))
                    yield ins

            def column_tiles(l, name, widths, n0, first):
                buf = k8(chunk(l, name))
                c = 0
                for i, m in enumerate(widths):
                    n = n0 + i
                    if n >= 8 and first + i >= 8:
                        pe.wait_ge(S("proj_copied"), at("proj_copied", l, n - 8))
                    bank = (first + i) % 8
                    for k in range(KT):
                        ins = pe.matmul(PS[0:m, bank, 0:T], buf[:, k, c:c + m], xn[:, k, 1:T + 1],
                                        start=(k == 0), stop=(k == KT - 1))
                    c += m
                    ins.then_inc(S("proj_done"), 1)
                release(spare())

            pe.wait_ge(S("setup"), 16 * N_SETUP)
            for k in range(KT):
                pe.transpose(PS[:, k, 0:META], xin[0:META, 0, k * P:(k + 1) * P], C("ident")[0:META, 0:META])
                for t in range(2):
                    ins = pe.transpose(PS[:, k, META + t * P:META + (t + 1) * P], xin[:, 1 + t, k * P:(k + 1) * P], C("ident"))
                ins.then_inc(S("in_turned"), 1)
            pe.wait_ge(S("in_copied"), 1)
            pe.matmul(PS[0:NE, 0, 0:LINE], relb[:, :], C("bucket")[0:NBUCKET, :], start=True, stop=True).then_inc(S("line_done"), 1)
            end_stage(pe, "pe")

            for l in range(DEPTH):
                norm(l, 0)
                end_stage(pe, "pe")
                column_tiles(l, "Aq", [P] * 4, 0, 0)
                column_tiles(l, "Ak", [P] * 4, 4, 4)
                buf = k8(chunk(l, "Av"))
                for t, (t0, n) in enumerate(((0, P), (P, P), (2 * P, T - 2 * P))):
                    pe.wait_ge(S("proj_copied"), at("proj_copied", l, t))
                    for k in range(KT):
                        ins = pe.matmul(PS[0:n, t, :], xn[:, k, 1 + t0:1 + t0 + n], buf[:, k, :], start=(k == 0), stop=(k == KT - 1))
                    ins.then_inc(S("proj_done"), 1)
                release(spare())
                end_stage(pe, "pe")

                def zscores(h):
                    if h >= 2:
                        pe.wait_ge(S("at_done"), at("at_done", l, h - 2))
                    p, r, b = h // 2, 64 * (h % 2), 2 * (h % 2)
                    kh, qh = kA[r:r + 64, p], qA[r:r + 64, p]
                    pe.matmul(PS[:, b, 0:T], kh[:, 0:P], qh[:, 0:T], start=True, stop=False, skip_group_check=True)
                    pe.matmul(PS[:, b + 1, 0:144], kh[:, P:2 * P], qh[:, P:T], start=True, stop=False, skip_group_check=True)
                    pe.matmul(PS[:, b + 1, 144:160], kh[:, 2 * P:3 * P], qh[:, 2 * P:T], start=False, stop=False,
                              skip_group_check=True).then_inc(S("z_done"), 1)

                zscores(0)
                for h in range(8):
                    if h < 7:
                        zscores(h + 1)
                    s, b = h % 2, 2 * (h % 2)
                    pe.wait_ge(S("sp_done"), at("sp_done", l, h))
                    sp_ = spA[:, s, :]
                    mm = lambda o, a, b_: pe.matmul(o, a, b_, start=False, stop=False, skip_group_check=True)
                    mm(PS[:, b, 0:T], C("negsuffix"), sp_[:, 0:T])
                    mm(PS[:, b, P:T], C("negones"), sp_[:, T:T + 144])
                    mm(PS[:, b, 2 * P:T], C("negones"), sp_[:, 416:432])
                    mm(PS[:, b, 0:P], C("ident"), C("negmask"))
                    mm(PS[:, b + 1, 0:160], C("negsuffix"), sp_[:, T:432])
                    mm(PS[:, b + 1, P:144], C("negones"), sp_[:, 416:432])
                    mm(PS[:, b + 1, 0:P], C("ident"), C("negmask"))
                    pe.matmul(PS[:, b + 1, 144:160], C("ident"), C("negmask", 0, 16), start=False, stop=True,
                              skip_group_check=True).then_inc(S("arg_done"), 1)
                    pe.wait_ge(S("at_done"), at("at_done", l, h))
                    p, r, yb = h // 2, 64 * (h % 2), 4 + (h // 2) % 2
                    if r == 0 and p >= 2:
                        pe.wait_ge(S("ya_copied"), at("ya_copied", l, p - 2))
                    vh = lambda J: vA[:, J, h * 64:h * 64 + 64]
                    a_ = atA[:, s, :]
                    pe.matmul(PS[r:r + 64, yb, 0:T], vh(0), a_[:, 0:T], start=True, stop=False, skip_group_check=True)
                    pe.matmul(PS[r:r + 64, yb, P:T], vh(1), a_[:, T:T + 144], start=False, stop=False, skip_group_check=True)
                    ins = pe.matmul(PS[r:r + 64, yb, 2 * P:T], vh(2), a_[:, 416:432], start=False, stop=True, skip_group_check=True)
                    if r:
                        ins.then_inc(S("ya_done"), 1)
                end_stage(pe, "pe")

                column_tiles(l, "Cq", [P] * 4, 11, 0)
                column_tiles(l, "Ckv", [P] * 2, 15, 4)
                pe.wait_ge(S("proj_copied"), at("proj_copied", l, 16))
                for w, (t0, n) in enumerate(((0, 80), (META, P), (META + 64, P), (META + 128, P))):
                    ins = pe.transpose(PS[0:n, 6, w * P:(w + 1) * P], vC[:, t0:t0 + n], C("ident"))
                ins.then_inc(S("c_vt"), 1)
                pe.wait_ge(S("c_vtc"), at("c_vtc", l, 0))
                for u in range(5):
                    meta_q = u == 4
                    if meta_q and l == DEPTH - 1:
                        break
                    for g in range(2):
                        r = 64 * g
                        for jp in range(1 if meta_q else 2):
                            if meta_q:
                                lhs, o, m = qCm[r:r + 64, :, :].rearrange("p a b -> p (a b)"), 0, 64
                            else:
                                lhs = qCx[r:r + 64, u, 2 * jp:2 * jp + 2, :].rearrange("p a b -> p (a b)")
                                o, m = (80 if u == 0 else 144) * jp, P
                            keys = [(0, META)] if meta_q else [(0, 80)] if u == 0 else [(0, META), (META + 64 * (u - 1), P)]
                            for t0, n in keys:
                                ins = pe.matmul(PS[0:m, g, o:o + n], lhs, kC[r:r + 64, t0:t0 + n], start=True, stop=True)
                                o += n
                    ins.then_inc(S("c_z"), 1)
                    pe.wait_ge(S("c_p"), at("c_p", l, u))
                    units, m = (2, 64) if meta_q else (4, P)
                    for v in range(units):
                        if meta_q or u == 0:
                            n = META if meta_q else 80
                            ins = pe.transpose(PS[0:n, 2, v * m:(v + 1) * m], sC[0:m, v, 0:n], C("ident")[0:m, 0:m])
                        else:
                            pe.transpose(PS[:, 2, v * P:(v + 1) * P], sC[:, v, META:144], C("ident"))
                            ins = pe.transpose(PS[0:META, 3, v * P:(v + 1) * P], sC[:, v, 0:META], C("ident"))
                    ins.then_inc(S("c_t"), 1)
                    pe.wait_ge(S("c_tc"), at("c_tc", l, u))
                    for g in range(2):
                        vcols = slice(64 * g, 64 * g + 64)
                        if meta_q:
                            ins = pe.matmul(PS[64 * g:64 * g + 64, 4, 0:64], vW[0:META, 0, vcols],
                                            pTC[0:META, :, :].rearrange("p a b -> p (a b)")[:, 64 * g:64 * g + 64], start=True, stop=True)
                        elif u == 0:
                            ins = pe.matmul(PS[64 * g:64 * g + 64, 4, 0:256], vW[0:80, 0, vcols],
                                            pTC[0:80, 2 * g:2 * g + 2, :], start=True, stop=True)
                        else:
                            pe.matmul(PS[64 * g:64 * g + 64, 4, 0:256], vW[:, u, vcols],
                                      pTC[:, 2 * g:2 * g + 2, :], start=True, stop=False, skip_group_check=True)
                            ins = pe.matmul(PS[64 * g:64 * g + 64, 4, 0:256], vW[0:META, 0, vcols],
                                            pTm[0:META, 2 * g:2 * g + 2, :], start=False, stop=True, skip_group_check=True)
                    ins.then_inc(S("c_y"), 1)
                    pe.wait_ge(S("c_yc"), at("c_yc", l, u))
                end_stage(pe, "pe")

                column_tiles(l, "Br", [P] * 4, 17, 0)
                column_tiles(l, "Bk", [P] * 4, 21, 4)
                column_tiles(l, "Bv", [P] * 4, 25, 8)
                buf = k8(chunk(l, "Bx"))
                for i, (c, m, lo) in enumerate(((0, 64, 0), (64, 64, 64), (128, P, 0), (256, 32, 0))):
                    if i != 1:
                        pe.wait_ge(S("proj_copied"), at("proj_copied", l, 21 + max(i - 1, 0)))
                    bank = 4 + max(i - 1, 0)
                    for k in range(KT):
                        ins = pe.matmul(PS[lo:lo + m, bank, 0:T], buf[:, k, c:c + m], xn[:, k, 1:T + 1],
                                        start=(k == 0), stop=(k == KT - 1))
                    if i:
                        ins.then_inc(S("proj_done"), 1)
                release(spare())
                end_stage(pe, "pe")

                pe.wait_ge(S("w_in"), at("w_in", l, 0))
                for p in range(4):
                    ins = pe.matmul(PS[:, p, 0:T], wwa[0:64, p * P:(p + 1) * P], PX[0:64, 0, PADC:TP], start=True, stop=True)
                ins.then_inc(S("w_mm"), 1)
                for p in range(4):
                    ins = pe.matmul(PS[:, 4 + p, 0:T], wwa[64:P, p * P:(p + 1) * P], PX[64:P, 0, PADC:TP], start=True, stop=True)
                ins.then_inc(S("w_mm"), 1)
                pe.wait_ge(S("w_ev"), at("w_ev", l, 0))
                for p in range(4):
                    pe.matmul(PS[:, p, 0:T], wg0[:, p * P:(p + 1) * P], PX[:, 1, PADC:TP], start=True, stop=False)
                    ins = pe.matmul(PS[:, p, 0:T], wg1[:, p * P:(p + 1) * P], PX[0:32, 2, PADC:TP], start=False, stop=True)
                ins.then_inc(S("w_mm"), 1)
                if l:
                    pe.wait_ge(S("w_ev"), at("w_ev", l, 1))
                    pe.wait_ge(S("xv_done"), 1)
                    for k in range(KT):
                        ins = pe.matmul(PS[0:32, 4, 0:T], vw1_sb[:, k, :], SQ_v[:, k, :], start=(k == 0), stop=(k == KT - 1))
                    ins.then_inc(S("v_mm"), 1)
                    pe.wait_ge(S("v_ev"), 1)
                    for p in range(4):
                        ins = pe.matmul(PS[:, 4 + p, 0:T], vw2_sb[:, p * P:(p + 1) * P], PX[0:32, 1, PADC:TP], start=True, stop=True)
                    ins.then_inc(S("v_mm"), 1)
                end_stage(pe, "pe")
                pe.wait_ge(S("k_sq"), at("k_sq", l, 0))
                for p in range(4):
                    ins = pe.matmul(PS[:, p, 0:T], C("headones"), DD[:, p, PADC:TP], start=True, stop=True)
                ins.then_inc(S("k_sum"), 1)
                pe.wait_ge(S("b_pr"), at("b_pr", l, 0))
                for p in range(4):
                    ins = pe.matmul(PS[:, 4 + p, 0:T], C("headones"), DD[:, p, PADC:TP], start=True, stop=True)
                ins.then_inc(S("b_sum"), 1)
                end_stage(pe, "pe")

                def signal(ins, name, s_):
                    ins.then_inc(S(f"r{s_}_{name}"), 1)

                for c in range(NCH):
                    pairs = lambda s_: (2 * s_, 2 * s_ + 1)

                    def pair_products(s_):
                        if s_ == 0:
                            pe.wait_ge(S("r_bd"), at("r_bd", l, c))
                            pe.wait_ge(S("r_kr"), at("r_kr", l, c))
                        if c:
                            pe.wait_ge(*W("st", s_, l, c - 1))
                            pe.wait_ge(*W("yc", s_, l, c - 1))
                        b0 = 4 * s_
                        for j, p in enumerate(pairs(s_)):
                            kr = KR[:, 2 * p:2 * p + 2, :]
                            pe.matmul(PS[:, b0, 256 * j:256 * j + P], Bbd[:, p, :], kr, start=True, stop=True)
                            pe.matmul(PS[:, b0, 256 * j + P:256 * j + 256], Hbd[:, p, :], kr, start=True, stop=True)
                            pe.matmul(PS[:, b0 + 2, j * CH:(j + 1) * CH], VTbd[:, p, :], C("stack"), start=True, stop=True)
                            pe.transpose(PS[:, b0 + 1, j * P:(j + 1) * P], Bbd[:, p, :], C("ident"))
                            ins = pe.transpose(PS[:, b0 + 1, 256 + j * P:256 + (j + 1) * P], Hbd[:, p, :], C("ident"))
                        signal(ins, "mm", s_)

                    def turn_inverse(s_):
                        pe.wait_ge(*W("tt", s_, l, c))
                        for j, p in enumerate(pairs(s_)):
                            ins = pe.transpose(PS[:, 4 * s_ + 3, j * P:(j + 1) * P], TT[:, p, :], C("ident"))
                        signal(ins, "t", s_)

                    def level_product(s_, w):
                        pe.wait_ge(*W("lv", s_, l, c, w))
                        pe.wait_ge(*W("ti", s_, l, c, w))
                        if w == 0:
                            pe.wait_ge(*W("vc", s_, l, c))
                        for j, p in enumerate(pairs(s_)):
                            ins = pe.matmul(PS[:, 4 * s_ + 2, j * P:(j + 1) * P], NTb[:, p, :], TI[:, p, :], start=True, stop=True)
                        signal(ins, "p", s_)

                    def level_update(s_, w):
                        pe.wait_ge(*W("pw", s_, l, c, w))
                        if w:
                            pe.wait_ge(*W("ttc", s_, l, c, w - 1))
                        for j, p in enumerate(pairs(s_)):
                            if w < 4:
                                pe.matmul(PS[:, 4 * s_ + 1, j * P:(j + 1) * P], TT[:, p, :], PW[:, p, :], start=True, stop=True)
                            ins = pe.matmul(PS[:, 4 * s_ + 3, j * P:(j + 1) * P], PW[:, p, :], TT[:, p, :], start=True, stop=True)
                        signal(ins, "d", s_)

                    def right_side(s_):
                        pe.wait_ge(*W("cp", s_, l, c))
                        if s_ == 0:
                            pe.wait_ge(S("r_kbd"), at("r_kbd", l, c))
                        for j, p in enumerate(pairs(s_)):
                            o = PS[:, 4 * s_ + 2, j * CH:(j + 1) * CH]
                            pe.matmul(o, Kbd[:, p, :], state[:, p, :], start=True, stop=False, skip_group_check=True)
                            ins = pe.matmul(o, M2bd[:, p, :], Vst[:, p, :], start=False, stop=True, skip_group_check=True)
                        signal(ins, "x", s_)

                    def solve(s_):
                        pe.wait_ge(*W("xc", s_, l, c))
                        pe.wait_ge(*W("ttc", s_, l, c, 4))
                        for j, p in enumerate(pairs(s_)):
                            ins = pe.matmul(PS[:, 4 * s_ + 3, j * CH:(j + 1) * CH], TT[:, p, :], Xst[:, p, :], start=True, stop=True)
                        signal(ins, "u", s_)

                    def outputs(s_):
                        pe.wait_ge(*W("uc", s_, l, c))
                        for j, p in enumerate(pairs(s_)):
                            o = PS[:, 4 * s_, j * CH:(j + 1) * CH]
                            pe.matmul(o, BT[:, p, :], Ust[:, p, :], start=True, stop=False, skip_group_check=True)
                            ins = pe.matmul(o, HT[:, p, :], Vst[:, p, :], start=False, stop=True, skip_group_check=True)
                        signal(ins, "s", s_)
                        for j, p in enumerate(pairs(s_)):
                            o = PS[:, 4 * s_ + 1, j * CH:(j + 1) * CH]
                            pe.matmul(o, Sbd[:, p, :], KR[:, 2 * p + 1, :], start=True, stop=False, skip_group_check=True)
                            pe.matmul(o, Vbd[:, p, :], AA[:, 2 * p + 1, :], start=False, stop=False, skip_group_check=True)
                            if j == 0:
                                pe.wait_ge(*W("ubd", s_, l, c))
                            ins = pe.matmul(o, Ubd[:, p, :], AA[:, 2 * p, :], start=False, stop=True, skip_group_check=True)
                        signal(ins, "y", s_)

                    steps = [pair_products, turn_inverse]
                    for w in range(5):
                        steps += [lambda s_, w=w: level_product(s_, w), lambda s_, w=w: level_update(s_, w)]
                    steps += [right_side, solve, outputs]
                    for step in steps:
                        for s_ in range(2):
                            step(s_)
                end_stage(pe, "pe")
                for p in range(4):
                    ins = pe.matmul(PS[:, p, 0:T], C("headones"), Y[:, p, PADC:TP], start=True, stop=True)
                ins.then_inc(S("n_m"), 1)
                pe.wait_ge(S("n_sq"), at("n_sq", l, 0))
                for p in range(4):
                    ins = pe.matmul(PS[:, 4 + p, 0:T], C("headones"), K[:, p, PADC:TP], start=True, stop=True)
                ins.then_inc(S("n_v"), 1)
                end_stage(pe, "pe")

                ycur = [yA[:, :, :], R[:, :, PADC:TP], yC[:, :, :]]
                for b in range(3):
                    wp = k4(chunk(l, f"P{b}"))
                    i_p = used[0]
                    used[0] += 1
                    for h in range(2):
                        i_g = position[(l, f"G{b}{h}")]
                        pe.wait_ge(S(f"landed{i_g % RING}"), landed_at[i_g])
                        gb = k8(ring[i_g % RING])
                        for dt in range(4):
                            n = b * 8 + h * 4 + dt
                            if n >= 4:
                                pe.wait_ge(S("m_acc"), at("m_acc", l, n - 4))
                            bank = n % 4
                            for k in range(KT):
                                ins = pe.matmul(PS[:, bank, 0:T], gb[:, k, dt * P:(dt + 1) * P], xn[:, k, 1:T + 1],
                                                start=(k == 0), stop=(k == KT - 1))
                            ins.then_inc(S("m_g"), 1)
                            for k in range(4):
                                ins = pe.matmul(PS[:, 4 + bank, 0:T], wp[:, k, (4 * h + dt) * P:(4 * h + dt + 1) * P],
                                                ycur[b][:, k, :], start=(k == 0), stop=(k == 3))
                            ins.then_inc(S("m_p"), 1)
                        if h == 1:
                            pe.drain().then_inc(S("chunk_used"), 3)
                            used[0] += 2
                pe.wait_ge(S("m_acc"), at("m_acc", l, 23))
                for h in range(2):
                    ob = k8(chunk(l, f"O{h}"))
                    for dt in range(4):
                        n = 4 * h + dt
                        for k in range(KT):
                            ins = pe.matmul(PS[:, n, 0:T], ob[:, k, dt * P:(dt + 1) * P], MG[:, k, :], start=(k == 0), stop=(k == KT - 1))
                        ins.then_inc(S("o_mm"), 1)
                    release(spare())
                end_stage(pe, "pe")
                norm(l, 1)
                end_stage(pe, "pe")
                if l == 0:
                    for f in range(FG):
                        for j, nm in enumerate(("DG", "DU")):
                            buf = k8(chunk(l, f"{nm}{f}"))
                            for i in range(4):
                                if f:
                                    pe.wait_ge(S("f_h"), 4 * (f - 1) + i + 1)
                                for k in range(KT):
                                    ins = pe.matmul(PS[:, 4 * j + i, 0:T], buf[:, k, i * P:(i + 1) * P], xn[:, k, 1:T + 1],
                                                    start=(k == 0), stop=(k == KT - 1))
                                ins.then_inc(S("f_mm"), 1)
                            release(spare())
                    pe.wait_ge(S("f_h"), 4 * FG)
                    for f in range(FG):
                        buf = k4(chunk(l, f"DD{f}"))
                        for i in range(4):
                            for d in range(KT):
                                ins = pe.matmul(PS[:, d, 0:T], buf[:, i, d * P:(d + 1) * P], HF[:, 4 * f + i, :],
                                                start=(f == 0 and i == 0), stop=(f == FG - 1 and i == 3))
                        release(ins if f < FG - 1 else spare())
                    pe.drain().then_inc(S("f_down"), 1)
                    end_stage(pe, "pe")

            for t in range(2):
                for k in range(KT):
                    ins = pe.matmul(PS[:, 0, 8 * t:8 * t + 8], xn[:, k, 1 + META + t * P:1 + META + (t + 1) * P],
                                    router_sb[:, k, :], start=(k == 0), stop=(k == KT - 1))
            ins.then_inc(S("q_log"), 1)
            for t in range(2):
                for q in range(2):
                    for k in range(4):
                        ins = pe.transpose(PS[:, 1 + 2 * t + q, k * P:(k + 1) * P],
                                           xn[:, 4 * q + k, 1 + META + t * P:1 + META + (t + 1) * P], C("ident"))
            ins.then_inc(S("q_turn"), 1)
            pe.wait_ge(S("q_sel"), 1)
            sel = lambda t: MR[:, 16 + 8 * t:24 + 8 * t]
            pe.matmul(PS[:, 5, 0:8], C("before"), sel(0), start=True, stop=True)
            pe.matmul(PS[:, 5, 8:16], C("ones"), sel(0), start=True, stop=False, skip_group_check=True)
            pe.matmul(PS[:, 5, 8:16], C("before"), sel(1), start=False, stop=True, skip_group_check=True)
            pe.matmul(PS[:, 5, 16:24], C("ones"), sel(0), start=True, stop=False, skip_group_check=True)
            pe.matmul(PS[:, 5, 16:24], C("ones"), sel(1), start=False, stop=True, skip_group_check=True).then_inc(S("q_rank"), 1)
            end_stage(pe, "pe")

            pe.drain().then_inc(S("w_used"), 3)

            def gather(wait_for):
                pe.wait_ge(S("e_sel"), wait_for)
                for k in range(KT):
                    for t in range(2):
                        ins = pe.matmul(PS[:, 2 + k // 4, (k % 4) * SLOTS:(k % 4 + 1) * SLOTS], hnT[:, t, k * P:(k + 1) * P],
                                        SEL[:, t, :], start=(t == 0), stop=(t == 1))
                ins.then_inc(S("e_xg"), 1)

            def three_products(o, lh, ll, rh, rl, first, last):
                pe.matmul(o, lh, rh, start=first, stop=False, skip_group_check=True)
                pe.matmul(o, ll, rh, start=False, stop=False, skip_group_check=True)
                return pe.matmul(o, lh, rl, start=False, stop=last, skip_group_check=True)

            def turn_hidden(n, f):
                pe.wait_ge(S("e_h"), n * FG + (f + 1))
                for q in range(4):
                    ins = pe.transpose(PS[:, 6, q * P:(q + 1) * P], MH[:, q * P:(q + 1) * P], C("ident"))
                ins.then_inc(S("e_ht"), 1)

            def expert_products(pe, e, n, run):
                pe.wait_ge(S("e_xgl"), n + run + 1)
                for j in range(HALVES):
                    kind, f = MOE_ORDER[j // 2]
                    half, s_ = j % 2, j % 3
                    if (kind, f, half) == ("g", 1, 0):
                        pe.wait_ge(S("e_free"), n + 1)
                    pe.wait_ge(S("w_lo_dve"), n * HALVES + (j + 1 + AHEAD))
                    pe.wait_ge(S("w_lo_pool"), n * HALVES + (j + 1 + AHEAD))
                    if kind in "gu":
                        o = PS[:, 2 * (f % 2) + (kind == "u"), :]
                        for i in range(4):
                            k = 4 * half + i
                            x_, w_ = slice(k * SLOTS, (k + 1) * SLOTS), slice(i * 512, (i + 1) * 512)
                            ins = three_products(o, XGH[:, x_], XGL[:, x_], WH[s_][:, w_], WL[s_][:, w_], k == 0, k == KT - 1)
                    else:
                        if half == 0:
                            pe.wait_ge(S("e_htl"), n * FG + (f + 1))
                        for i in range(2):
                            q = 2 * half + i
                            for hf in range(2):
                                x_, w_ = slice(q * P, (q + 1) * P), slice(i * D + hf * 512, i * D + hf * 512 + 512)
                                ins = three_products(PS[:, 4 + hf, :], HTH[:, x_], HTL[:, x_], WH[s_][:, w_], WL[s_][:, w_],
                                                     f == 0 and q == 0, f == FG - 1 and q == 3)
                    ins.then_inc(S("w_used"), 1)
                    if kind == "g" and f and half == 0:
                        turn_hidden(n, f - 1)
                    if (kind, f, half) == ("u", 3, 1):
                        pe.wait_ge(S("e_selg"), n + 1)
                        for t in range(2):
                            ins = pe.transpose(PS[:, 7, t * P:(t + 1) * P], SEL[:, 2 + t, :], C("ident"))
                        ins.then_inc(S("e_st"), 1)
                    if (kind, f, half) == ("u", FG - 1, 1):
                        turn_hidden(n, f)
                        gather(n + run + 2)
                pe.wait_ge(S("e_stc"), n + 1)
                pe.wait_ge(S("e_y"), n + 1)
                pe.wait_ge(S("e_xgl"), n + run + 2)
                for k in range(KT):
                    bank = (2, 3, 6, 7)[k // 2]
                    ins = pe.matmul(PS[:, bank, (k % 2) * SEQ:(k % 2 + 1) * SEQ], YE[:, k * P:(k + 1) * P], SELT[:, :],
                                    start=True, stop=True)
                ins.then_inc(S("e_sc"), 1)

            def first_gather(pe, run):
                gather(run * (NE + 1) + 1)

            for_all_experts(pe, expert_products, first_gather)
            end_stage(pe, "pe")
            norm(DEPTH, 0)
            pe.wait_ge(S("fin"), 1)
            for t in range(2):
                for q in range(2):
                    for k in range(4):
                        ins = pe.transpose(PS[:, 1 + 2 * t + q, k * P:(k + 1) * P], xn[:, 4 * q + k, 1 + META + t * P:1 + META + (t + 1) * P],
                                           C("ident"))
                    ins.then_inc(S("out_turned"), 1)

        @block.scalar
        def _(act):
            def a(ins):
                link(act, ins, "act_chain")

            n_dma = [0]

            def load(dst, src):
                act.dma_start(dst, src).then_inc(S("setup"), 16)
                n_dma[0] += 1

            load(cst[:, :], consts)
            load(prm[:, :, :], params.rearrange("l p n -> p l n"))
            load(xin[0:META, 0, :], meta)
            for t in range(2):
                load(xin[:, 1 + t, :], x[0, t * P:(t + 1) * P, :])
            load(relb[:, :], rel_bias)

            def low_rank(l, ld):
                ld(wwa[0:64, :], w2[l])
                ld(wwa[64:P, :], a2[l])
                ld(wg0[:, :], g2[l, 0:P, :])
                ld(wg1[:, :], g2[l, P:P + 32, :])

            low_rank(0, load)
            load(vw1_sb[:, :, :], vw1[0].rearrange("(k p) n -> p k n", p=P))
            load(vw2_sb[:, :], vw2[0])
            load(router_sb[:, :, :], router[0].rearrange("(k p) n -> p k n", p=P))
            act.wait_ge(S("setup"), 16 * n_dma[0])
            assert n_dma[0] == N_SETUP, n_dma

            for k in range(KT):
                act.wait_ge(S("in_turned"), k + 1)
                ins = act.activation(hT[:, k, :], PS[:, k, 0:T], ACT.Copy)
                if k == 0:
                    ins.then_inc(S("in_copied"), 1)
            act.wait_ge(S("line_done"), 1)
            link(act, act.activation(lin[:, :], PS[0:NE, 0, 0:LINE], ACT.Copy), "lin_copied")
            act.dma_start(line, bc(lin[:, :], [NE, CH, LINE], 1)).then_inc(S("line_stored"), 16)
            act.wait_ge(S("line_stored"), 16)

            def toeplitz(dst, head0, r0, rows, unit_step, units, n):
                src = bass.AP(tensor=line.tensor, offset=head0 * CH * LINE + r0,
                              ap=[[LINE - 1, rows], [unit_step * CH * LINE, units], [1, n]])
                act.dma_start(dst, src).then_inc(S("bias_ready"), 16)

            for j2 in range(2):
                rows = slice(64 * j2, 64 * j2 + 64)
                toeplitz(bias0[rows, :, :], j2, LINE_TOP - META, 64, 2, 4, 80)
                toeplitz(biasb[rows, :, :], j2, LINE_TOP - 64, 64, 2, 4, P)
                for c in range(1, NXC):
                    toeplitz(biasm[rows, c - 1, :, :], j2, LINE_TOP - META - 64 * c, 64, 2, 4, META)
            for j in range(4):
                toeplitz(biasq[16 * j:16 * j + 16, :, :], j, LINE_TOP, META, 4, 2, META)
            end_stage(act, "act")

            def norm(l, which):
                act.activation(SQ[:, :, :], hT[:, :, :], ACT.Square).then_inc(S("sq_done"), 1)
                act.wait_ge(S("ms_done"), 2 * l + which + 1)
                act.activation(rstd[:, :], rstd[:, :], ACT.Sqrt).then_inc(S("rt_done"), 1)

            def copies(l, n0, dsts, scale=1.0, first=0):
                for i, dst in enumerate(dsts):
                    n = n0 + i
                    act.wait_ge(S("proj_done"), at("proj_done", l, n))
                    src = PS[:, (first + i) % 8, 0:T]
                    ins = None
                    for d_, s_ in dst(src):
                        if ins is not None:
                            a(ins)
                        ins = act.activation(d_, s_, ACT.Copy, scale=scale)
                    ins.then_inc(S("proj_copied"), 1)

            for l in range(DEPTH):
                norm(l, 0)
                end_stage(act, "act")
                copies(l, 0, [lambda s, p=p: [(qA[:, p, :], s)] for p in range(4)], QS)
                copies(l, 4, [lambda s, p=p: [(kA[:, p, 0:T], s)] for p in range(4)], 1.0, 4)
                for t, n in enumerate((P, P, T - 2 * P)):
                    act.wait_ge(S("proj_done"), at("proj_done", l, 8 + t))
                    act.activation(vA[0:n, t, :], PS[0:n, t, :], ACT.Copy).then_inc(S("proj_copied"), 1)
                end_stage(act, "act")
                def soft(h):
                    s, b = h % 2, 2 * (h % 2)
                    act.wait_ge(S("z_done"), at("z_done", l, h))
                    if h >= 2:
                        act.wait_ge(S("sp_done"), at("sp_done", l, h - 2))
                    act.activation(uA[:, s, 0:T], PS[:, b, 0:T], ACT.Abs)
                    a(act.activation(uA[:, s, T:432], PS[:, b + 1, 0:160], ACT.Abs))
                    a(act.activation(uA[:, s, :], uA[:, s, :], ACT.Exp, scale=-1.0))
                    act.activation(uA[:, s, :], uA[:, s, :], ACT.Ln, bias=1.0).then_inc(S("u_done"), 1)

                soft(0)
                for h in range(8):
                    if h < 7:
                        soft(h + 1)
                    s, b = h % 2, 2 * (h % 2)
                    act.wait_ge(S("arg_done"), at("arg_done", l, h))
                    act.activation(atA[:, s, 0:T], PS[:, b, 0:T], ACT.Exp)
                    act.activation(atA[:, s, T:432], PS[:, b + 1, 0:160], ACT.Exp).then_inc(S("at_done"), 1)
                end_stage(act, "act")
                copies(l, 11, [lambda s, j=j: [(qCm[:, j, :], s[:, 0:META]),
                                               (qCx[:, :, j, :], s[:, META:T].rearrange("p (c q) -> p c q", q=CH))]
                               for j in range(4)], QS)
                copies(l, 15, [lambda s: [(kC[:, :], s)], lambda s: [(vC[:, :], s)]], 1.0, 4)
                act.wait_ge(S("c_vt"), at("c_vt", l, 0))
                act.activation(vW[0:80, 0, :], PS[0:80, 6, 0:P], ACT.Copy)
                act.activation(vW[:, 1:4, :], PS[:, 6, P:4 * P].rearrange("p (a b) -> p a b", b=P), ACT.Copy).then_inc(S("c_vtc"), 1)
                for u in range(5):
                    meta_q = u == 4
                    if meta_q and l == DEPTH - 1:
                        break
                    m, v, n = (64, 2, META) if meta_q else (P, 4, 80 if u == 0 else 144)
                    act.wait_ge(S("c_m"), at("c_m", l, u))
                    act.activation(sC[0:m, 0:v, 0:n], sC[0:m, 0:v, 0:n], ACT.Exp)
                    act.activation(mC[0:m, 8:8 + v], mC[0:m, 4:4 + v], ACT.Exp).then_inc(S("c_e"), 1)
                    act.wait_ge(S("c_t"), at("c_t", l, u))
                    if meta_q or u == 0:
                        rows, w = (META, P) if meta_q else (80, 512)
                        act.activation(pTC[0:rows, :, :].rearrange("p a b -> p (a b)")[:, 0:w], PS[0:rows, 2, 0:w], ACT.Copy)\
                            .then_inc(S("c_tc"), 1)
                    else:
                        act.activation(pTC[:, :, :].rearrange("p a b -> p (a b)"), PS[:, 2, :], ACT.Copy)
                        act.activation(pTm[0:META, :, :].rearrange("p a b -> p (a b)"), PS[0:META, 3, :], ACT.Copy)\
                            .then_inc(S("c_tc"), 1)
                    act.wait_ge(S("c_y"), at("c_y", l, u))
                    if meta_q:
                        act.activation(yC[:, :, 0:META], PS[:, 4, 0:64].rearrange("p (a b) -> p a b", b=META), ACT.Copy).then_inc(S("c_yc"), 1)
                    else:
                        t0 = META + CH * u
                        act.activation(yC[:, :, t0:t0 + CH], PS[:, 4, 0:256].rearrange("p (a b) -> p a b", b=CH), ACT.Copy)\
                            .then_inc(S("c_yc"), 1)
                end_stage(act, "act")
                for i, (X_, f0) in enumerate(((R, 0), (K, 4), (V, 8))):
                    copies(l, 17 + 4 * i, [lambda s, p=p, X_=X_: [(X_[:, p, PADC:TP], s)] for p in range(4)], 1.0, f0)
                for i, rows in enumerate((P, P, 32)):
                    act.wait_ge(S("proj_done"), at("proj_done", l, 29 + i))
                    act.activation(PX[0:rows, i, PADC:TP], PS[0:rows, 4 + i, 0:T], ACT.Copy).then_inc(S("proj_copied"), 1)
                end_stage(act, "act")
                act.wait_ge(S("x_mixed"), l + 1)
                act.activation(PX[0:64, 0, PADC:TP], PX[0:64, 0, PADC:TP], ACT.Tanh)
                act.activation(PX[:, 1, PADC:TP], PX[:, 1, PADC:TP], ACT.Sigmoid)
                act.activation(PX[0:32, 2, PADC:TP], PX[0:32, 2, PADC:TP], ACT.Sigmoid).then_inc(S("w_in"), 1)
                act.wait_ge(S("w_mm"), at("w_mm", l, 0))
                for p in range(4):
                    ins = act.activation(LW[:, p, PADC:TP], PS[:, p, 0:T], ACT.Sigmoid, bias=prm_col(l, "w0", p))
                ins.then_inc(S("w_ev"), 1)
                act.wait_ge(S("w_mm"), at("w_mm", l, 1))
                for p in range(4):
                    ins = act.activation(AI[:, p, PADC:TP], PS[:, 4 + p, 0:T], ACT.Sigmoid, bias=prm_col(l, "a0", p))
                ins.then_inc(S("w_ev"), 1)
                act.wait_ge(S("w_mm"), at("w_mm", l, 2))
                act.activation(GT[:, :, PADC:TP], PS[:, 0:4, 0:T], ACT.Copy).then_inc(S("w_ev"), 1)
                if l:
                    act.wait_ge(S("v_mm"), 1)
                    act.activation(PX[0:32, 1, PADC:TP], PS[0:32, 4, 0:T], ACT.Copy).then_inc(S("v_ev"), 1)
                    act.wait_ge(S("v_mm"), 2)
                    for p in range(4):
                        ins = act.activation(DD[:, p, PADC:TP], PS[:, 4 + p, 0:T], ACT.Sigmoid, bias=prm_col(l, "vres_b", p))
                    ins.then_inc(S("v_ev"), 1)
                end_stage(act, "act")
                act.wait_ge(S("k_sum"), at("k_sum", l, 0))
                act.activation(BN[:, :, PADC:TP], PS[:, 0:4, 0:T], ACT.Sqrt).then_inc(S("k_rt"), 1)
                for i in range(3):
                    act.wait_ge(S("g_done"), 3 * l + i + 1)
                    src = (LWG, LWG, LW)[i]
                    act.activation(DD[:, :, :], src[:, :, :], ACT.Exp, scale=-1.0 if i == 1 else 1.0).then_inc(S("e_done"), 1)
                end_stage(act, "act")
                for c in range(NCH):
                    cc = slice(c * CH, (c + 1) * CH)

                    def copy(name, s_, o, src, scale=1.0):
                        act.activation(o[:, 2 * s_:2 * s_ + 2, :], src.rearrange("p (a b) -> p a b", a=2), ACT.Copy, scale=scale)\
                            .then_inc(S(f"r{s_}_{name}"), 1)

                    def keys_rows(s_):
                        act.wait_ge(*W("mm", s_, l, c))
                        copy("vc", s_, Vst, PS[:, 4 * s_ + 2, 0:P])
                        act.activation(BT[:, 2 * s_:2 * s_ + 2, :], PS[:, 4 * s_ + 1, 0:256].rearrange("p (a b) -> p a b", a=2), ACT.Copy)
                        act.activation(HT[:, 2 * s_:2 * s_ + 2, :], PS[:, 4 * s_ + 1, 256:512].rearrange("p (a b) -> p a b", a=2), ACT.Copy)

                    def turned(s_):
                        act.wait_ge(*W("t", s_, l, c))
                        copy("ti", s_, TI, PS[:, 4 * s_ + 3, 0:256])

                    def update(s_, w):
                        act.wait_ge(*W("d", s_, l, c, w))
                        if w < 4:
                            copy("ti", s_, TI, PS[:, 4 * s_ + 1, 0:256])
                        copy("ttc", s_, TT, PS[:, 4 * s_ + 3, 0:256])

                    def right(s_):
                        act.wait_ge(*W("x", s_, l, c))
                        copy("xc", s_, Xst, PS[:, 4 * s_ + 2, 0:P], -1.0)

                    def solved(s_):
                        act.wait_ge(*W("u", s_, l, c))
                        copy("uc", s_, Ust, PS[:, 4 * s_ + 3, 0:P])

                    def result(s_):
                        act.wait_ge(*W("y", s_, l, c))
                        act.activation(Y[:, 2 * s_:2 * s_ + 2, cc], PS[:, 4 * s_ + 1, 0:P].rearrange("p (a b) -> p a b", a=2), ACT.Copy)\
                            .then_inc(S(f"r{s_}_yc"), 1)

                    if c:
                        for s_ in range(2):
                            act.wait_ge(*W("y", s_, l, c - 1))
                    kr = KR[:, :, :].rearrange("p (a b) c -> p a b c", b=2)
                    act.activation(kr[:, :, 0, :], KK[:, :, cc], ACT.Copy)
                    act.activation(kr[:, :, 1, :], R[:, :, cc], ACT.Copy).then_inc(S("r_kr"), 1)
                    steps = [keys_rows, turned] + [lambda s_, w=w: update(s_, w) for w in range(5)] + [right, solved, result]
                    for step in steps:
                        for s_ in range(2):
                            step(s_)
                end_stage(act, "act")
                act.wait_ge(S("n_d"), at("n_d", l, 0))
                act.activation(K[:, :, PADC:TP], Y[:, :, PADC:TP], ACT.Square).then_inc(S("n_sq"), 1)
                act.wait_ge(S("n_e"), at("n_e", l, 0))
                act.activation(K[:, :, PADC:TP], K[:, :, PADC:TP], ACT.Sqrt).then_inc(S("n_s"), 1)
                end_stage(act, "act")
                for n in range(24):
                    act.wait_ge(S("m_g"), at("m_g", l, n))
                    if n >= 2:
                        act.wait_ge(S("m_acc"), at("m_acc", l, n - 2))
                    act.activation(SG[:, n % 2, :], PS[:, n % 4, 0:T], ACT.Sigmoid).then_inc(S("m_s"), 1)
                if l == 0:
                    low_rank(1, lambda d_, s_: act.dma_start(d_, s_).then_inc(S("low_rank1"), 16))
                    act.wait_ge(S("low_rank1"), 64)
                end_stage(act, "act")
                norm(l, 1)
                end_stage(act, "act")
                if l == 0:
                    for f in range(FG):
                        for i in range(4):
                            act.wait_ge(S("f_mm"), 8 * f + i + 1)
                            if f:
                                act.wait_ge(S("f_h"), 4 * (f - 1) + i + 1)
                            act.activation(SF[:, i, :], PS[:, i, 0:T], ACT.Silu).then_inc(S("f_s"), 1)
                    end_stage(act, "act")

            act.wait_ge(S("q_turn"), 1)
            for t in range(2):
                ins = act.activation(hnT[:, t, :].rearrange("p (a b) -> p a b", a=2), PS[:, 1 + 2 * t:3 + 2 * t, :], ACT.Copy)
            a(ins)
            act.wait_ge(S("q_gap"), 1)
            act.activation(MR[:, 176:178], MR[:, 176:178], ACT.Exp).then_inc(S("q_exp"), 1)
            end_stage(act, "act")

            def gathered_high(act, wait_for):
                act.wait_ge(S("e_xg"), wait_for)
                act.activation(XGH[:, :].rearrange("p (a b) -> p a b", a=2), PS[:, 2:4, :], ACT.Copy).then_inc(S("e_xgh"), 1)

            def expert_highs(act, e, n, run):
                def gate(f):
                    act.wait_ge(S("w_used"), used(n, "g", f))
                    act.activation(MS[:, :], PS[:, 2 * (f % 2), :], ACT.Silu).then_inc(S("e_s"), 1)

                def hidden_high(f):
                    act.wait_ge(S("e_ht"), n * FG + (f + 1))
                    act.activation(HTH[:, :], PS[:, 6, :], ACT.Copy).then_inc(S("e_hth"), 1)

                def scatter_rows(f):
                    act.wait_ge(S("e_st"), n + 1)
                    act.activation(SELT[:, :], PS[:, 7, 0:SEQ], ACT.Copy).then_inc(S("e_stc"), 1)

                events = {}
                for f in range(FG):
                    at_half(events, "g", f, 1, 2).append((gate, f))
                    at_half(events, "u", f, 1, 3).append((hidden_high, f))
                at_half(events, "u", 3, 1, 4).append((scatter_rows, 3))
                for j in range(HALVES):
                    i, half = j // 2, j % 2
                    b = (MOE0 + i) % RING
                    if half == 0:
                        act.wait_ge(S(f"landed{b}"), n * (32 * PER_BUF) + (landed_moe0[b] + 32 * (i // RING + 1)))
                    act.wait_ge(S("w_used"), n * HALVES + (j + 1))
                    act.activation(WH[j % 3][:, :], ring[b][:, 2048 * half:2048 * half + 2048], ACT.Copy).then_inc(S("w_hi"), 1)
                    for do, f in events.get(j, []):
                        do(f)
                gathered_high(act, n + run + 2)
                act.wait_ge(S("w_used"), used(n, "d", FG - 1))
                act.activation(YE[:, :].rearrange("p (a b) -> p a b", a=2), PS[:, 4:6, :], ACT.Copy).then_inc(S("e_y"), 1)

            for_all_experts(act, expert_highs, lambda act, run: gathered_high(act, run * (NE + 1) + 1))
            end_stage(act, "act")
            norm(DEPTH, 0)
            for t in range(4):
                act.wait_ge(S("out_turned"), t + 1)
                act.activation(ostage[:, t // 2, 512 * (t % 2):512 * (t % 2) + 512], PS[:, 1 + t, :], ACT.Copy).then_inc(S("out_copied"), 1)

        @block.gpsimd
        def _(pool):
            mask4 = bc(C("bd").rearrange("p (a b) -> p a b", a=2), [P, 4, 2, CH], 1)

            def block_diagonal(o, src):
                return pool.tensor_tensor(o[:, :, :].rearrange("p a (b c) -> p a b c", b=2), bc(src, [P, 4, 2, CH], 2), mask4, ALU.mult)

            for l in range(DEPTH):
                pool.wait_ge(S("r_open"), at("r_open", l, 0))
                for c in range(NCH):
                    cc = slice(c * CH, (c + 1) * CH)
                    if c:
                        for s_ in range(2):
                            pool.wait_ge(*W("mm", s_, l, c - 1))
                    block_diagonal(Bbd, AI[:, :, cc])
                    block_diagonal(Hbd, K[:, :, cc])
                    block_diagonal(VTbd, V[:, :, cc]).then_inc(S("r_bd"), 1)
                    if c:
                        for s_ in range(2):
                            pool.wait_ge(*W("x", s_, l, c - 1))
                    block_diagonal(Kbd, KK[:, :, cc]).then_inc(S("r_kbd"), 1)
            pool.wait_ge(S("w_lo_dve"), AHEAD)
            pool.drain().then_inc(S("w_lo_pool"), AHEAD)

            def expert_lows(pool, e, n, run):
                for j in range(HALVES):
                    i, half = j // 2, j % 2
                    c0 = 2048 - POOL_COLS
                    pool.wait_ge(S("w_hi"), n * HALVES + (j + 1))
                    pool.tensor_tensor(WL[j % 3][:, c0:2048], ring[(MOE0 + i) % RING][:, 2048 * half + c0:2048 * half + 2048],
                                       WH[j % 3][:, c0:2048].bitcast(F32), ALU.subtract).then_inc(S("w_lo_pool"), 1)

            for_all_experts(pool, expert_lows)

        @block.vector
        def _(dve):
            def v(ins):
                link(dve, ins, "dve_chain")

            tt = lambda o, a_, b_, op: dve.tensor_tensor(o, a_, b_, op)

            dve.memset(xn[:, :, 0:1], 0.0)
            v(dve.memset(egc[:, :, :], 0.0))
            end_stage(dve, "dve")

            def norm(l, which, gain):
                dve.wait_ge(S("sum_done"), 2 * l + which + 1)
                dve.tensor_scalar(rstd[:, :], PS[:, 0, 0:T], 1.0 / D, EPS, ALU.mult, ALU.add).then_inc(S("ms_done"), 1)
                dve.wait_ge(S("rt_done"), 2 * l + which + 1)
                v(dve.reciprocal(rstd[:, :], rstd[:, :]))
                for k in range(KT):
                    ins = dve.scalar_tensor_tensor(xn[:, k, 1:T + 1], hT[:, k, :], prm_col(min(l, DEPTH - 1), gain, k), rstd[:, :],
                                                   ALU.mult, ALU.mult)
                return ins

            for l in range(DEPTH):
                dve.memset(kA[:, :, T:384], 0.0)
                dve.memset(vA[:, 2, :], 0.0)
                v(norm(l, 0, "norm_mix"))
                end_stage(dve, "dve")
                end_stage(dve, "dve")
                for h in range(8):
                    s, b = h % 2, 2 * (h % 2)
                    dve.wait_ge(S("u_done"), 8 * l + h + 1)
                    if h >= 2:
                        dve.wait_ge(S("arg_done"), at("arg_done", l, h - 2))
                    dve.scalar_tensor_tensor(spA[:, s, 0:T], PS[:, b, 0:T], 0.0, uA[:, s, 0:T], ALU.max, ALU.add)
                    v(dve.scalar_tensor_tensor(spA[:, s, T:432], PS[:, b + 1, 0:160], 0.0, uA[:, s, T:432], ALU.max, ALU.add))
                    tt(spA[:, s, :], spA[:, s, :], C("sbmask"), ALU.mult).then_inc(S("sp_done"), 1)
                    if h % 2 == 1:
                        p = h // 2
                        dve.wait_ge(S("ya_done"), at("ya_done", l, p))
                        dve.tensor_copy(yA[:, p, :], PS[:, 4 + p % 2, 0:T]).then_inc(S("ya_copied"), 1)
                end_stage(dve, "dve")
                if l == 0:
                    dve.wait_ge(S("bias_ready"), 16 * 14)
                for u in range(5):
                    meta_q = u == 4
                    if meta_q and l == DEPTH - 1:
                        break
                    m, w, n = (64, 2, META) if meta_q else (P, 4, 80 if u == 0 else 144)
                    dve.wait_ge(S("c_z"), at("c_z", l, u))
                    for g in range(2):
                        if meta_q:
                            tt(sC[0:64, g, 0:META], PS[0:64, g, 0:META], biasq[:, g, :], ALU.add)
                            continue
                        src = PS[:, g, 0:2 * n].rearrange("p (a b) -> p a b", a=2)
                        if u == 0:
                            ins = tt(sC[:, 2 * g:2 * g + 2, 0:80], src, bias0[:, 2 * g:2 * g + 2, :], ALU.add)
                        else:
                            tt(sC[:, 2 * g:2 * g + 2, 0:META], src[:, :, 0:META], biasm[:, u - 1, 2 * g:2 * g + 2, :], ALU.add)
                            ins = tt(sC[:, 2 * g:2 * g + 2, META:144], src[:, :, META:144], biasb[:, 2 * g:2 * g + 2, :], ALU.add)
                    sv = sC[0:m, 0:w, 0:n]
                    o, _ = PARAM_COLS["sink_meta" if meta_q else "sink"]
                    v(dve.memset(small[:, 60:61], 0.0))
                    v(dve.tensor_reduce(mC[0:m, 0:w], sv, AX.X, ALU.max))
                    v(tt(mC[0:m, 0:w], mC[0:m, 0:w], prm[0:m, l, o:o + w], ALU.max))
                    tt(mC[0:m, 4:4 + w], prm[0:m, l, o:o + w], mC[0:m, 0:w], ALU.subtract)
                    tt(sv, sv, bc(mC[0:m, 0:w], [m, w, n], 2), ALU.subtract).then_inc(S("c_m"), 1)
                    dve.wait_ge(S("c_e"), at("c_e", l, u))
                    v(dve.tensor_reduce(mC[0:m, 12:12 + w], sv, AX.X, ALU.add))
                    v(tt(mC[0:m, 12:12 + w], mC[0:m, 12:12 + w], mC[0:m, 8:8 + w], ALU.add))
                    v(dve.reciprocal(mC[0:m, 12:12 + w], mC[0:m, 12:12 + w]))
                    tt(sv, sv, bc(mC[0:m, 12:12 + w], [m, w, n], 2), ALU.mult).then_inc(S("c_p"), 1)
                    dve.wait_ge(S("c_t"), at("c_t", l, u))
                end_stage(dve, "dve")
                for X_ in (R, K, V, LW, AI, KK):
                    dve.memset(X_[:, :, 0:PADC], 0.0)
                v(dve.memset(PX[:, :, 0:PADC], 0.0))
                end_stage(dve, "dve")
                def mix(X_, rows, mus, sem=None):
                    w = X_.shape[1]
                    d_ = DD[0:rows, 0:w, PADC:TP]
                    v(tt(d_, X_[0:rows, :, PADC - 1:TP - 1], X_[0:rows, :, PADC:TP], ALU.subtract))
                    for i in range(w):
                        ins = dve.scalar_tensor_tensor(X_[0:rows, i, PADC:TP], d_[:, i, :], mus(i)[0:rows], X_[0:rows, i, PADC:TP],
                                                       ALU.mult, ALU.add)
                    return ins

                v(mix(PX[:, 0:1, :], P, lambda i: prm_col(l, "mu_wa", 0)))
                v(mix(PX[:, 1:2, :], P, lambda i: prm_col(l, "mu_g0", 0)))
                mix(PX[:, 2:3, :], 32, lambda i: prm_col(l, "mu_g1", 0)).then_inc(S("x_mixed"), 1)
                dve.wait_ge(S("x_mixed"), l + 1)
                v(mix(R, P, lambda i: prm_col(l, "mu_r", i)))
                v(mix(K, P, lambda i: prm_col(l, "mu_k", i)))
                v(mix(V, P, lambda i: prm_col(l, "mu_v", i)))
                if l == 0:
                    v(dve.tensor_copy(VF[:, :, :], V[:, :, :]))
                else:
                    v(tt(SQ_v[:, :, :], xn[:, :, 0:T], xn[:, :, 1:T + 1], ALU.subtract))
                    for k in range(KT):
                        ins = dve.scalar_tensor_tensor(SQ_v[:, k, :], SQ_v[:, k, :], prm_col(l, "vres_mu", k), xn[:, k, 1:T + 1],
                                                       ALU.mult, ALU.add)
                    ins.then_inc(S("xv_done"), 1)
                end_stage(dve, "dve")
                TR = slice(PADC, TP)
                if l:
                    v(tt(SV[:, :, TR], VF[:, :, TR], V[:, :, TR], ALU.subtract))
                    v(tt(SV[:, :, TR], SV[:, :, TR], DD[:, :, TR], ALU.mult))
                    v(tt(V[:, :, TR], V[:, :, TR], SV[:, :, TR], ALU.add))
                    dve.memset(KK[:, :, 0:PADC], 0.0)
                v(dve.tensor_scalar(LW[:, :, TR], LW[:, :, TR], DECAY_SCALE, None, ALU.mult))
                for p in range(4):
                    ins = dve.tensor_scalar(KK[:, p, TR], K[:, p, TR], prm_col(l, "k_k", p), None, ALU.mult)
                v(ins)
                tt(DD[:, :, TR], KK[:, :, TR], KK[:, :, TR], ALU.mult).then_inc(S("k_sq"), 1)
                dve.wait_ge(S("k_sum"), at("k_sum", l, 0))
                for p in range(4):
                    ins = dve.tensor_scalar(DD[:, p, TR], AI[:, p, TR], -1.0, prm_col(l, "k_a", p), ALU.add, ALU.mult)
                v(ins)
                v(dve.scalar_tensor_tensor(K[:, :, TR], DD[:, :, TR], 1.0, K[:, :, TR], ALU.add, ALU.mult))
                v(tt(DD[:, :, TR], R[:, :, TR], K[:, :, TR], ALU.mult))
                for p in range(4):
                    ins = dve.tensor_scalar(DD[:, p, TR], DD[:, p, TR], prm_col(l, "r_k", p), None, ALU.mult)
                ins.then_inc(S("b_pr"), 1)
                dve.wait_ge(S("k_rt"), at("k_rt", l, 0))
                v(dve.tensor_scalar(BN[:, :, TR], BN[:, :, TR], 1e-12, None, ALU.max))
                v(dve.reciprocal(BN[:, :, TR], BN[:, :, TR]))
                v(tt(KK[:, :, TR], KK[:, :, TR], BN[:, :, TR], ALU.mult))
                v(tt(AI[:, :, TR], AI[:, :, TR], KK[:, :, TR], ALU.mult))
                dve.wait_ge(S("b_sum"), at("b_sum", l, 0))
                for p in range(4):
                    ins = dve.tensor_tensor_scan(LWG[:, p, :], C("reset"), LW[:, p, :], 0.0, ALU.mult, ALU.add)
                ins.then_inc(S("g_done"), 1)
                dve.wait_ge(S("e_done"), at("e_done", l, 0))
                dve.tensor_copy(egc[:, :, :], DD[:, :, :].rearrange("p a (c q) -> p a c q", q=CH)[:, :, :, CH - 1])
                v(tt(R[:, :, :], R[:, :, :], DD[:, :, :], ALU.mult))
                tt(LW[:, :, :], LWG[:, :, :], LW[:, :, :], ALU.subtract).then_inc(S("g_done"), 1)
                dve.wait_ge(S("e_done"), at("e_done", l, 1))
                tt(AI[:, :, :], AI[:, :, :], DD[:, :, :], ALU.mult)
                v(tt(K[:, :, :], K[:, :, :], DD[:, :, :], ALU.mult))
                dve.memset(small[:, 61:62], 0.0).then_inc(S("g_done"), 1)
                dve.wait_ge(S("e_done"), at("e_done", l, 2))
                v(tt(KK[:, :, :], KK[:, :, :], DD[:, :, :], ALU.mult))
                v(tt(BN[:, :, TR], V[:, :, TR], PS[:, 4:8, 0:T], ALU.mult))
                dve.memset(state[:, :, :], 0.0)
                v(dve.memset(Sbd[:, :, :], 0.0))
                end_stage(dve, "dve")
                dve.memset(small[:, 57:58], 0.0).then_inc(S("r_open"), 1)

                mask = lambda m_, n: bc(m_.rearrange("p (a b) -> p a b", a=2), [P, n, 2, CH], 1)
                wide = lambda x_: bc(x_, [P, x_.shape[1], 2, CH], 2)
                two = lambda x_, s_: x_[:, 2 * s_:2 * s_ + 2, :].rearrange("p a (b c) -> p a b c", b=2)
                for c in range(NCH):
                    first = lambda s_: PS[:, 4 * s_, :].rearrange("p (j m x q) -> p j m x q", j=2, m=2, x=2)

                    def signal(ins, name, s_):
                        ins.then_inc(S(f"r{s_}_{name}"), 1)

                    def level_mask(s_, w):
                        signal(tt(two(NTb, s_), wide(first(s_)[:, :, 0, 0, :]), mask(C("level", (w + 1) * P, P), 2), ALU.mult), "lv", s_)

                    def start(s_):
                        dve.wait_ge(*W("mm", s_, l, c))
                        v(tt(two(TT, s_), wide(first(s_)[:, :, 0, 0, :]), mask(C("level", 0, P), 2), ALU.mult))
                        t2 = TT[:, 2 * s_:2 * s_ + 2, :]
                        signal(tt(t2, bc(C("ident"), [P, 2, P], 1), t2, ALU.subtract), "tt", s_)
                        level_mask(s_, 0)

                    def operands(s_):
                        tt(two(M2bd, s_), wide(first(s_)[:, :, 1, 0, :]), mask(C("strict"), 2), ALU.mult)
                        tt(AA[:, 4 * s_:4 * s_ + 4, :].rearrange("p (j m) q -> p j m q", m=2), first(s_)[:, :, :, 1, :],
                           bc(bc(C("incl"), [P, 2, CH], 1), [P, 2, 2, CH], 1), ALU.mult)
                        dve.wait_ge(*W("vc", s_, l, c))
                        signal(tt(two(Vbd, s_), wide(Vst[:, 2 * s_:2 * s_ + 2, :]), mask(C("bd"), 2), ALU.mult), "cp", s_)

                    def power(s_, w):
                        dve.wait_ge(*W("p", s_, l, c, w))
                        signal(tt(PW[:, 2 * s_:2 * s_ + 2, :], bc(C("ident"), [P, 2, P], 1),
                                  PS[:, 4 * s_ + 2, 0:256].rearrange("p (a b) -> p a b", a=2), ALU.subtract), "pw", s_)
                        if w < 4:
                            level_mask(s_, w + 1)

                    def solution(s_):
                        dve.wait_ge(*W("uc", s_, l, c))
                        signal(tt(two(Ubd, s_), wide(Ust[:, 2 * s_:2 * s_ + 2, :]), mask(C("bd"), 2), ALU.mult), "ubd", s_)

                    def new_state(s_):
                        dve.wait_ge(*W("s", s_, l, c))
                        st = state[:, 2 * s_:2 * s_ + 2, :]
                        v(tt(st, st, PS[:, 4 * s_, 0:P].rearrange("p (a b) -> p a b", b=CH), ALU.add))
                        v(tt(st, st, bc(egc[:, 2 * s_:2 * s_ + 2, c], [P, 2, CH], 2), ALU.mult))
                        dve.wait_ge(*W("y", s_, l, c))
                        signal(tt(two(Sbd, s_), wide(st), mask(C("bd"), 2), ALU.mult), "st", s_)

                    steps = [start] + [lambda s_: power(s_, 0), operands] + [lambda s_, w=w: power(s_, w) for w in range(1, 5)]
                    steps += [solution, new_state]
                    for step in steps:
                        for s_ in range(2):
                            step(s_)
                end_stage(dve, "dve")
                dve.wait_ge(S("n_m"), at("n_m", l, 0))
                dve.scalar_tensor_tensor(Y[:, :, TR], PS[:, 0:4, 0:T], -1.0 / HD, Y[:, :, TR], ALU.mult, ALU.add).then_inc(S("n_d"), 1)
                dve.wait_ge(S("n_v"), at("n_v", l, 0))
                dve.tensor_scalar(K[:, :, TR], PS[:, 4:8, 0:T], 1.0 / HD, GN_EPS, ALU.mult, ALU.add).then_inc(S("n_e"), 1)
                dve.wait_ge(S("n_s"), at("n_s", l, 0))
                v(dve.reciprocal(K[:, :, TR], K[:, :, TR]))
                v(tt(Y[:, :, TR], Y[:, :, TR], K[:, :, TR], ALU.mult))
                for p in range(4):
                    ins = dve.tensor_scalar(Y[:, p, TR], Y[:, p, TR], prm_col(l, "ln_g", p), prm_col(l, "ln_b", p), ALU.mult, ALU.add)
                v(ins)
                v(tt(Y[:, :, TR], Y[:, :, TR], BN[:, :, TR], ALU.add))
                v(tt(R[:, :, TR], Y[:, :, TR], GT[:, :, TR], ALU.mult))
                end_stage(dve, "dve")
                for n in range(24):
                    d_ = n % 8
                    dve.wait_ge(S("m_p"), at("m_p", l, n))
                    dve.wait_ge(S("m_s"), at("m_s", l, n))
                    if n < 8:
                        tt(MG[:, d_, :], SG[:, n % 2, :], PS[:, 4 + n % 4, 0:T], ALU.mult).then_inc(S("m_acc"), 1)
                    else:
                        v(tt(TMP[:, n % 2, :], SG[:, n % 2, :], PS[:, 4 + n % 4, 0:T], ALU.mult))
                        tt(MG[:, d_, :], MG[:, d_, :], TMP[:, n % 2, :], ALU.add).then_inc(S("m_acc"), 1)
                for n in range(8):
                    dve.wait_ge(S("o_mm"), at("o_mm", l, n))
                    ins = tt(hT[:, n, :], hT[:, n, :], PS[:, n, 0:T], ALU.add)
                v(ins)
                end_stage(dve, "dve")
                if l == DEPTH - 1:
                    dve.drain().then_inc(S("w_lo_dve"), AHEAD)
                v(norm(l, 1, "norm_ffn"))
                end_stage(dve, "dve")
                if l == 0:
                    for f in range(FG):
                        for i in range(4):
                            dve.wait_ge(S("f_mm"), 8 * f + 4 + i + 1)
                            dve.wait_ge(S("f_s"), 4 * f + i + 1)
                            tt(HF[:, 4 * f + i, :], SF[:, i, :], PS[:, 4 + i, 0:T], ALU.mult).then_inc(S("f_h"), 1)
                    dve.wait_ge(S("f_down"), 1)
                    v(tt(hT[:, :, :], hT[:, :, :], PS[:, :, 0:T], ALU.add))
                    end_stage(dve, "dve")

            dve.wait_ge(S("q_log"), 1)
            idx = MR[:, 96:112].bitcast(U32)
            v(dve.tensor_copy(MR[:, 0:16], PS[:, 0, 0:16]))
            for t in range(2):
                v(dve.max(MR[:, 112 + 8 * t:120 + 8 * t], MR[:, 8 * t:8 * t + 8]))
                v(dve.max_index(idx[:, 8 * t:8 * t + 8], MR[:, 112 + 8 * t:120 + 8 * t], MR[:, 8 * t:8 * t + 8]))
            v(dve.tensor_copy(MR[:, 128:144], idx))
            for t in range(2):
                v(tt(MR[:, 176 + t:177 + t], MR[:, 113 + 8 * t:114 + 8 * t], MR[:, 112 + 8 * t:113 + 8 * t], ALU.subtract))
            dve.memset(small[:, 63:64], 0.0).then_inc(S("q_gap"), 1)
            dve.wait_ge(S("q_exp"), 1)
            v(dve.tensor_scalar(MR[:, 178:180], MR[:, 176:178], 1.0, None, ALU.add))
            v(dve.reciprocal(MR[:, 178:180], MR[:, 178:180]))
            v(tt(MR[:, 180:182], MR[:, 176:178], MR[:, 178:180], ALU.mult))
            for t in range(2):
                sel, gate = MR[:, 16 + 8 * t:24 + 8 * t], MR[:, 32 + 8 * t:40 + 8 * t]
                one, two = MR[:, 48:56], MR[:, 56:64]
                v(dve.tensor_scalar(one, C("iota8"), MR[:, 128 + 8 * t:129 + 8 * t], None, ALU.is_equal))
                v(dve.tensor_scalar(two, C("iota8"), MR[:, 129 + 8 * t:130 + 8 * t], None, ALU.is_equal))
                v(tt(sel, one, two, ALU.add))
                v(dve.tensor_scalar(one, one, MR[:, 178 + t:179 + t], None, ALU.mult))
                v(dve.scalar_tensor_tensor(gate, two, MR[:, 180 + t:181 + t], one, ALU.mult, ALU.add))
            dve.memset(small[:, 63:64], 0.0).then_inc(S("q_sel"), 1)
            dve.wait_ge(S("q_rank"), 1)
            v(dve.memset(MR[:, 64:82], -1.0))
            for t in range(2):
                slot = MR[:, 64 + 9 * t:72 + 9 * t]
                v(dve.scalar_tensor_tensor(slot, PS[:, 5, 8 * t:8 * t + 8], 1.0, MR[:, 16 + 8 * t:24 + 8 * t], ALU.add, ALU.mult))
                v(dve.tensor_scalar(slot, slot, -1.0, None, ALU.add))
            v(dve.tensor_reduce(small[:, 41:42], PS[:, 5, 16:24], AX.X, ALU.max))
            dve.tensor_scalar(small[:, 40:41].bitcast(I32), small[:, 41:42], float(SLOTS), None, ALU.is_gt).then_inc(S("route_flag"), 1)
            dve.wait_ge(S("route_flag"), 1)
            end_stage(dve, "dve")

            slots = MR[:, 64:64 + 2 * (NE + 1)].rearrange("p (t e) -> p t e", t=2)
            gates = MR[:, 32:48].rearrange("p (t e) -> p t e", t=2)

            def v_e(wait_for, ins):
                ins.then_inc(S("e_chain"), 1)
                dve.wait_ge(S("e_chain"), wait_for)

            def expert_hidden(dve, e, n, run):
                steps = 4

                def link_e(i, ins):
                    v_e(n * steps + (i + 1), ins)

                dve.memset(small[:, 59:60], 0.0).then_inc(S("e_free"), 1)
                link_e(0, dve.tensor_copy(MR[:, 164:166], gates[:, :, bass.ds(e, 1)]))
                link_e(1, dve.tensor_copy(MR[:, 160:162], slots[:, :, bass.ds(e, 1)]))
                for t in range(2):
                    ins = dve.tensor_scalar(SEL[:, 2 + t, :], C("iota", 0, SLOTS), MR[:, 160 + t:161 + t], MR[:, 164 + t:165 + t],
                                            ALU.is_equal, ALU.mult)
                ins.then_inc(S("e_selg"), 1)
                link_e(2, dve.tensor_copy(MR[:, 162:164], slots[:, :, bass.ds(e + 1, 1)]))
                dve.wait_ge(S("e_xg"), n + run + 1)
                select_next(S("e_sel"))

                def hidden(f):
                    dve.wait_ge(S("w_used"), used(n, "u", f))
                    dve.wait_ge(S("e_s"), n * FG + (f + 1))
                    tt(MH[:, :], MS[:, :], PS[:, 2 * (f % 2) + 1, :], ALU.mult).then_inc(S("e_h"), 1)

                def hidden_low(f):
                    dve.wait_ge(S("e_hth"), n * FG + (f + 1))
                    tt(HTL[:, :], PS[:, 6, :], HTH[:, :].bitcast(F32), ALU.subtract).then_inc(S("e_htl"), 1)

                events = {}
                for f in range(FG):
                    at_half(events, "u", f, 1, 2).append((hidden, f))
                    at_half(events, "u", f, 1, 3).append((hidden_low, f))
                lows = 2048 - POOL_COLS
                for j in range(HALVES):
                    i, half = j // 2, j % 2
                    dve.wait_ge(S("w_hi"), n * HALVES + (j + 1))
                    tt(WL[j % 3][:, 0:lows], ring[(MOE0 + i) % RING][:, 2048 * half:2048 * half + lows],
                       WH[j % 3][:, 0:lows].bitcast(F32), ALU.subtract).then_inc(S("w_lo_dve"), 1)
                    for do, f in events.get(j, []):
                        do(f)
                gathered_low(n + run + 2)
                dve.wait_ge(S("e_sc"), n + 1)
                halves = lambda x_: x_.rearrange("p (a b) n -> p a b n", b=2)
                for i, b in enumerate((2, 6)):
                    o = halves(hT[:, 4 * i:4 * i + 4, META:T])
                    ins = tt(o, o, PS[:, b:b + 2, :].rearrange("p a (b n) -> p a b n", b=2), ALU.add)
                link_e(3, ins)

            def gathered_low(wait_for):
                dve.wait_ge(S("e_xgh"), wait_for)
                tt(XGL[:, :].rearrange("p (a b) -> p a b", a=2), PS[:, 2:4, :], XGH[:, :].bitcast(F32).rearrange("p (a b) -> p a b", a=2),
                   ALU.subtract).then_inc(S("e_xgl"), 1)

            def select_next(sem):
                for t in range(2):
                    ins = dve.tensor_scalar(SEL[:, t, :], C("iota", 0, SLOTS), MR[:, 162 + t:163 + t], None, ALU.is_equal)
                ins.then_inc(sem, 1)

            def first_select(dve, run):
                if not isinstance(run, int):
                    ins = dve.tensor_scalar(slots, slots, -float(SLOTS), None, ALU.add)
                    ins.then_inc(S("p_chain"), 1)
                    dve.wait_ge(S("p_chain"), run * 2)
                dve.tensor_copy(MR[:, 162:164], slots[:, :, 0]).then_inc(S("p_chain"), 1)
                dve.wait_ge(S("p_chain"), run * 2 + 1)
                select_next(S("e_sel"))
                gathered_low(run * (NE + 1) + 1)

            for_all_experts(dve, expert_hidden, first_select)
            end_stage(dve, "dve")
            norm(DEPTH, 0, "norm_final").then_inc(S("fin"), 1)

    return nc


def constant_array():
    c = np.zeros((P, NCONST), np.float32)

    def put(name, v):
        o, w = CONST_COLS[name]
        assert v.shape[1] == w
        c[:v.shape[0], o:o + w] = v

    i = np.arange(P)
    row, col = i[:, None], i[None, :]
    head = (row // HD) == (col // HD)
    put("ident", row == col)
    put("ones", np.ones((P, P)))
    put("headones", head)
    put("negsuffix", -1.0 * (row >= col))
    put("negones", -np.ones((P, P)))
    put("negmask", -1e30 * (row >= col))
    put("before", row < col)
    sb = np.ones((P, 432))
    sb[:, 0:P] = row < col
    sb[:, T:T + P] = row < col
    sb[:, 416:432] = (row < col)[:, 0:16]
    put("sbmask", sb)
    rs, cs = row % CH, col % CH
    level = []
    for v in range(6):
        b = 1 << v
        level.append(head & (rs // (2 * b) == cs // (2 * b)) & (rs // b % 2 == 0) & (cs // b % 2 == 1))
    put("level", np.concatenate(level, 1))
    put("strict", head & (rs < cs))
    put("bd", head)
    put("incl", (row % CH) <= np.arange(CH)[None, :])
    put("stack", (row % CH) == np.arange(CH)[None, :])
    put("reset", np.tile((np.arange(TP) % CH != 0)[None], (P, 1)))
    put("iota", np.tile(np.arange(2 * P)[None], (P, 1)))
    put("iota8", np.tile(np.arange(NE)[None], (P, 1)))
    n = np.maximum(LINE_TOP - np.arange(LINE), 0)
    large = 16 + (np.log(np.maximum(n, 1).astype(np.float32) / np.float32(16)) / np.float32(np.log(8.0)) * np.float32(16)).astype(np.int32)
    bucket = np.where(n < 16, n, np.minimum(large, NBUCKET - 1))
    put("bucket", np.arange(NBUCKET)[:, None] == bucket[None])
    return c


def parameter_array(a):
    out = np.zeros((DEPTH, P, NPARAM), np.float32)
    for l in range(DEPTH):
        def put(name, v):
            o, w = PARAM_COLS[name]
            out[l, :v.shape[0], o:o + w] = v

        tiles = lambda v: np.asarray(v).reshape(-1, P).T
        mu = np.asarray(a["tshift_mu"][l])
        b = COL_R
        put("norm_mix", tiles(a["norm_mix"][l]))
        put("norm_ffn", tiles(a["norm_ffn"][l]))
        put("mu_r", tiles(mu[0:512]))
        put("mu_k", tiles(mu[COL_K - b:COL_K - b + 512]))
        put("mu_v", tiles(mu[COL_V - b:COL_V - b + 512]))
        put("mu_wa", np.concatenate([mu[COL_W - b:COL_W - b + 64], mu[COL_A - b:COL_A - b + 64]])[:, None])
        put("mu_g0", mu[COL_G - b:COL_G - b + P][:, None])
        put("mu_g1", mu[COL_G - b + P:COL_G - b + P + 32][:, None])
        for n, k in (("w0", "rwkv_w0"), ("a0", "rwkv_a0"), ("k_k", "rwkv_k_k"), ("k_a", "rwkv_k_a"), ("r_k", "rwkv_r_k"),
                     ("ln_g", "rwkv_ln_g"), ("ln_b", "rwkv_ln_b")):
            put(n, tiles(np.asarray(a[k][l]).reshape(-1)))
        if l:
            put("vres_mu", tiles(a["vres_mu"][l - 1]))
            put("vres_b", tiles(a["vres_b"][l - 1]))
        sinks = np.asarray(a["sinks"][l])
        put("sink", np.repeat(sinks.reshape(4, 2).T, 64, axis=0))
        put("sink_meta", np.repeat(sinks.reshape(2, 4).T, META, axis=0))
        put("norm_final", tiles(a["norm_final"]))
    return out


_PLAIN = ["x", "meta_tokens", "w_in", "w_proj_a", "w_proj_b", "w_proj_c", "w_out", "dense_w_gate", "dense_w_up", "dense_w_down",
          "moe_router", "moe_w_gate", "moe_w_up", "moe_w_down", "rwkv_w2", "rwkv_a2", "rwkv_g2", "vres_w1", "vres_w2", "rel_bias"]


def kernel(**inputs):
    import concourse.bacc as bacc
    from concourse.bass_utils import run_bass_kernel_spmd

    nc = bacc.Bacc("TRN2", target_bir_lowering=False, num_devices=1)
    arrays, args = {}, []
    given = [(n, np.ascontiguousarray(inputs[n])) for n in _PLAIN]
    given += [("consts", constant_array()), ("params", parameter_array(inputs))]
    for name, a in given:
        arrays[f"in_{name}"] = a
        args.append(nc.dram_tensor(f"in_{name}", a.shape, mybir.dt.from_np(a.dtype), kind="ExternalInput").ap())
    args.append(nc.dram_tensor("out_0", (1, SEQ, D), F32, kind="ExternalOutput").ap())
    build_trunk(nc, *args)
    r = run_bass_kernel_spmd(nc, [arrays], core_ids=[0])
    return r.results[0]["out_0"]
```

```python
from contextlib import ExitStack

import numpy as np

import concourse.bass as bass
from concourse import mybir

F32 = mybir.dt.float32
F32R = mybir.dt.float32r
I32 = mybir.dt.int32
U32 = mybir.dt.uint32
ALU = mybir.AluOpType
ACT = mybir.ActivationFunctionType
AX = mybir.AxisListType

P = 128
D = 1024
KT = D // P
SEQ, META = 256, 16
T = SEQ + META
DEPTH = 2
HD = 64
HALF = D // 2
NP_ = HALF // P
CH = 64
PADC = 48
TP = T + PADC
NCH = TP // CH
NXC = SEQ // CH
FF = 3584
FG = FF // 512
NE = 8
SLOTS = 128
PASSES = -(-SEQ // SLOTS)
N_IN = 7200
COL_R, COL_W, COL_K, COL_V, COL_A, COL_G = 1536, 2048, 2112, 2624, 3136, 3200
COL_CQ, COL_CK, COL_GATE = 3360, 3872, 4128
NBUCKET = 32
LINE = 336
LINE_TOP = T - 1
RING = 3
DENSE_BLOCKS = (range(0, 4), range(4, FG))
EPS = 1e-6
GN_EPS = 64e-5
DECAY_SCALE = -float(np.exp(-0.5))
QS = HD ** -0.5

CONST_COLS = {}
_at = 0
for _n, _w in (("ident", P), ("ones", P), ("headones", P), ("negsuffix", P), ("negones", P), ("negmask", P),
               ("before", P), ("sbmask", 432), ("level", 6 * P), ("strict", P), ("bd", P), ("incl", CH),
               ("stack", CH), ("reset", TP), ("iota", 2 * P), ("iota8", NE), ("bucket", LINE)):
    CONST_COLS[_n] = (_at, _w)
    _at += _w
NCONST = _at

PARAM_COLS = {}
_at = 0
for _n, _w in (("norm_mix", KT), ("norm_ffn", KT), ("mu_r", 4), ("mu_k", 4), ("mu_v", 4), ("mu_wa", 1),
               ("mu_g0", 1), ("mu_g1", 1), ("w0", 4), ("a0", 4), ("k_k", 4), ("k_a", 4), ("r_k", 4),
               ("ln_g", 4), ("ln_b", 4), ("vres_mu", KT), ("vres_b", 4), ("sink", 4), ("sink_meta", 2),
               ("norm_final", KT)):
    PARAM_COLS[_n] = (_at, _w)
    _at += _w
NPARAM = _at

PER_LAYER = dict(
    sq_done=2, proj_done=32, proj_copied=32, z_done=8, sp_done=8, arg_done=8, at_done=8, ya_done=4,
    ya_copied=4, c_z=5, c_m=5, c_e=5, c_p=5, c_t=5, c_tc=5, c_y=5, c_yc=5, c_vt=1, c_vtc=1, w_mm=3, w_ev=3,
    w_in=1, k_sq=1, k_sum=1, k_rt=1, b_pr=1, b_sum=1, e_done=3, r_bd=5, r_kbd=5, r_kr=5, r_open=1, n_m=1,
    n_d=1, n_sq=1, n_v=1, n_e=1, n_s=1, m_s=6, m_read=6,
)


def weight_chunks(w_in, w_a, w_b, w_c, w_out, dg, du, dd):
    out = []
    rows = lambda w: w.rearrange("(k p) n -> p k n", p=P)
    for l in range(DEPTH):
        wl = rows(w_in[l])

        def cols(name, c0, n):
            out.append((l, name, "k", [(slice(0, 4), 0, n, wl[:, 0:4, c0:c0 + n]),
                                       (slice(4, 8), 0, n, wl[:, 4:8, c0:c0 + n])]))

        cols("Aq", 0, 512)
        cols("Ak", 512, 512)
        cols("Av", 1024, 512)
        out.append((l, "Cq", "q", [(g, 0, 0, wl[:, :, COL_CQ + 256 * g:COL_CQ + 256 * (g + 1)]
                                    .rearrange("p k (j d) -> p k j d", j=4)) for g in range(2)]))
        cols("Ckv", COL_CK, 256)
        cols("Br", COL_R, 512)
        cols("Bk", COL_K, 512)
        cols("Bv", COL_V, 512)
        out.append((l, "Bx", "k", [(slice(0, 8), 0, 64, wl[:, :, COL_W:COL_W + 64]),
                                   (slice(0, 8), 64, 224, wl[:, :, COL_A:COL_A + 224])]))
        for h in range(2):
            cols(f"E{h}", COL_GATE + 512 * h, 512)
        for b, wp in enumerate((w_a, w_b, w_c)):
            for h in range(2 if b else 0):
                cols(f"G{b}{h}", COL_GATE + D * b + 512 * h, 512)
            if b < 2:
                wr = rows(wp[l])
                out.append((l, f"P{b}", "w", [(slice(0, 2), 0, 0, wr[:, 0:2, :]), (slice(2, 4), 0, 0, wr[:, 2:4, :])]))
            else:
                wc = wp[l].rearrange("(g j d) n -> g d j n", g=2, j=4)
                out.append((l, "P2", "c", [(g, 0, 0, wc[g]) for g in range(2)]))
        wo = rows(w_out[l])
        for h in range(2):
            out.append((l, f"O{h}", "k", [(slice(0, 4), 0, 512, wo[:, 0:4, 512 * h:512 * h + 512]),
                                          (slice(4, 8), 0, 512, wo[:, 4:8, 512 * h:512 * h + 512])]))
        if l == 0:
            for block in DENSE_BLOCKS:
                for f in block:
                    for nm, w in (("DG", dg), ("DU", du)):
                        wr = rows(w[0])
                        out.append((l, f"{nm}{f}", "k",
                                    [(slice(0, 4), 0, 512, wr[:, 0:4, 512 * f:512 * f + 512]),
                                     (slice(4, 8), 0, 512, wr[:, 4:8, 512 * f:512 * f + 512])]))
                for f in block:
                    wr = rows(dd[0, 512 * f:512 * f + 512, :])
                    out.append((l, f"DD{f}", "w", [(slice(0, 2), 0, 0, wr[:, 0:2, :]), (slice(2, 4), 0, 0, wr[:, 2:4, :])]))
    return out


def build_trunk(nc, x, meta, w_in, w_a, w_b, w_c, w_out, dg, du, dd, router, mg, mu_, md, w2, a2, g2, vw1, vw2,
                rel_bias, consts, params, out):
    chunks = weight_chunks(w_in, w_a, w_b, w_c, w_out, dg, du, dd)
    position = {(l, n): i for i, (l, n, _, _) in enumerate(chunks)}
    MOE0 = len(chunks)
    split_half, first_split = {}, {0: None, 1: None, "dense": None}
    halves = 0
    for l_, name, _, _ in chunks:
        if name[0] in "GPOD":
            stage = "dense" if name[0] == "D" else l_
            if first_split[stage] is None:
                first_split[stage] = halves
            split_half[(l_, name)] = halves
            halves += 2
    BASE = halves
    line = nc.dram_tensor("bias_line", (NE, CH, LINE), F32, kind="Internal").ap()

    with ExitStack() as ctx:
        def sb(name, shape, dt=F32):
            return ctx.enter_context(nc.sbuf_tensor(name, shape, dt))

        sems = {}

        def S(name):
            if name not in sems:
                sems[name] = ctx.enter_context(nc.semaphore(name))
            return sems[name]

        def at(name, l, i):
            assert 0 <= i < PER_LAYER[name], name
            return l * PER_LAYER[name] + i + 1

        ring = [sb(f"ring{i}", [P, 4096]) for i in range(RING)]
        hT = sb("hT", [P, KT, T])
        at_xn = -(-nc.sbuf_base // 32) * 32
        xn = sb("xn", [P, KT, T + 1])
        cst = sb("cst", [P, NCONST])
        prm = sb("prm", [P, DEPTH, NPARAM])
        wwa = sb("wwa", [P, HALF])
        wg0 = sb("wg0", [P, HALF])
        wg1 = sb("wg1", [32, HALF])
        vw1_sb = sb("vw1_sb", [P, KT, 32])
        vw2_sb = sb("vw2_sb", [32, HALF])
        router_sb = sb("router_sb", [P, KT, NE])
        relb = sb("relb", [NBUCKET, NE])
        lin = sb("lin", [NE, LINE])
        bias0 = sb("bias0", [P, 4, 80])
        biasb = sb("biasb", [P, 4, P])
        biasm = sb("biasm", [P, 3, 4, META])
        biasq = sb("biasq", [64, 2, META])
        at_ya = -(-nc.sbuf_base // 32) * 32
        yA = sb("yA", [P, NP_, T])
        at_yc = -(-nc.sbuf_base // 32) * 32
        yC = sb("yC", [P, NP_, T])
        VF = sb("VF", [P, NP_, TP])
        rstd = sb("rstd", [P, T])
        egc = sb("egc", [P, NP_, NCH])
        state = sb("state", [P, NP_, CH])
        small = sb("small", [P, 64])
        def pinned(name, shape, offset):
            return nc.alloc_sbuf_tensor_at(name, shape, F32R, offset=offset)

        at1 = -(-nc.sbuf_base // 32) * 32
        area1 = sb("area1", [P, 2 * 3 * 2048])
        at2 = -(-nc.sbuf_base // 32) * 32
        area2 = sb("area2", [P, 12544])
        WH = [pinned(f"WH{i}", [P, 2048], at1 + 4 * 2048 * 2 * i) for i in range(3)]
        WL = [pinned(f"WL{i}", [P, 2048], at1 + 4 * 2048 * (2 * i + 1)) for i in range(3)]
        XGH, XGL = [pinned(nm, [P, D], at2 + 4 * o) for nm, o in (("XGH", 8448), ("XGL", 9472))]
        HTH, HTL = [[pinned(f"{nm}{i}", [P, 512], at2 + 4 * (o + 512 * i)) for i in range(2)] for nm, o in (("HTH", 10496), ("HTL", 11520))]
        XL = pinned("XL", [P, KT, T + 1], at_xn)
        YL = [pinned("YL0", [P, NP_, T], at_ya), pinned("YL1", [P, NP_, TP], at2), pinned("YL2", [P, NP_, T], at_yc)]
        ML, XH = pinned("ML", [P, KT, T], at2 + 4 * 4 * TP), pinned("XH", [P, KT, T], at2 + 4 * (4 * TP + 2 * KT * T + 4 * T))
        YH = [pinned(f"YH{b}", [P, NP_, T], at2 + 4 * (4 * TP + 3 * KT * T + 4 * T + b * NP_ * T)) for b in range(3)]
        FXH = pinned("FXH", [P, KT, T], at2)
        FHH, FHL = [pinned(nm, [P, 16, T], at2 + 4 * (KT * T + i * 16 * T)) for i, nm in enumerate(("FHH", "FHL"))]
        PS = ctx.enter_context(nc.psum_tensor("PS", [P, 8, 512], F32))

        def C(name, lo=0, n=None):
            o, w = CONST_COLS[name]
            return cst[:, o + lo:o + (w if n is None else lo + n)]

        def prm_col(l, name, i):
            o, w = PARAM_COLS[name]
            return prm[:, l, o + i:o + i + 1]

        def carve(area, specs):
            got, o = [], 0
            for shape in specs:
                n = int(np.prod(shape))
                v = area[:, o:o + n]
                if len(shape) == 2:
                    v = v.rearrange("p (a b) -> p a b", b=shape[1])
                if len(shape) == 3:
                    v = v.rearrange("p (a b c) -> p a b c", b=shape[1], c=shape[2])
                got.append(v)
                o += n
            assert o <= area.shape[1], (o, area.shape)
            return got

        (xin,) = carve(area1, [(3, D)])
        qA, kA, vA, uA, spA, atA, qCm, qCx, kC, vC = carve(
            area1, [(8, T), (4, 384), (3, 512), (2, 432), (2, 432), (2, 432), (4, META), (NXC, 4, CH), (T,), (T,)])
        vW, sC, mC, pTC, pTm = carve(area1, [(4, P), (4, 144), (32,), (4, P), (4, P)])
        (Bbd, Kbd, Hbd, VTbd, Vbd, Ubd, Sbd, BT, HT, TT, TI, PW, NTb, M2bd) = carve(area1, [(4, P)] * 14)[:14]
        AA, Vst, Xst, Ust, KR = carve(area1[:, 14 * 512:], [(8, CH), (4, CH), (4, CH), (4, CH), (8, CH)])
        EG = area1[:, area1.shape[1] - KT * T:].rearrange("p (a b) -> p a b", b=T)
        assert area1.shape[1] - KT * T >= 14 * 512 + 28 * CH
        R, K, V, LW, G, AI, KK, DD, GT = carve(area2, [(4, TP)] * 9)
        (PX,) = carve(area2[:, 9 * 4 * TP:], [(3, TP)])
        Y, BN = LW, G
        (_, MG, SG, TMP) = carve(area2, [(4, TP), (KT, T), (KT, T), (4, T)])
        (_, _, HF, SF) = carve(area2, [(KT, T), (16, T), (16, T), (4, T)])
        (SQ,) = carve(area2, [(KT, T)])
        LWG, SV = G, KK
        SQ_v = area2[:, 6 * 4 * TP:6 * 4 * TP + KT * T].rearrange("p (a b) -> p a b", b=T)
        (_, hnT, MS, MH, SEL, SELT, YE, MR) = carve(
            area2, [(KT, T), (2, D), (512,), (512,), (4, SLOTS), (SEQ,), (D,), (192,)])
        ostage = area2[:, 0:2 * D].rearrange("p (a n) -> p a n", a=2)

        STREAM = dict(mm=1, tt=1, t=1, ti=5, ttc=5, lv=5, cp=1, p=5, pw=5, d=5, x=1, xc=1, u=1, uc=1, ubd=1,
                      y=1, yc=1, s=1, st=1, tr=1, vc=1)

        def W(name, s_, l, c, i=0):
            return S(f"r{s_}_{name}"), (l * NCH + c) * STREAM[name] + i + 1

        N_TILES = 15
        N_UNITS = (5, 4)

        def unit_tiles(l, u):
            lo, hi = N_TILES * u // N_UNITS[l], N_TILES * (u + 1) // N_UNITS[l]
            return range(lo, lo + 2), range(lo + 2, hi)

        n_linked = {}

        def link(eng, ins, name):
            n_linked[name] = n_linked.get(name, 0) + 1
            ins.then_inc(S(name), 1)
            eng.wait_ge(S(name), n_linked[name])

        ENGINES = ("pe", "act", "dve")
        stage_no = dict.fromkeys(ENGINES, 0)

        def end_stage(eng, who):
            stage_no[who] += 1
            eng.drain().then_inc(S(f"{who}_stage"), 1)
            for other in ENGINES:
                if other != who:
                    eng.wait_ge(S(f"{other}_stage"), stage_no[who])

        def bc(v, shape, axis):
            return v.unsqueeze(axis).broadcast_to(shape)

        N_SETUP = 10

        block = ctx.enter_context(nc.Block())

        landed_at = []
        total = [0] * RING
        for i, (_, _, kind, _) in enumerate(chunks):
            total[i % RING] += 256 if kind == "q" else 32
            landed_at.append(total[i % RING])
        landed_moe0 = list(total)

        MOE_ORDER = []
        for f in range(FG):
            MOE_ORDER += [("g", f), ("u", f)]
            if f:
                MOE_ORDER.append(("d", f - 1))
        MOE_ORDER.append(("d", FG - 1))
        assert len(MOE_ORDER) % RING == 0
        PER_BUF = len(MOE_ORDER) // RING
        HALVES = 2 * len(MOE_ORDER)
        POOL_COLS = 640
        assert HALVES % 3 == 0
        first_half = {key: 2 * i for i, key in enumerate(MOE_ORDER)}

        def used(n, kind, f, half=1):
            return n * HALVES + (first_half[(kind, f)] + half + 1 + BASE)

        half_chunk = [name for name in split_half for _ in range(2)]

        def after_half(events, l, name, half):
            return events.setdefault(split_half[(l, name)] + half + 2, [])

        def split_stage(work, first, count, events, done=0):
            for g in range(first, first + count + 2):
                if first + done <= g < first + count:
                    work(g)
                for do, *args in events.get(g, []):
                    do(*args)

        def at_half(events, kind, f, half, later):
            events.setdefault(min(first_half[(kind, f)] + half + later, HALVES - 1), [])
            return events[min(first_half[(kind, f)] + half + later, HALVES - 1)]

        def expert_loads(sp, e, n, run, last):
            for i, (kind, f) in enumerate(MOE_ORDER):
                b = (MOE0 + i) % RING
                w = {"g": mg, "u": mu_, "d": md}[kind]
                if kind == "d":
                    src = w[0, e, 512 * f:512 * f + 512, :].rearrange("(k p) n -> p k n", p=P)
                    dst = ring[b][:, :].rearrange("p (k n) -> p k n", k=4)
                    halves = [(dst[:, 0:2], src[:, 0:2]), (dst[:, 2:4], src[:, 2:4])]
                else:
                    src = w[0, e, :, 512 * f:512 * f + 512].rearrange("(k p) n -> p k n", p=P)
                    dst = ring[b][:, :].rearrange("p (k n) -> p k n", k=8)
                    halves = [(dst[:, 0:4], src[:, 0:4]), (dst[:, 4:8], src[:, 4:8])]
                for lo in ("w_lo_dve", "w_lo_pool"):
                    sp.wait_ge(S(lo), n * HALVES + (2 * i - 2 * RING + 2 + BASE))
                for d_, s_ in halves:
                    sp.dma_start(d_, s_).then_inc(S(f"landed{b}"), 16)

        def for_all_experts(eng, body, before=None):
            if before:
                before(eng, 0)
            with eng.Fori(0, NE - 1) as e:
                body(eng, e, e, 0, False)
            body(eng, NE - 1, NE - 1, 0, True)
            with overflow_branch(eng):
                with eng.Fori(0, PASSES - 1) as again:
                    if before:
                        before(eng, again + 1)
                    with eng.Fori(0, NE - 1) as e:
                        body(eng, e, again * NE + e + NE, again + 1, False)
                    body(eng, NE - 1, again * NE + (2 * NE - 1), again + 1, True)

        def overflow_branch(eng):
            eng.wait_ge(S("route_flag"), 1)
            flag = eng.value_load(small[0:1, 40:41].bitcast(I32), min_val=0, max_val=1)
            return eng.If(flag > 0)

        @block.sync
        def _(sp):
            def bias_tables():
                sp.wait_ge(S("lin_copied"), 1)
                sp.dma_start(line, bc(lin[:, :], [NE, CH, LINE], 1)).then_inc(S("line_stored"), 16)
                sp.wait_ge(S("line_stored"), 16)

                def toeplitz(dst, head0, r0, rows, unit_step, units, n):
                    src = bass.AP(tensor=line.tensor, offset=head0 * CH * LINE + r0,
                                  ap=[[LINE - 1, rows], [unit_step * CH * LINE, units], [1, n]])
                    sp.dma_start(dst, src).then_inc(S("bias_ready"), 16)

                for j2 in range(2):
                    rows = slice(64 * j2, 64 * j2 + 64)
                    toeplitz(bias0[rows, :, :], j2, LINE_TOP - META, 64, 2, 4, 80)
                    toeplitz(biasb[rows, :, :], j2, LINE_TOP - 64, 64, 2, 4, P)
                    for c in range(1, NXC):
                        toeplitz(biasm[rows, c - 1, :, :], j2, LINE_TOP - META - 64 * c, 64, 2, 4, META)
                for j in range(4):
                    toeplitz(biasq[16 * j:16 * j + 16, :, :], j, LINE_TOP, META, 4, 2, META)

            sp.wait_ge(S("setup_x"), 64)
            for i, (l, name, kind, parts) in enumerate(chunks):
                buf = ring[i % RING]
                if i == RING:
                    bias_tables()
                if i >= RING:
                    last = chunks[i - RING][:2]
                    if last in split_half:
                        for lo in ("w_lo_dve", "w_lo_pool"):
                            sp.wait_ge(S(lo), split_half[last] + 2)
                    else:
                        sp.wait_ge(S("chunk_used"), sum(c[:2] not in split_half for c in chunks[:i - RING + 1]))
                for a, c0, n, src in parts:
                    if kind == "k":
                        dst = buf[:, :].rearrange("p (k n) -> p k n", k=8)[:, a, c0:c0 + n]
                    elif kind == "w":
                        dst = buf[:, :].rearrange("p (k n) -> p k n", k=4)[:, a, :]
                    elif kind == "c":
                        dst = buf[64 * a:64 * a + 64, :].rearrange("p (k n) -> p k n", k=4)
                    else:
                        dst = buf[:, :].rearrange("p (k j g d) -> p k j g d", k=8, j=4, g=2)[:, :, :, a, :]
                    if kind == "q":
                        for k in range(KT):
                            sp.dma_start(dst[:, k], src[:, k]).then_inc(S(f"landed{i % RING}"), 16)
                    else:
                        sp.dma_start(dst, src).then_inc(S(f"landed{i % RING}"), 16)
            for_all_experts(sp, expert_loads)
            for h in range(2):
                sp.wait_ge(S("out_copied"), 2 * h + 2)
                sp.dma_start(out[0, h * P:(h + 1) * P, :], ostage[:, h, :]).then_inc(S("out_stored"), 16)
            sp.wait_ge(S("out_stored"), 32)

        @block.tensor
        def _(pe):
            def chunk(l, name):
                i = position[(l, name)]
                pe.wait_ge(S(f"landed{i % RING}"), landed_at[i])
                return ring[i % RING]

            def release(ins):
                ins.then_inc(S("chunk_used"), 1)

            def k8(buf, n=512):
                return buf[:, :].rearrange("p (k n) -> p k n", k=8)[:, :, 0:n]

            def three_products(o, lh, ll, rh, rl, first, last):
                pe.matmul(o, lh, rh, start=first, stop=False, skip_group_check=True)
                pe.matmul(o, ll, rh, start=False, stop=False, skip_group_check=True)
                return pe.matmul(o, lh, rl, start=False, stop=last, skip_group_check=True)

            def half_ready(g):
                pe.wait_ge(S("w_lo_dve"), g + 1)
                pe.wait_ge(S("w_lo_pool"), g + 1)
                return WH[g % 3], WL[g % 3]

            def columns_half(l, name, half, bank0, xh, xl, before=None):
                g = split_half[(l, name)] + half
                wh, wl = half_ready(g)
                if before:
                    before()
                for dt in range(4):
                    for i in range(4):
                        k, c = 4 * half + i, slice(i * 512 + dt * P, i * 512 + dt * P + P)
                        ins = three_products(PS[:, bank0 + dt, 0:T], wh[:, c], wl[:, c], xh(k), xl(k), k == 0, k == KT - 1)
                ins.then_inc(S("w_used"), 1)

            def rows_half(l, name, half, xh, xl, first, last, before=None, mid=None):
                g = split_half[(l, name)] + half
                wh, wl = half_ready(g)
                for d_ in range(KT):
                    if before:
                        before(d_)
                    for i in range(2):
                        k, c = 2 * half + i, slice(i * D + d_ * P, i * D + d_ * P + P)
                        ins = three_products(PS[:, d_, 0:T], wh[:, c], wl[:, c], xh(k), xl(k), first and i == 0, last and i == 1)
                    if mid and d_ == 3:
                        ins.then_inc(S(mid), 1)
                ins.then_inc(S("w_used"), 1)

            def spare():
                return pe.drain()

            def norm(l, which):
                pe.wait_ge(S("sq_done"), at("sq_done", l, which) if l < DEPTH else 2 * DEPTH + 1)
                for k in range(KT):
                    ins = pe.matmul(PS[:, 0, 0:T], C("ones"), SQ[:, k, :], start=(k == 0), stop=(k == KT - 1))
                ins.then_inc(S("sum_done"), 1)

            def column_tiles(l, name, widths, n0, first):
                buf = k8(chunk(l, name))
                c = 0
                for i, m in enumerate(widths):
                    n = n0 + i
                    if n >= 8 and first + i >= 8:
                        pe.wait_ge(S("proj_copied"), at("proj_copied", l, n - 8))
                    bank = (first + i) % 8
                    for k in range(KT):
                        ins = pe.matmul(PS[0:m, bank, 0:T], buf[:, k, c:c + m], xn[:, k, 1:T + 1],
                                        start=(k == 0), stop=(k == KT - 1))
                    c += m
                    ins.then_inc(S("proj_done"), 1)
                release(spare())

            pe.wait_ge(S("setup_x"), 64)
            for k in range(KT):
                pe.transpose(PS[:, k, 0:META], xin[0:META, 0, k * P:(k + 1) * P], C("ident")[0:META, 0:META])
                for t in range(2):
                    ins = pe.transpose(PS[:, k, META + t * P:META + (t + 1) * P], xin[:, 1 + t, k * P:(k + 1) * P], C("ident"))
                ins.then_inc(S("in_turned"), 1)
            pe.wait_ge(S("setup"), 16 * N_SETUP)
            pe.wait_ge(S("in_copied"), 1)
            pe.matmul(PS[0:NE, 0, 0:LINE], relb[:, :], C("bucket")[0:NBUCKET, :], start=True, stop=True).then_inc(S("line_done"), 1)
            end_stage(pe, "pe")

            for l in range(DEPTH):
                norm(l, 0)
                end_stage(pe, "pe")
                column_tiles(l, "Aq", [P] * 4, 0, 0)
                column_tiles(l, "Ak", [P] * 4, 4, 4)
                buf = k8(chunk(l, "Av"))
                for t, (t0, n) in enumerate(((0, P), (P, P), (2 * P, T - 2 * P))):
                    pe.wait_ge(S("proj_copied"), at("proj_copied", l, t))
                    for k in range(KT):
                        ins = pe.matmul(PS[0:n, t, :], xn[:, k, 1 + t0:1 + t0 + n], buf[:, k, :], start=(k == 0), stop=(k == KT - 1))
                    ins.then_inc(S("proj_done"), 1)
                release(spare())
                end_stage(pe, "pe")

                def zscores(h):
                    if h >= 2:
                        pe.wait_ge(S("at_done"), at("at_done", l, h - 2))
                    p, r, b = h // 2, 64 * (h % 2), 2 * (h % 2)
                    kh, qh = kA[:, p], qA[:, h]
                    pe.matmul(PS[:, b, 0:T], kh[:, 0:P], qh[:, 0:T], start=True, stop=False, skip_group_check=True)
                    pe.matmul(PS[:, b + 1, 0:144], kh[:, P:2 * P], qh[:, P:T], start=True, stop=False, skip_group_check=True)
                    pe.matmul(PS[:, b + 1, 144:160], kh[:, 2 * P:3 * P], qh[:, 2 * P:T], start=False, stop=False,
                              skip_group_check=True).then_inc(S("z_done"), 1)

                def window_tile(i):
                    name, c = ("Cq", i * P) if i < 4 else ("Ckv", (i - 4) * P)
                    if c == 0:
                        window_bufs[0] = k8(chunk(l, name))
                    if i >= 2:
                        pe.wait_ge(S("proj_copied"), at("proj_copied", l, 11 + i - 2))
                    for k in range(KT):
                        ins = pe.matmul(PS[:, 6 + i % 2, 0:T], window_bufs[0][:, k, c:c + P], xn[:, k, 1:T + 1], start=(k == 0), stop=(k == KT - 1))
                    ins.then_inc(S("proj_done"), 1)
                    if i in (3, 5):
                        release(spare())

                window_bufs = [None]
                zscores(0)
                for h in range(8):
                    if h < 7:
                        zscores(h + 1)
                    s, b = h % 2, 2 * (h % 2)
                    pe.wait_ge(S("sp_done"), at("sp_done", l, h))
                    sp_ = spA[:, s, :]
                    mm = lambda o, a, b_: pe.matmul(o, a, b_, start=False, stop=False, skip_group_check=True)
                    mm(PS[:, b, 0:T], C("negsuffix"), sp_[:, 0:T])
                    mm(PS[:, b, P:T], C("negones"), sp_[:, T:T + 144])
                    mm(PS[:, b, 2 * P:T], C("negones"), sp_[:, 416:432])
                    mm(PS[:, b, 0:P], C("ident"), C("negmask"))
                    mm(PS[:, b + 1, 0:160], C("negsuffix"), sp_[:, T:432])
                    mm(PS[:, b + 1, P:144], C("negones"), sp_[:, 416:432])
                    mm(PS[:, b + 1, 0:P], C("ident"), C("negmask"))
                    pe.matmul(PS[:, b + 1, 144:160], C("ident"), C("negmask", 0, 16), start=False, stop=True,
                              skip_group_check=True).then_inc(S("arg_done"), 1)
                    if h < 6:
                        window_tile(h)
                    pe.wait_ge(S("at_done"), at("at_done", l, h))
                    p, r, yb = h // 2, 64 * (h % 2), 4 + (h // 2) % 2
                    if r == 0 and p >= 2:
                        pe.wait_ge(S("ya_copied"), at("ya_copied", l, p - 2))
                    vh = lambda J: vA[:, J, h * 64:h * 64 + 64]
                    a_ = atA[:, s, :]
                    pe.matmul(PS[r:r + 64, yb, 0:T], vh(0), a_[:, 0:T], start=True, stop=False, skip_group_check=True)
                    pe.matmul(PS[r:r + 64, yb, P:T], vh(1), a_[:, T:T + 144], start=False, stop=False, skip_group_check=True)
                    ins = pe.matmul(PS[r:r + 64, yb, 2 * P:T], vh(2), a_[:, 416:432], start=False, stop=True, skip_group_check=True)
                    if r:
                        ins.then_inc(S("ya_done"), 1)
                end_stage(pe, "pe")

                for w, (t0, n) in enumerate(((0, 80), (META, P), (META + 64, P), (META + 128, P))):
                    ins = pe.transpose(PS[0:n, 6, w * P:(w + 1) * P], vC[:, t0:t0 + n], C("ident"))
                ins.then_inc(S("c_vt"), 1)
                pe.wait_ge(S("c_vtc"), at("c_vtc", l, 0))
                chunk_bufs = {}

                def projection_tile(t):
                    name = ("Br", "Bk", "Bv", "Bx")[t // 4]
                    if t % 4 == 0:
                        chunk_bufs[name] = k8(chunk(l, name))
                    if t >= 3:
                        pe.wait_ge(S("proj_copied"), at("proj_copied", l, 17 + t - 3))
                    if t < 12:
                        parts = [(P * (t % 4), P, 0)]
                    else:
                        parts = [[(0, 64, 0), (64, 64, 64)], [(128, P, 0)], [(256, 32, 0)]][t - 12]
                    for c, m, lo in parts:
                        for k in range(KT):
                            ins = pe.matmul(PS[lo:lo + m, 5 + t % 3, 0:T], chunk_bufs[name][:, k, c:c + m], xn[:, k, 1:T + 1],
                                            start=(k == 0), stop=(k == KT - 1))
                    ins.then_inc(S("proj_done"), 1)
                    if t % 4 == 3 or t == N_TILES - 1:
                        release(spare())

                def scores(u):
                    meta_q = u == 4
                    for g in range(2):
                        r = 64 * g
                        for jp in range(1 if meta_q else 2):
                            if meta_q:
                                lhs, o, m = qCm[r:r + 64, :, :].rearrange("p a b -> p (a b)"), 0, 64
                            else:
                                lhs = qCx[r:r + 64, u, 2 * jp:2 * jp + 2, :].rearrange("p a b -> p (a b)")
                                o, m = (80 if u == 0 else 144) * jp, P
                            keys = [(0, META)] if meta_q else [(0, 80)] if u == 0 else [(0, META), (META + 64 * (u - 1), P)]
                            for t0, n in keys:
                                ins = pe.matmul(PS[0:m, g, o:o + n], lhs, kC[r:r + 64, t0:t0 + n], start=True, stop=True)
                                o += n
                    ins.then_inc(S("c_z"), 1)

                scores(0)
                for u in range(N_UNITS[l]):
                    meta_q = u == 4
                    ahead, behind = unit_tiles(l, u)
                    for t in ahead:
                        projection_tile(t)
                    pe.wait_ge(S("c_p"), at("c_p", l, u))
                    units, m = (2, 64) if meta_q else (4, P)
                    for v in range(units):
                        if meta_q or u == 0:
                            n = META if meta_q else 80
                            ins = pe.transpose(PS[0:n, 2, v * m:(v + 1) * m], sC[0:m, v, 0:n], C("ident")[0:m, 0:m])
                        else:
                            pe.transpose(PS[:, 2, v * P:(v + 1) * P], sC[:, v, META:144], C("ident"))
                            ins = pe.transpose(PS[0:META, 3, v * P:(v + 1) * P], sC[:, v, 0:META], C("ident"))
                    ins.then_inc(S("c_t"), 1)
                    if u + 1 < N_UNITS[l]:
                        scores(u + 1)
                    for t in behind:
                        projection_tile(t)
                    pe.wait_ge(S("c_tc"), at("c_tc", l, u))
                    if u:
                        pe.wait_ge(S("c_yc"), at("c_yc", l, u - 1))
                    for g in range(2):
                        vcols = slice(64 * g, 64 * g + 64)
                        if meta_q:
                            ins = pe.matmul(PS[64 * g:64 * g + 64, 4, 0:64], vW[0:META, 0, vcols],
                                            pTC[0:META, :, :].rearrange("p a b -> p (a b)")[:, 64 * g:64 * g + 64], start=True, stop=True)
                        elif u == 0:
                            ins = pe.matmul(PS[64 * g:64 * g + 64, 4, 0:256], vW[0:80, 0, vcols],
                                            pTC[0:80, 2 * g:2 * g + 2, :], start=True, stop=True)
                        else:
                            pe.matmul(PS[64 * g:64 * g + 64, 4, 0:256], vW[:, u, vcols],
                                      pTC[:, 2 * g:2 * g + 2, :], start=True, stop=False, skip_group_check=True)
                            ins = pe.matmul(PS[64 * g:64 * g + 64, 4, 0:256], vW[0:META, 0, vcols],
                                            pTm[0:META, 2 * g:2 * g + 2, :], start=False, stop=True, skip_group_check=True)
                    ins.then_inc(S("c_y"), 1)
                end_stage(pe, "pe")

                pe.wait_ge(S("w_in"), at("w_in", l, 0))
                for p in range(4):
                    ins = pe.matmul(PS[:, p, 0:T], wwa[0:64, p * P:(p + 1) * P], PX[0:64, 0, PADC:TP], start=True, stop=True)
                ins.then_inc(S("w_mm"), 1)
                for p in range(4):
                    ins = pe.matmul(PS[:, 4 + p, 0:T], wwa[64:P, p * P:(p + 1) * P], PX[64:P, 0, PADC:TP], start=True, stop=True)
                ins.then_inc(S("w_mm"), 1)
                pe.wait_ge(S("w_ev"), at("w_ev", l, 0))
                for p in range(4):
                    pe.matmul(PS[:, p, 0:T], wg0[:, p * P:(p + 1) * P], PX[:, 1, PADC:TP], start=True, stop=False)
                    ins = pe.matmul(PS[:, p, 0:T], wg1[:, p * P:(p + 1) * P], PX[0:32, 2, PADC:TP], start=False, stop=True)
                ins.then_inc(S("w_mm"), 1)
                if l:
                    pe.wait_ge(S("w_ev"), at("w_ev", l, 1))
                    pe.wait_ge(S("xv_done"), 1)
                    for k in range(KT):
                        ins = pe.matmul(PS[0:32, 4, 0:T], vw1_sb[:, k, :], SQ_v[:, k, :], start=(k == 0), stop=(k == KT - 1))
                    ins.then_inc(S("v_mm"), 1)
                    pe.wait_ge(S("v_ev"), 1)
                    for p in range(4):
                        ins = pe.matmul(PS[:, 4 + p, 0:T], vw2_sb[:, p * P:(p + 1) * P], PX[0:32, 1, PADC:TP], start=True, stop=True)
                    ins.then_inc(S("v_mm"), 1)
                end_stage(pe, "pe")
                pe.wait_ge(S("k_sq"), at("k_sq", l, 0))
                for p in range(4):
                    ins = pe.matmul(PS[:, p, 0:T], C("headones"), DD[:, p, PADC:TP], start=True, stop=True)
                ins.then_inc(S("k_sum"), 1)

                def early_gate(n):
                    if n % 4 == 0:
                        early_bufs[0] = k8(chunk(l, f"E{n // 4}"))
                    if n == 0:
                        pe.wait_ge(S("k_rt"), at("k_rt", l, 0))
                    if n >= 4:
                        pe.wait_ge(S("eg_copied"), 8 * l + n - 3)
                    for k in range(KT):
                        ins = pe.matmul(PS[:, n % 4, 0:T], early_bufs[0][:, k, (n % 4) * P:(n % 4 + 1) * P], xn[:, k, 1:T + 1],
                                        start=(k == 0), stop=(k == KT - 1))
                    ins.then_inc(S("eg_done"), 1)
                    if n % 4 == 3:
                        release(spare())

                early_bufs = [None]
                early_gate(0)
                pe.wait_ge(S("b_pr"), at("b_pr", l, 0))
                for p in range(4):
                    ins = pe.matmul(PS[:, 4 + p, 0:T], C("headones"), DD[:, p, PADC:TP], start=True, stop=True)
                ins.then_inc(S("b_sum"), 1)
                for n in range(1, 8):
                    early_gate(n)
                end_stage(pe, "pe")

                def signal(ins, name, s_):
                    ins.then_inc(S(f"r{s_}_{name}"), 1)

                for c in range(NCH):
                    pairs = lambda s_: (2 * s_, 2 * s_ + 1)

                    def pair_products(s_):
                        if s_ == 0:
                            pe.wait_ge(S("r_bd"), at("r_bd", l, c))
                            pe.wait_ge(S("r_kr"), at("r_kr", l, c))
                        if c:
                            pe.wait_ge(*W("st", s_, l, c - 1))
                            pe.wait_ge(*W("yc", s_, l, c - 1))
                        b0 = 4 * s_
                        for j, p in enumerate(pairs(s_)):
                            kr = KR[:, 2 * p:2 * p + 2, :]
                            pe.matmul(PS[:, b0, 256 * j:256 * j + P], Bbd[:, p, :], kr, start=True, stop=True)
                            pe.matmul(PS[:, b0, 256 * j + P:256 * j + 256], Hbd[:, p, :], kr, start=True, stop=True)
                            pe.matmul(PS[:, b0 + 2, j * CH:(j + 1) * CH], VTbd[:, p, :], C("stack"), start=True, stop=True)
                            pe.transpose(PS[:, b0 + 1, j * P:(j + 1) * P], Bbd[:, p, :], C("ident"))
                            ins = pe.transpose(PS[:, b0 + 1, 256 + j * P:256 + (j + 1) * P], Hbd[:, p, :], C("ident"))
                        signal(ins, "mm", s_)

                    def turn_inverse(s_):
                        pe.wait_ge(*W("tt", s_, l, c))
                        for j, p in enumerate(pairs(s_)):
                            ins = pe.transpose(PS[:, 4 * s_ + 3, j * P:(j + 1) * P], TT[:, p, :], C("ident"))
                        signal(ins, "t", s_)

                    def level_product(s_, w):
                        pe.wait_ge(*W("lv", s_, l, c, w))
                        pe.wait_ge(*W("ti", s_, l, c, w))
                        if w == 0:
                            pe.wait_ge(*W("vc", s_, l, c))
                        for j, p in enumerate(pairs(s_)):
                            ins = pe.matmul(PS[:, 4 * s_ + 2, j * P:(j + 1) * P], NTb[:, p, :], TI[:, p, :], start=True, stop=True)
                        signal(ins, "p", s_)

                    def level_update(s_, w):
                        pe.wait_ge(*W("pw", s_, l, c, w))
                        if w:
                            pe.wait_ge(*W("ttc", s_, l, c, w - 1))
                        for j, p in enumerate(pairs(s_)):
                            if w < 4:
                                pe.matmul(PS[:, 4 * s_ + 1, j * P:(j + 1) * P], TT[:, p, :], PW[:, p, :], start=True, stop=True)
                            ins = pe.matmul(PS[:, 4 * s_ + 3, j * P:(j + 1) * P], PW[:, p, :], TT[:, p, :], start=True, stop=True)
                        signal(ins, "d", s_)

                    def right_side(s_):
                        pe.wait_ge(*W("cp", s_, l, c))
                        if s_ == 0:
                            pe.wait_ge(S("r_kbd"), at("r_kbd", l, c))
                        for j, p in enumerate(pairs(s_)):
                            o = PS[:, 4 * s_ + 2, j * CH:(j + 1) * CH]
                            pe.matmul(o, Kbd[:, p, :], state[:, p, :], start=True, stop=False, skip_group_check=True)
                            ins = pe.matmul(o, M2bd[:, p, :], Vst[:, p, :], start=False, stop=True, skip_group_check=True)
                        signal(ins, "x", s_)

                    def solve(s_):
                        pe.wait_ge(*W("xc", s_, l, c))
                        pe.wait_ge(*W("ttc", s_, l, c, 4))
                        for j, p in enumerate(pairs(s_)):
                            ins = pe.matmul(PS[:, 4 * s_ + 3, j * CH:(j + 1) * CH], TT[:, p, :], Xst[:, p, :], start=True, stop=True)
                        signal(ins, "u", s_)

                    def outputs(s_):
                        pe.wait_ge(*W("uc", s_, l, c))
                        for j, p in enumerate(pairs(s_)):
                            o = PS[:, 4 * s_, j * CH:(j + 1) * CH]
                            pe.matmul(o, BT[:, p, :], Ust[:, p, :], start=True, stop=False, skip_group_check=True)
                            ins = pe.matmul(o, HT[:, p, :], Vst[:, p, :], start=False, stop=True, skip_group_check=True)
                        signal(ins, "s", s_)
                        for j, p in enumerate(pairs(s_)):
                            o = PS[:, 4 * s_ + 1, j * CH:(j + 1) * CH]
                            pe.matmul(o, Sbd[:, p, :], KR[:, 2 * p + 1, :], start=True, stop=False, skip_group_check=True)
                            pe.matmul(o, Vbd[:, p, :], AA[:, 2 * p + 1, :], start=False, stop=False, skip_group_check=True)
                            if j == 0:
                                pe.wait_ge(*W("ubd", s_, l, c))
                            ins = pe.matmul(o, Ubd[:, p, :], AA[:, 2 * p, :], start=False, stop=True, skip_group_check=True)
                        signal(ins, "y", s_)

                    steps = [pair_products, turn_inverse]
                    for w in range(5):
                        steps += [lambda s_, w=w: level_product(s_, w), lambda s_, w=w: level_update(s_, w)]
                    steps += [right_side, solve, outputs]
                    for step in steps:
                        for s_ in range(2):
                            step(s_)
                end_stage(pe, "pe")
                for p in range(4):
                    ins = pe.matmul(PS[:, p, 0:T], C("headones"), Y[:, p, PADC:TP], start=True, stop=True)
                ins.then_inc(S("n_m"), 1)
                pe.wait_ge(S("n_sq"), at("n_sq", l, 0))
                for p in range(4):
                    ins = pe.matmul(PS[:, 4 + p, 0:T], C("headones"), K[:, p, PADC:TP], start=True, stop=True)
                ins.then_inc(S("n_v"), 1)
                end_stage(pe, "pe")

                for b in range(3):
                    for h in range(2 if b else 0):
                        for half in range(2):
                            def before():
                                if b == 1 and h == 0:
                                    pe.wait_ge(S("x_lo"), 7 * l + half + 2)
                                if half == 0:
                                    pe.wait_ge(S("m_read"), at("m_read", l, 2 * (b - 1) + h))
                            columns_half(l, f"G{b}{h}", half, 4 * h, lambda k: XH[:, k, :], lambda k: XL[:, k, 1:T + 1], before)
                    pe.wait_ge(S("x_lo"), 7 * l + (1, 4, 5)[b])
                    y_lo = [YL[0], YL[1][:, :, PADC:TP], YL[2]][b]
                    for half in range(2):
                        def before(d_):
                            if b and half == 0 and d_ % 4 == 0:
                                pe.wait_ge(S("m_s"), at("m_s", l, 2 * b + d_ // 4))
                        rows_half(l, f"P{b}", half, lambda k: YH[b][:, k, :], lambda k: y_lo[:, k, :], half == 0, half == 1, before,
                                  "m_p" if half else None)
                for h in range(2):
                    for half in range(2):
                        def before():
                            if h == 0:
                                pe.wait_ge(S("x_lo"), 7 * l + 6 + half)
                        columns_half(l, f"O{h}", half, 4 * h, lambda k: XH[:, k, :], lambda k: ML[:, k, :], before)
                end_stage(pe, "pe")
                norm(l, 1)
                end_stage(pe, "pe")
                if l == 0:
                    for n, block in enumerate(DENSE_BLOCKS):
                        for f in block:
                            for j, nm in enumerate(("DG", "DU")):
                                for half in range(2):
                                    def before():
                                        if f == 0 and j == 0:
                                            pe.wait_ge(S("fx_lo"), half + 1)
                                        elif half == 0:
                                            if f:
                                                pe.wait_ge(S("f_h" if j else "f_s"), f)
                                            if n and f == block[0]:
                                                pe.wait_ge(S("f_acc"), 2 * n - 1 + j)
                                    columns_half(l, f"{nm}{f}", half, 4 * j, lambda k: FXH[:, k, :], lambda k: XL[:, k, 1:T + 1], before)
                        for f in block:
                            pe.wait_ge(S("f_lo"), f + 1)
                            if f == block[0]:
                                pe.wait_ge(S("f_h"), block[-1] + 1)
                            for half in range(2):
                                q0 = 4 * (f - block[0])
                                rows_half(l, f"DD{f}", half, lambda k: FHH[:, q0 + k, :], lambda k: FHL[:, q0 + k, :],
                                          f == block[0] and half == 0, f == block[-1] and half == 1)
                    end_stage(pe, "pe")

            for t in range(2):
                for k in range(KT):
                    ins = pe.matmul(PS[:, 0, 8 * t:8 * t + 8], xn[:, k, 1 + META + t * P:1 + META + (t + 1) * P],
                                    router_sb[:, k, :], start=(k == 0), stop=(k == KT - 1))
            ins.then_inc(S("q_log"), 1)
            for t in range(2):
                for q in range(2):
                    for k in range(4):
                        ins = pe.transpose(PS[:, 1 + 2 * t + q, k * P:(k + 1) * P],
                                           xn[:, 4 * q + k, 1 + META + t * P:1 + META + (t + 1) * P], C("ident"))
            ins.then_inc(S("q_turn"), 1)
            pe.wait_ge(S("q_sel"), 1)
            sel = lambda t: MR[:, 16 + 8 * t:24 + 8 * t]
            pe.matmul(PS[:, 5, 0:8], C("before"), sel(0), start=True, stop=True)
            pe.matmul(PS[:, 5, 8:16], C("ones"), sel(0), start=True, stop=False, skip_group_check=True)
            pe.matmul(PS[:, 5, 8:16], C("before"), sel(1), start=False, stop=True, skip_group_check=True)
            pe.matmul(PS[:, 5, 16:24], C("ones"), sel(0), start=True, stop=False, skip_group_check=True)
            pe.matmul(PS[:, 5, 16:24], C("ones"), sel(1), start=False, stop=True, skip_group_check=True).then_inc(S("q_rank"), 1)
            end_stage(pe, "pe")

            def gather(wait_for):
                pe.wait_ge(S("e_sel"), wait_for)
                for k in range(KT):
                    for t in range(2):
                        ins = pe.matmul(PS[:, 2 + k // 4, (k % 4) * SLOTS:(k % 4 + 1) * SLOTS], hnT[:, t, k * P:(k + 1) * P],
                                        SEL[:, t, :], start=(t == 0), stop=(t == 1))
                ins.then_inc(S("e_xg"), 1)

            def turn_hidden(n, f):
                pe.wait_ge(S("e_h"), n * FG + (f + 1))
                for q in range(4):
                    ins = pe.transpose(PS[:, 6, q * P:(q + 1) * P], MH[:, q * P:(q + 1) * P], C("ident"))
                ins.then_inc(S("e_ht"), 1)

            def half_products(n, j):
                kind, f = MOE_ORDER[j // 2]
                half, s_ = j % 2, (BASE + j) % 3
                if (kind, f, half) == ("g", 1, 0):
                    pe.wait_ge(S("e_free"), n + 1)
                pe.wait_ge(S("w_lo_dve"), n * HALVES + (j + 1 + BASE))
                pe.wait_ge(S("w_lo_pool"), n * HALVES + (j + 1 + BASE))
                if kind in "gu":
                    o = PS[:, 2 * (f % 2) + (kind == "u"), :]
                    for i in range(4):
                        k = 4 * half + i
                        x_, w_ = slice(k * SLOTS, (k + 1) * SLOTS), slice(i * 512, (i + 1) * 512)
                        ins = three_products(o, XGH[:, x_], XGL[:, x_], WH[s_][:, w_], WL[s_][:, w_], k == 0, k == KT - 1)
                else:
                    if half == 0:
                        pe.wait_ge(S("e_htl"), n * FG + (f + 1))
                    for i in range(2):
                        q = 2 * half + i
                        for hf in range(2):
                            x_, w_ = slice(q * P, (q + 1) * P), slice(i * D + hf * 512, i * D + hf * 512 + 512)
                            ins = three_products(PS[:, 4 + hf, :], HTH[f % 2][:, x_], HTL[f % 2][:, x_], WH[s_][:, w_], WL[s_][:, w_],
                                                 f == 0 and q == 0, f == FG - 1 and q == 3)
                ins.then_inc(S("w_used"), 1)

            def expert_products(pe, e, n, run, last):
                for j in range(1, HALVES):
                    kind, f = MOE_ORDER[j // 2]
                    half = j % 2
                    half_products(n, j)
                    if kind == "g" and f and half == 0:
                        turn_hidden(n, f - 1)
                    if (kind, f, half) == ("u", 3, 1):
                        pe.wait_ge(S("e_selg"), n + 1)
                        for t in range(2):
                            ins = pe.transpose(PS[:, 7, t * P:(t + 1) * P], SEL[:, 2 + t, :], C("ident"))
                        ins.then_inc(S("e_st"), 1)
                    if (kind, f, half) == ("d", FG - 2, 0):
                        turn_hidden(n, FG - 1)
                        gather(n + run + 2)
                pe.wait_ge(S("e_xgl"), n + run + 2)
                if not last:
                    half_products(n + 1, 0)
                pe.wait_ge(S("e_stc"), n + 1)
                pe.wait_ge(S("e_y"), n + 1)
                for k in range(KT):
                    bank = (2, 3, 6, 7)[k // 2]
                    ins = pe.matmul(PS[:, bank, (k % 2) * SEQ:(k % 2 + 1) * SEQ], YE[:, k * P:(k + 1) * P], SELT[:, :],
                                    start=True, stop=True)
                ins.then_inc(S("e_sc"), 1)

            def first_gather(pe, run):
                gather(run * (NE + 1) + 1)
                pe.wait_ge(S("e_xgl"), run * (NE + 1) + 1)
                half_products(run * NE, 0)

            for_all_experts(pe, expert_products, first_gather)
            end_stage(pe, "pe")
            norm(DEPTH, 0)
            pe.wait_ge(S("fin"), 1)
            for t in range(2):
                for q in range(2):
                    for k in range(4):
                        ins = pe.transpose(PS[:, 1 + 2 * t + q, k * P:(k + 1) * P], xn[:, 4 * q + k, 1 + META + t * P:1 + META + (t + 1) * P],
                                           C("ident"))
                    ins.then_inc(S("out_turned"), 1)

        @block.scalar
        def _(act):
            def a(ins):
                link(act, ins, "act_chain")

            n_dma = [0]

            def load(dst, src):
                act.dma_start(dst, src).then_inc(S("setup"), 16)
                n_dma[0] += 1

            act.dma_start(cst[:, 0:P], consts[:, 0:P]).then_inc(S("setup_x"), 16)
            act.dma_start(xin[0:META, 0, :], meta).then_inc(S("setup_x"), 16)
            for t in range(2):
                act.dma_start(xin[:, 1 + t, :], x[0, t * P:(t + 1) * P, :]).then_inc(S("setup_x"), 16)
            load(cst[:, P:NCONST], consts[:, P:NCONST])
            load(prm[:, :, :], params.rearrange("l p n -> p l n"))
            load(relb[:, :], rel_bias)

            def low_rank(l, ld):
                ld(wwa[0:64, :], w2[l])
                ld(wwa[64:P, :], a2[l])
                ld(wg0[:, :], g2[l, 0:P, :])
                ld(wg1[:, :], g2[l, P:P + 32, :])

            low_rank(0, load)
            load(vw1_sb[:, :, :], vw1[0].rearrange("(k p) n -> p k n", p=P))
            load(vw2_sb[:, :], vw2[0])
            load(router_sb[:, :, :], router[0].rearrange("(k p) n -> p k n", p=P))
            assert n_dma[0] == N_SETUP, n_dma

            act.wait_ge(S("setup_x"), 64)
            for k in range(KT):
                act.wait_ge(S("in_turned"), k + 1)
                ins = act.activation(hT[:, k, :], PS[:, k, 0:T], ACT.Copy)
                if k == 0:
                    ins.then_inc(S("in_copied"), 1)
            act.wait_ge(S("line_done"), 1)
            act.activation(lin[:, :], PS[0:NE, 0, 0:LINE], ACT.Copy).then_inc(S("lin_copied"), 1)
            act.wait_ge(S("setup"), 16 * N_SETUP)
            end_stage(act, "act")

            def high_half(g):
                name = half_chunk[g]
                b = position[name] % RING
                if g % 2 == 0:
                    act.wait_ge(S(f"landed{b}"), landed_at[position[name]])
                if g >= 3:
                    act.wait_ge(S("w_used"), g - 2)
                act.activation(WH[g % 3][:, :], ring[b][:, 2048 * (g % 2):2048 * (g % 2) + 2048], ACT.Copy).then_inc(S("w_hi"), 1)

            def norm(l, which, fill=()):
                act.activation(SQ[:, :, :], hT[:, :, :], ACT.Square).then_inc(S("sq_done"), 1)
                for g in fill[:1]:
                    high_half(g)
                act.wait_ge(S("ms_done"), 2 * l + which + 1)
                act.activation(rstd[:, :], rstd[:, :], ACT.Sqrt).then_inc(S("rt_done"), 1)
                for g in fill[1:]:
                    high_half(g)

            def copies(l, n0, dsts, scale=1.0, first=0):
                for i, dst in enumerate(dsts):
                    n = n0 + i
                    act.wait_ge(S("proj_done"), at("proj_done", l, n))
                    src = PS[:, (first + i) % 8, 0:T]
                    ins = None
                    for d_, s_ in dst(src):
                        if ins is not None:
                            a(ins)
                        ins = act.activation(d_, s_, ACT.Copy, scale=scale)
                    ins.then_inc(S("proj_copied"), 1)

            for l in range(DEPTH):
                norm(l, 0)
                end_stage(act, "act")
                copies(l, 0, [lambda s, p=p: [(qA[0:64, 2 * p, :], s[0:64]), (qA[64:P, 2 * p + 1, :], s[64:P])] for p in range(4)], QS)
                copies(l, 4, [lambda s, p=p: [(kA[:, p, 0:T], s)] for p in range(4)], 1.0, 4)
                for t, n in enumerate((P, P, T - 2 * P)):
                    act.wait_ge(S("proj_done"), at("proj_done", l, 8 + t))
                    act.activation(vA[0:n, t, :], PS[0:n, t, :], ACT.Copy).then_inc(S("proj_copied"), 1)
                end_stage(act, "act")
                def soft(h):
                    s, b = h % 2, 2 * (h % 2)
                    act.wait_ge(S("z_done"), at("z_done", l, h))
                    if h >= 2:
                        act.wait_ge(S("sp_done"), at("sp_done", l, h - 2))
                    act.activation(uA[:, s, 0:T], PS[:, b, 0:T], ACT.Abs)
                    a(act.activation(uA[:, s, T:432], PS[:, b + 1, 0:160], ACT.Abs))
                    a(act.activation(uA[:, s, :], uA[:, s, :], ACT.Exp, scale=-1.0))
                    act.activation(uA[:, s, :], uA[:, s, :], ACT.Ln, bias=1.0).then_inc(S("u_done"), 1)

                soft(0)
                for h in range(8):
                    if h < 7:
                        soft(h + 1)
                    s, b = h % 2, 2 * (h % 2)
                    act.wait_ge(S("arg_done"), at("arg_done", l, h))
                    act.activation(atA[:, s, 0:T], PS[:, b, 0:T], ACT.Exp)
                    act.activation(atA[:, s, T:432], PS[:, b + 1, 0:160], ACT.Exp).then_inc(S("at_done"), 1)
                    if h < 4:
                        copies(l, 11 + h, [lambda s, j=h: [(qCm[:, j, :], s[:, 0:META]),
                                                           (qCx[:, :, j, :], s[:, META:T].rearrange("p (c q) -> p c q", q=CH))]],
                               QS, 6 + h % 2)
                    elif h < 6:
                        copies(l, 11 + h, [lambda s: [((kC, vC)[h - 4][:, :], s)]], 1.0, 6 + h % 2)
                end_stage(act, "act")
                act.wait_ge(S("c_vt"), at("c_vt", l, 0))
                act.activation(vW[0:80, 0, :], PS[0:80, 6, 0:P], ACT.Copy)
                act.activation(vW[:, 1:4, :], PS[:, 6, P:4 * P].rearrange("p (a b) -> p a b", b=P), ACT.Copy).then_inc(S("c_vtc"), 1)

                def projected(t):
                    act.wait_ge(S("proj_done"), at("proj_done", l, 17 + t))
                    if t < 12:
                        dst, rows = (R, K, V)[t // 4][:, t % 4, PADC:TP], P
                    else:
                        rows = (P, P, 32)[t - 12]
                        dst = PX[0:rows, t - 12, PADC:TP]
                    act.activation(dst, PS[0:rows, 5 + t % 3, 0:T], ACT.Copy).then_inc(S("proj_copied"), 1)

                for u in range(N_UNITS[l]):
                    meta_q = u == 4
                    m, v, n = (64, 2, META) if meta_q else (P, 4, 80 if u == 0 else 144)
                    act.wait_ge(S("c_m"), at("c_m", l, u))
                    act.activation(sC[0:m, 0:v, 0:n], sC[0:m, 0:v, 0:n], ACT.Exp)
                    act.activation(mC[0:m, 8:8 + v], mC[0:m, 4:4 + v], ACT.Exp).then_inc(S("c_e"), 1)
                    ahead, behind = unit_tiles(l, u)
                    for t in ahead:
                        projected(t)
                    act.wait_ge(S("c_t"), at("c_t", l, u))
                    if meta_q or u == 0:
                        rows, w = (META, P) if meta_q else (80, 512)
                        act.activation(pTC[0:rows, :, :].rearrange("p a b -> p (a b)")[:, 0:w], PS[0:rows, 2, 0:w], ACT.Copy)\
                            .then_inc(S("c_tc"), 1)
                    else:
                        act.activation(pTC[:, :, :].rearrange("p a b -> p (a b)"), PS[:, 2, :], ACT.Copy)
                        act.activation(pTm[0:META, :, :].rearrange("p a b -> p (a b)"), PS[0:META, 3, :], ACT.Copy)\
                            .then_inc(S("c_tc"), 1)
                    for t in behind:
                        projected(t)
                    act.wait_ge(S("c_y"), at("c_y", l, u))
                    if meta_q:
                        act.activation(yC[:, :, 0:META], PS[:, 4, 0:64].rearrange("p (a b) -> p a b", b=META), ACT.Copy).then_inc(S("c_yc"), 1)
                    else:
                        t0 = META + CH * u
                        act.activation(yC[:, :, t0:t0 + CH], PS[:, 4, 0:256].rearrange("p (a b) -> p a b", b=CH), ACT.Copy)\
                            .then_inc(S("c_yc"), 1)
                end_stage(act, "act")
                act.wait_ge(S("x_mixed"), l + 1)
                act.activation(PX[0:64, 0, PADC:TP], PX[0:64, 0, PADC:TP], ACT.Tanh)
                act.activation(PX[:, 1, PADC:TP], PX[:, 1, PADC:TP], ACT.Sigmoid)
                act.activation(PX[0:32, 2, PADC:TP], PX[0:32, 2, PADC:TP], ACT.Sigmoid).then_inc(S("w_in"), 1)
                act.wait_ge(S("w_mm"), at("w_mm", l, 0))
                for p in range(4):
                    ins = act.activation(LW[:, p, PADC:TP], PS[:, p, 0:T], ACT.Sigmoid, bias=prm_col(l, "w0", p))
                ins.then_inc(S("w_ev"), 1)
                act.wait_ge(S("w_mm"), at("w_mm", l, 1))
                for p in range(4):
                    ins = act.activation(AI[:, p, PADC:TP], PS[:, 4 + p, 0:T], ACT.Sigmoid, bias=prm_col(l, "a0", p))
                ins.then_inc(S("w_ev"), 1)
                act.wait_ge(S("w_mm"), at("w_mm", l, 2))
                act.activation(GT[:, :, PADC:TP], PS[:, 0:4, 0:T], ACT.Copy).then_inc(S("w_ev"), 1)
                if l:
                    act.wait_ge(S("v_mm"), 1)
                    act.activation(PX[0:32, 1, PADC:TP], PS[0:32, 4, 0:T], ACT.Copy).then_inc(S("v_ev"), 1)
                    act.wait_ge(S("v_mm"), 2)
                    for p in range(4):
                        ins = act.activation(DD[:, p, PADC:TP], PS[:, 4 + p, 0:T], ACT.Sigmoid, bias=prm_col(l, "vres_b", p))
                    ins.then_inc(S("v_ev"), 1)
                end_stage(act, "act")
                act.wait_ge(S("k_sum"), at("k_sum", l, 0))
                act.activation(BN[:, :, PADC:TP], PS[:, 0:4, 0:T], ACT.Sqrt).then_inc(S("k_rt"), 1)
                for i in range(3):
                    act.wait_ge(S("g_done"), 3 * l + i + 1)
                    src = (LWG, LWG, LW)[i]
                    act.activation(DD[:, :, :], src[:, :, :], ACT.Exp, scale=-1.0 if i == 1 else 1.0).then_inc(S("e_done"), 1)
                    for n in ((0, 1, 2), (3, 4, 5), (6, 7))[i]:
                        act.wait_ge(S("eg_done"), 8 * l + n + 1)
                        act.activation(EG[:, n, :], PS[:, n % 4, 0:T], ACT.Copy).then_inc(S("eg_copied"), 1)
                end_stage(act, "act")
                for c in range(NCH):
                    cc = slice(c * CH, (c + 1) * CH)

                    def copy(name, s_, o, src, scale=1.0):
                        act.activation(o[:, 2 * s_:2 * s_ + 2, :], src.rearrange("p (a b) -> p a b", a=2), ACT.Copy, scale=scale)\
                            .then_inc(S(f"r{s_}_{name}"), 1)

                    def keys_rows(s_):
                        act.wait_ge(*W("mm", s_, l, c))
                        copy("vc", s_, Vst, PS[:, 4 * s_ + 2, 0:P])
                        act.activation(BT[:, 2 * s_:2 * s_ + 2, :], PS[:, 4 * s_ + 1, 0:256].rearrange("p (a b) -> p a b", a=2), ACT.Copy)
                        act.activation(HT[:, 2 * s_:2 * s_ + 2, :], PS[:, 4 * s_ + 1, 256:512].rearrange("p (a b) -> p a b", a=2), ACT.Copy)

                    def turned(s_):
                        act.wait_ge(*W("t", s_, l, c))
                        copy("ti", s_, TI, PS[:, 4 * s_ + 3, 0:256])

                    def update(s_, w):
                        act.wait_ge(*W("d", s_, l, c, w))
                        if w < 4:
                            copy("ti", s_, TI, PS[:, 4 * s_ + 1, 0:256])
                        copy("ttc", s_, TT, PS[:, 4 * s_ + 3, 0:256])

                    def right(s_):
                        act.wait_ge(*W("x", s_, l, c))
                        copy("xc", s_, Xst, PS[:, 4 * s_ + 2, 0:P], -1.0)

                    def solved(s_):
                        act.wait_ge(*W("u", s_, l, c))
                        copy("uc", s_, Ust, PS[:, 4 * s_ + 3, 0:P])

                    def result(s_):
                        act.wait_ge(*W("y", s_, l, c))
                        act.activation(Y[:, 2 * s_:2 * s_ + 2, cc], PS[:, 4 * s_ + 1, 0:P].rearrange("p (a b) -> p a b", a=2), ACT.Copy)\
                            .then_inc(S(f"r{s_}_yc"), 1)

                    if c:
                        for s_ in range(2):
                            act.wait_ge(*W("y", s_, l, c - 1))
                    kr = KR[:, :, :].rearrange("p (a b) c -> p a b c", b=2)
                    act.activation(kr[:, :, 0, :], KK[:, :, cc], ACT.Copy)
                    act.activation(kr[:, :, 1, :], R[:, :, cc], ACT.Copy).then_inc(S("r_kr"), 1)
                    steps = [keys_rows, turned] + [lambda s_, w=w: update(s_, w) for w in range(5)] + [right, solved, result]
                    for step in steps:
                        for s_ in range(2):
                            step(s_)
                end_stage(act, "act")
                act.wait_ge(S("n_d"), at("n_d", l, 0))
                act.activation(K[:, :, PADC:TP], Y[:, :, PADC:TP], ACT.Square).then_inc(S("n_sq"), 1)
                high_half(first_split[l])
                act.wait_ge(S("n_e"), at("n_e", l, 0))
                act.activation(K[:, :, PADC:TP], K[:, :, PADC:TP], ACT.Sqrt).then_inc(S("n_s"), 1)
                high_half(first_split[l] + 1)
                end_stage(act, "act")
                act.activation(YH[0][:, :, :], yA[:, :, :], ACT.Copy).then_inc(S("x_hi"), 1)
                for h in range(2):
                    act.activation(SG[:, 4 * h:4 * h + 4, :], EG[:, 4 * h:4 * h + 4, :], ACT.Sigmoid).then_inc(S("m_s"), 1)
                act.wait_ge(S("m_s"), at("m_s", l, 1))
                high_half(first_split[l] + 2)
                act.activation(XH[:, 0:4, :], xn[:, 0:4, 1:T + 1], ACT.Copy).then_inc(S("x_hi"), 1)
                act.activation(XH[:, 4:8, :], xn[:, 4:8, 1:T + 1], ACT.Copy).then_inc(S("x_hi"), 1)
                for b, y in ((1, R[:, :, PADC:TP]), (2, yC[:, :, :])):
                    act.activation(YH[b][:, :, :], y, ACT.Copy).then_inc(S("x_hi"), 1)

                def gates(b, h):
                    act.wait_ge(S("w_used"), split_half[(l, f"G{b}{h}")] + 2)
                    if b:
                        act.wait_ge(S("m_read"), at("m_read", l, 2 * (b - 1) + h))
                    act.activation(SG[:, 4 * h:4 * h + 4, :], PS[:, 4 * h:4 * h + 4, 0:T], ACT.Sigmoid).then_inc(S("m_s"), 1)

                def merged_high(h):
                    act.wait_ge(S("m_sum"), 2 * l + h + 1)
                    act.activation(XH[:, 4 * h:4 * h + 4, :], MG[:, 4 * h:4 * h + 4, :], ACT.Copy).then_inc(S("x_hi"), 1)

                events = {}
                for b in range(1, 3):
                    for h in range(2):
                        after_half(events, l, f"G{b}{h}", 1).append((gates, b, h))
                for h in range(2):
                    after_half(events, l, "P2", 1).append((merged_high, h))
                split_stage(high_half, first_split[l], 18, events, 3)
                if l == 0:
                    low_rank(1, lambda d_, s_: act.dma_start(d_, s_).then_inc(S("low_rank1"), 16))
                    act.wait_ge(S("low_rank1"), 64)
                end_stage(act, "act")
                norm(l, 1, [first_split["dense"] + i for i in range(3)] if l == 0 else ())
                end_stage(act, "act")
                if l == 0:
                    act.activation(FXH[:, 0:4, :], xn[:, 0:4, 1:T + 1], ACT.Copy).then_inc(S("fx_hi"), 1)
                    act.activation(FXH[:, 4:8, :], xn[:, 4:8, 1:T + 1], ACT.Copy).then_inc(S("fx_hi"), 1)

                    def silu(f):
                        act.wait_ge(S("w_used"), split_half[(0, f"DG{f}")] + 2)
                        if f:
                            act.wait_ge(S("f_h"), f)
                        act.activation(SF[:, :, :], PS[:, 0:4, 0:T], ACT.Silu).then_inc(S("f_s"), 1)

                    def hidden_high(f):
                        q = 4 * (f % 4)
                        act.wait_ge(S("f_h"), f + 1)
                        act.activation(FHH[:, q:q + 4, :], HF[:, q:q + 4, :], ACT.Copy).then_inc(S("f_hi"), 1)

                    events = {}
                    for f in range(FG):
                        after_half(events, l, f"DG{f}", 1).append((silu, f))
                        after_half(events, l, f"DU{f}", 1).append((hidden_high, f))
                    split_stage(high_half, first_split["dense"], 6 * FG, events, 3)
                    end_stage(act, "act")

            act.wait_ge(S("q_turn"), 1)
            for t in range(2):
                ins = act.activation(hnT[:, t, :].rearrange("p (a b) -> p a b", a=2), PS[:, 1 + 2 * t:3 + 2 * t, :], ACT.Copy)
            a(ins)
            act.wait_ge(S("q_gap"), 1)
            act.activation(MR[:, 176:178], MR[:, 176:178], ACT.Exp).then_inc(S("q_exp"), 1)
            end_stage(act, "act")

            def expert_high(n, j):
                b = (MOE0 + j // 2) % RING
                if j % 2 == 0:
                    act.wait_ge(S(f"landed{b}"), n * (32 * PER_BUF) + (landed_moe0[b] + 32 * (j // 2 // RING + 1)))
                act.wait_ge(S("w_used"), n * HALVES + (j - 2 + BASE))
                act.activation(WH[(BASE + j) % 3][:, :], ring[b][:, 2048 * (j % 2):2048 * (j % 2) + 2048], ACT.Copy).then_inc(S("w_hi"), 1)

            def gathered_high(act, wait_for):
                act.wait_ge(S("e_xg"), wait_for)
                act.activation(XGH[:, :].rearrange("p (a b) -> p a b", a=2), PS[:, 2:4, :], ACT.Copy).then_inc(S("e_xgh"), 1)

            def expert_highs(act, e, n, run, last):
                def gate(f):
                    act.wait_ge(S("w_used"), used(n, "g", f))
                    act.activation(MS[:, :], PS[:, 2 * (f % 2), :], ACT.Silu).then_inc(S("e_s"), 1)

                def hidden_high(f):
                    act.wait_ge(S("e_ht"), n * FG + (f + 1))
                    act.activation(HTH[f % 2][:, :], PS[:, 6, :], ACT.Copy).then_inc(S("e_hth"), 1)

                def scatter_rows(f):
                    act.wait_ge(S("e_st"), n + 1)
                    act.activation(SELT[:, :], PS[:, 7, 0:SEQ], ACT.Copy).then_inc(S("e_stc"), 1)

                events = {}
                for f in range(FG):
                    at_half(events, "g", f, 1, 2).append((gate, f))
                    at_half(events, "u", f, 1, 5 if f < FG - 1 else 3).append((hidden_high, f))
                at_half(events, "u", 3, 1, 4).append((scatter_rows, 3))
                for j in range(3, HALVES):
                    expert_high(n, j)
                    for do, f in events.get(j, []):
                        do(f)
                gathered_high(act, n + run + 2)
                if not last:
                    expert_high(n + 1, 0)
                    expert_high(n + 1, 1)
                act.wait_ge(S("w_used"), used(n, "d", FG - 1))
                act.activation(YE[:, :].rearrange("p (a b) -> p a b", a=2), PS[:, 4:6, :], ACT.Copy).then_inc(S("e_y"), 1)
                if not last:
                    expert_high(n + 1, 2)

            def first_highs(act, run):
                for j in range(3):
                    expert_high(run * NE, j)
                gathered_high(act, run * (NE + 1) + 1)

            for_all_experts(act, expert_highs, first_highs)
            end_stage(act, "act")
            norm(DEPTH, 0)
            for t in range(4):
                act.wait_ge(S("out_turned"), t + 1)
                act.activation(ostage[:, t // 2, 512 * (t % 2):512 * (t % 2) + 512], PS[:, 1 + t, :], ACT.Copy).then_inc(S("out_copied"), 1)

        @block.gpsimd
        def _(pool):
            mask4 = bc(C("bd").rearrange("p (a b) -> p a b", a=2), [P, 4, 2, CH], 1)

            def block_diagonal(o, src):
                return pool.tensor_tensor(o[:, :, :].rearrange("p a (b c) -> p a b c", b=2), bc(src, [P, 4, 2, CH], 2), mask4, ALU.mult)

            c0 = 2048 - POOL_COLS

            def low_half(g):
                pool.wait_ge(S("w_hi"), g + 1)
                pool.tensor_tensor(WL[g % 3][:, c0:2048], ring[position[half_chunk[g]] % RING][:, 2048 * (g % 2) + c0:2048 * (g % 2) + 2048],
                                   WH[g % 3][:, c0:2048].bitcast(F32), ALU.subtract).then_inc(S("w_lo_pool"), 1)

            for l in range(DEPTH):
                pool.wait_ge(S("r_open"), at("r_open", l, 0))
                for c in range(NCH):
                    cc = slice(c * CH, (c + 1) * CH)
                    if c:
                        for s_ in range(2):
                            pool.wait_ge(*W("mm", s_, l, c - 1))
                    block_diagonal(Bbd, AI[:, :, cc])
                    block_diagonal(Hbd, K[:, :, cc])
                    block_diagonal(VTbd, V[:, :, cc]).then_inc(S("r_bd"), 1)
                    if c:
                        for s_ in range(2):
                            pool.wait_ge(*W("x", s_, l, c - 1))
                    block_diagonal(Kbd, KK[:, :, cc]).then_inc(S("r_kbd"), 1)
                split_stage(low_half, first_split[l], 18, {})
                if l == 0:
                    split_stage(low_half, first_split["dense"], 6 * FG, {})

            def expert_lows(pool, e, n, run, last):
                for j in range(HALVES):
                    i, half = j // 2, j % 2
                    pool.wait_ge(S("w_hi"), n * HALVES + (j + 1 + BASE))
                    pool.tensor_tensor(WL[(BASE + j) % 3][:, c0:2048], ring[(MOE0 + i) % RING][:, 2048 * half + c0:2048 * half + 2048],
                                       WH[(BASE + j) % 3][:, c0:2048].bitcast(F32), ALU.subtract).then_inc(S("w_lo_pool"), 1)

            for_all_experts(pool, expert_lows)

        @block.vector
        def _(dve):
            def v(ins):
                link(dve, ins, "dve_chain")

            tt = lambda o, a_, b_, op: dve.tensor_tensor(o, a_, b_, op)

            dve.memset(xn[:, :, 0:1], 0.0)
            v(dve.memset(egc[:, :, :], 0.0))
            end_stage(dve, "dve")

            lows = 2048 - POOL_COLS

            def low_half(g):
                dve.wait_ge(S("w_hi"), g + 1)
                tt(WL[g % 3][:, 0:lows], ring[position[half_chunk[g]] % RING][:, 2048 * (g % 2):2048 * (g % 2) + lows],
                   WH[g % 3][:, 0:lows].bitcast(F32), ALU.subtract).then_inc(S("w_lo_dve"), 1)

            def norm(l, which, gain):
                dve.wait_ge(S("sum_done"), 2 * l + which + 1)
                dve.tensor_scalar(rstd[:, :], PS[:, 0, 0:T], 1.0 / D, EPS, ALU.mult, ALU.add).then_inc(S("ms_done"), 1)
                dve.wait_ge(S("rt_done"), 2 * l + which + 1)
                v(dve.reciprocal(rstd[:, :], rstd[:, :]))
                for k in range(KT):
                    ins = dve.scalar_tensor_tensor(xn[:, k, 1:T + 1], hT[:, k, :], prm_col(min(l, DEPTH - 1), gain, k), rstd[:, :],
                                                   ALU.mult, ALU.mult)
                return ins

            for l in range(DEPTH):
                dve.memset(kA[:, :, T:384], 0.0)
                dve.memset(qA[:, :, :], 0.0)
                dve.memset(vA[:, 2, :], 0.0)
                v(norm(l, 0, "norm_mix"))
                end_stage(dve, "dve")
                end_stage(dve, "dve")
                for h in range(8):
                    s, b = h % 2, 2 * (h % 2)
                    dve.wait_ge(S("u_done"), 8 * l + h + 1)
                    if h >= 2:
                        dve.wait_ge(S("arg_done"), at("arg_done", l, h - 2))
                    dve.scalar_tensor_tensor(spA[:, s, 0:T], PS[:, b, 0:T], 0.0, uA[:, s, 0:T], ALU.max, ALU.add)
                    v(dve.scalar_tensor_tensor(spA[:, s, T:432], PS[:, b + 1, 0:160], 0.0, uA[:, s, T:432], ALU.max, ALU.add))
                    tt(spA[:, s, :], spA[:, s, :], C("sbmask"), ALU.mult).then_inc(S("sp_done"), 1)
                    if h % 2 == 1:
                        p = h // 2
                        dve.wait_ge(S("ya_done"), at("ya_done", l, p))
                        dve.tensor_copy(yA[:, p, :], PS[:, 4 + p % 2, 0:T]).then_inc(S("ya_copied"), 1)
                end_stage(dve, "dve")
                if l == 0:
                    dve.wait_ge(S("bias_ready"), 16 * 14)
                for u in range(5):
                    meta_q = u == 4
                    if meta_q and l == DEPTH - 1:
                        dve.memset(yC[:, :, 0:META], 0.0)
                        break
                    m, w, n = (64, 2, META) if meta_q else (P, 4, 80 if u == 0 else 144)
                    dve.wait_ge(S("c_z"), at("c_z", l, u))
                    for g in range(2):
                        if meta_q:
                            tt(sC[0:64, g, 0:META], PS[0:64, g, 0:META], biasq[:, g, :], ALU.add)
                            continue
                        src = PS[:, g, 0:2 * n].rearrange("p (a b) -> p a b", a=2)
                        if u == 0:
                            ins = tt(sC[:, 2 * g:2 * g + 2, 0:80], src, bias0[:, 2 * g:2 * g + 2, :], ALU.add)
                        else:
                            tt(sC[:, 2 * g:2 * g + 2, 0:META], src[:, :, 0:META], biasm[:, u - 1, 2 * g:2 * g + 2, :], ALU.add)
                            ins = tt(sC[:, 2 * g:2 * g + 2, META:144], src[:, :, META:144], biasb[:, 2 * g:2 * g + 2, :], ALU.add)
                    sv = sC[0:m, 0:w, 0:n]
                    o, _ = PARAM_COLS["sink_meta" if meta_q else "sink"]
                    v(dve.memset(small[:, 60:61], 0.0))
                    v(dve.tensor_reduce(mC[0:m, 0:w], sv, AX.X, ALU.max))
                    v(tt(mC[0:m, 0:w], mC[0:m, 0:w], prm[0:m, l, o:o + w], ALU.max))
                    tt(mC[0:m, 4:4 + w], prm[0:m, l, o:o + w], mC[0:m, 0:w], ALU.subtract)
                    tt(sv, sv, bc(mC[0:m, 0:w], [m, w, n], 2), ALU.subtract).then_inc(S("c_m"), 1)
                    dve.wait_ge(S("c_e"), at("c_e", l, u))
                    v(dve.tensor_reduce(mC[0:m, 12:12 + w], sv, AX.X, ALU.add))
                    v(tt(mC[0:m, 12:12 + w], mC[0:m, 12:12 + w], mC[0:m, 8:8 + w], ALU.add))
                    v(dve.reciprocal(mC[0:m, 12:12 + w], mC[0:m, 12:12 + w]))
                    tt(sv, sv, bc(mC[0:m, 12:12 + w], [m, w, n], 2), ALU.mult).then_inc(S("c_p"), 1)
                    dve.wait_ge(S("c_t"), at("c_t", l, u))
                for X_ in (R, K, V, LW, AI, KK):
                    dve.memset(X_[:, :, 0:PADC], 0.0)
                v(dve.memset(PX[:, :, 0:PADC], 0.0))
                end_stage(dve, "dve")
                def mix(X_, rows, mus, sem=None):
                    w = X_.shape[1]
                    d_ = DD[0:rows, 0:w, PADC:TP]
                    v(tt(d_, X_[0:rows, :, PADC - 1:TP - 1], X_[0:rows, :, PADC:TP], ALU.subtract))
                    for i in range(w):
                        ins = dve.scalar_tensor_tensor(X_[0:rows, i, PADC:TP], d_[:, i, :], mus(i)[0:rows], X_[0:rows, i, PADC:TP],
                                                       ALU.mult, ALU.add)
                    return ins

                v(mix(PX[:, 0:1, :], P, lambda i: prm_col(l, "mu_wa", 0)))
                v(mix(PX[:, 1:2, :], P, lambda i: prm_col(l, "mu_g0", 0)))
                mix(PX[:, 2:3, :], 32, lambda i: prm_col(l, "mu_g1", 0)).then_inc(S("x_mixed"), 1)
                dve.wait_ge(S("x_mixed"), l + 1)
                v(mix(R, P, lambda i: prm_col(l, "mu_r", i)))
                v(mix(K, P, lambda i: prm_col(l, "mu_k", i)))
                v(mix(V, P, lambda i: prm_col(l, "mu_v", i)))
                if l == 0:
                    v(dve.tensor_copy(VF[:, :, :], V[:, :, :]))
                else:
                    v(tt(SQ_v[:, :, :], xn[:, :, 0:T], xn[:, :, 1:T + 1], ALU.subtract))
                    for k in range(KT):
                        ins = dve.scalar_tensor_tensor(SQ_v[:, k, :], SQ_v[:, k, :], prm_col(l, "vres_mu", k), xn[:, k, 1:T + 1],
                                                       ALU.mult, ALU.add)
                    ins.then_inc(S("xv_done"), 1)
                end_stage(dve, "dve")
                TR = slice(PADC, TP)
                if l:
                    v(tt(SV[:, :, TR], VF[:, :, TR], V[:, :, TR], ALU.subtract))
                    v(tt(SV[:, :, TR], SV[:, :, TR], DD[:, :, TR], ALU.mult))
                    v(tt(V[:, :, TR], V[:, :, TR], SV[:, :, TR], ALU.add))
                    dve.memset(KK[:, :, 0:PADC], 0.0)
                v(dve.tensor_scalar(LW[:, :, TR], LW[:, :, TR], DECAY_SCALE, None, ALU.mult))
                for p in range(4):
                    ins = dve.tensor_scalar(KK[:, p, TR], K[:, p, TR], prm_col(l, "k_k", p), None, ALU.mult)
                v(ins)
                tt(DD[:, :, TR], KK[:, :, TR], KK[:, :, TR], ALU.mult).then_inc(S("k_sq"), 1)
                dve.wait_ge(S("k_sum"), at("k_sum", l, 0))
                for p in range(4):
                    ins = dve.tensor_scalar(DD[:, p, TR], AI[:, p, TR], -1.0, prm_col(l, "k_a", p), ALU.add, ALU.mult)
                v(ins)
                v(dve.scalar_tensor_tensor(K[:, :, TR], DD[:, :, TR], 1.0, K[:, :, TR], ALU.add, ALU.mult))
                v(tt(DD[:, :, TR], R[:, :, TR], K[:, :, TR], ALU.mult))
                for p in range(4):
                    ins = dve.tensor_scalar(DD[:, p, TR], DD[:, p, TR], prm_col(l, "r_k", p), None, ALU.mult)
                ins.then_inc(S("b_pr"), 1)
                dve.wait_ge(S("k_rt"), at("k_rt", l, 0))
                v(dve.tensor_scalar(BN[:, :, TR], BN[:, :, TR], 1e-12, None, ALU.max))
                v(dve.reciprocal(BN[:, :, TR], BN[:, :, TR]))
                v(tt(KK[:, :, TR], KK[:, :, TR], BN[:, :, TR], ALU.mult))
                v(tt(AI[:, :, TR], AI[:, :, TR], KK[:, :, TR], ALU.mult))
                dve.wait_ge(S("b_sum"), at("b_sum", l, 0))
                for p in range(4):
                    ins = dve.tensor_tensor_scan(LWG[:, p, :], C("reset"), LW[:, p, :], 0.0, ALU.mult, ALU.add)
                ins.then_inc(S("g_done"), 1)
                dve.wait_ge(S("e_done"), at("e_done", l, 0))
                dve.tensor_copy(egc[:, :, :], DD[:, :, :].rearrange("p a (c q) -> p a c q", q=CH)[:, :, :, CH - 1])
                v(tt(R[:, :, :], R[:, :, :], DD[:, :, :], ALU.mult))
                tt(LW[:, :, :], LWG[:, :, :], LW[:, :, :], ALU.subtract).then_inc(S("g_done"), 1)
                dve.wait_ge(S("e_done"), at("e_done", l, 1))
                tt(AI[:, :, :], AI[:, :, :], DD[:, :, :], ALU.mult)
                v(tt(K[:, :, :], K[:, :, :], DD[:, :, :], ALU.mult))
                dve.memset(small[:, 61:62], 0.0).then_inc(S("g_done"), 1)
                dve.wait_ge(S("e_done"), at("e_done", l, 2))
                v(tt(KK[:, :, :], KK[:, :, :], DD[:, :, :], ALU.mult))
                v(tt(BN[:, :, TR], V[:, :, TR], PS[:, 4:8, 0:T], ALU.mult))
                dve.memset(state[:, :, :], 0.0)
                v(dve.memset(Sbd[:, :, :], 0.0))
                end_stage(dve, "dve")
                dve.memset(small[:, 57:58], 0.0).then_inc(S("r_open"), 1)

                mask = lambda m_, n: bc(m_.rearrange("p (a b) -> p a b", a=2), [P, n, 2, CH], 1)
                wide = lambda x_: bc(x_, [P, x_.shape[1], 2, CH], 2)
                two = lambda x_, s_: x_[:, 2 * s_:2 * s_ + 2, :].rearrange("p a (b c) -> p a b c", b=2)
                for c in range(NCH):
                    first = lambda s_: PS[:, 4 * s_, :].rearrange("p (j m x q) -> p j m x q", j=2, m=2, x=2)

                    def signal(ins, name, s_):
                        ins.then_inc(S(f"r{s_}_{name}"), 1)

                    def level_mask(s_, w):
                        signal(tt(two(NTb, s_), wide(first(s_)[:, :, 0, 0, :]), mask(C("level", (w + 1) * P, P), 2), ALU.mult), "lv", s_)

                    def start(s_):
                        dve.wait_ge(*W("mm", s_, l, c))
                        v(tt(two(TT, s_), wide(first(s_)[:, :, 0, 0, :]), mask(C("level", 0, P), 2), ALU.mult))
                        t2 = TT[:, 2 * s_:2 * s_ + 2, :]
                        signal(tt(t2, bc(C("ident"), [P, 2, P], 1), t2, ALU.subtract), "tt", s_)
                        level_mask(s_, 0)

                    def operands(s_):
                        tt(two(M2bd, s_), wide(first(s_)[:, :, 1, 0, :]), mask(C("strict"), 2), ALU.mult)
                        tt(AA[:, 4 * s_:4 * s_ + 4, :].rearrange("p (j m) q -> p j m q", m=2), first(s_)[:, :, :, 1, :],
                           bc(bc(C("incl"), [P, 2, CH], 1), [P, 2, 2, CH], 1), ALU.mult)
                        dve.wait_ge(*W("vc", s_, l, c))
                        signal(tt(two(Vbd, s_), wide(Vst[:, 2 * s_:2 * s_ + 2, :]), mask(C("bd"), 2), ALU.mult), "cp", s_)

                    def power(s_, w):
                        dve.wait_ge(*W("p", s_, l, c, w))
                        signal(tt(PW[:, 2 * s_:2 * s_ + 2, :], bc(C("ident"), [P, 2, P], 1),
                                  PS[:, 4 * s_ + 2, 0:256].rearrange("p (a b) -> p a b", a=2), ALU.subtract), "pw", s_)
                        if w < 4:
                            level_mask(s_, w + 1)

                    def solution(s_):
                        dve.wait_ge(*W("uc", s_, l, c))
                        signal(tt(two(Ubd, s_), wide(Ust[:, 2 * s_:2 * s_ + 2, :]), mask(C("bd"), 2), ALU.mult), "ubd", s_)

                    def new_state(s_):
                        dve.wait_ge(*W("s", s_, l, c))
                        st = state[:, 2 * s_:2 * s_ + 2, :]
                        v(tt(st, st, PS[:, 4 * s_, 0:P].rearrange("p (a b) -> p a b", b=CH), ALU.add))
                        v(tt(st, st, bc(egc[:, 2 * s_:2 * s_ + 2, c], [P, 2, CH], 2), ALU.mult))
                        dve.wait_ge(*W("y", s_, l, c))
                        signal(tt(two(Sbd, s_), wide(st), mask(C("bd"), 2), ALU.mult), "st", s_)

                    steps = [start] + [lambda s_: power(s_, 0), operands] + [lambda s_, w=w: power(s_, w) for w in range(1, 5)]
                    steps += [solution, new_state]
                    for step in steps:
                        for s_ in range(2):
                            step(s_)
                end_stage(dve, "dve")
                dve.wait_ge(S("n_m"), at("n_m", l, 0))
                dve.scalar_tensor_tensor(Y[:, :, TR], PS[:, 0:4, 0:T], -1.0 / HD, Y[:, :, TR], ALU.mult, ALU.add).then_inc(S("n_d"), 1)
                dve.wait_ge(S("n_v"), at("n_v", l, 0))
                dve.tensor_scalar(K[:, :, TR], PS[:, 4:8, 0:T], 1.0 / HD, GN_EPS, ALU.mult, ALU.add).then_inc(S("n_e"), 1)
                dve.wait_ge(S("n_s"), at("n_s", l, 0))
                v(dve.reciprocal(K[:, :, TR], K[:, :, TR]))
                v(tt(Y[:, :, TR], Y[:, :, TR], K[:, :, TR], ALU.mult))
                for p in range(4):
                    ins = dve.tensor_scalar(Y[:, p, TR], Y[:, p, TR], prm_col(l, "ln_g", p), prm_col(l, "ln_b", p), ALU.mult, ALU.add)
                v(ins)
                v(tt(Y[:, :, TR], Y[:, :, TR], BN[:, :, TR], ALU.add))
                v(tt(R[:, :, TR], Y[:, :, TR], GT[:, :, TR], ALU.mult))
                end_stage(dve, "dve")
                def operand_low(n, lo, x_, hi):
                    dve.wait_ge(S("x_hi"), 7 * l + n)
                    tt(lo, x_, hi.bitcast(F32), ALU.subtract).then_inc(S("x_lo"), 1)

                low_half(first_split[l])
                low_half(first_split[l] + 1)
                operand_low(1, YL[0][:, :, :], yA[:, :, :], YH[0][:, :, :])
                low_half(first_split[l] + 2)
                for i in range(2):
                    q = slice(4 * i, 4 * i + 4)
                    operand_low(2 + i, XL[:, q, 1:T + 1], xn[:, q, 1:T + 1], XH[:, q, :])
                operand_low(4, YL[1][:, :, TR], R[:, :, TR], YH[1][:, :, :])
                operand_low(5, YL[2][:, :, :], yC[:, :, :], YH[2][:, :, :])

                def gated(b, h):
                    q = slice(4 * h, 4 * h + 4)
                    if h == 0:
                        dve.wait_ge(S("m_p"), 3 * l + b + 1)
                    else:
                        dve.wait_ge(S("w_used"), split_half[(l, f"P{b}")] + 2)
                    dst = TMP[:, :, :] if b else MG[:, q, :]
                    tt(dst, SG[:, q, :], PS[:, q, 0:T], ALU.mult).then_inc(S("m_read"), 1)
                    dve.wait_ge(S("m_read"), at("m_read", l, 2 * b + h))
                    if b:
                        v(tt(MG[:, q, :], MG[:, q, :], TMP[:, :, :], ALU.add))
                    if b == 2:
                        dve.memset(small[:, 55:56], 0.0).then_inc(S("m_sum"), 1)

                def merged_low(h):
                    q = slice(4 * h, 4 * h + 4)
                    dve.wait_ge(S("x_hi"), 7 * l + 6 + h)
                    tt(ML[:, q, :], MG[:, q, :], XH[:, q, :].bitcast(F32), ALU.subtract).then_inc(S("x_lo"), 1)

                def residual(h):
                    q = slice(4 * h, 4 * h + 4)
                    dve.wait_ge(S("w_used"), split_half[(l, f"O{h}")] + 2)
                    v(tt(hT[:, q, :], hT[:, q, :], PS[:, q, 0:T], ALU.add))

                events = {}
                for b in range(3):
                    for h in range(2):
                        after_half(events, l, f"P{b}", 1).append((gated, b, h))
                        if b == 2:
                            after_half(events, l, f"P{b}", 1).append((merged_low, h))
                for h in range(2):
                    after_half(events, l, f"O{h}", 1).append((residual, h))
                split_stage(low_half, first_split[l], 18, events, 3)
                end_stage(dve, "dve")
                v(norm(l, 1, "norm_ffn"))
                end_stage(dve, "dve")
                if l == 0:
                    for i in range(2):
                        dve.wait_ge(S("fx_hi"), i + 1)
                        q = slice(4 * i, 4 * i + 4)
                        tt(XL[:, q, 1:T + 1], xn[:, q, 1:T + 1], FXH[:, q, :].bitcast(F32), ALU.subtract).then_inc(S("fx_lo"), 1)

                    def hidden(f):
                        dve.wait_ge(S("w_used"), split_half[(0, f"DU{f}")] + 2)
                        dve.wait_ge(S("f_s"), f + 1)
                        q = 4 * (f % 4)
                        tt(HF[:, q:q + 4, :], SF[:, :, :], PS[:, 4:8, 0:T], ALU.mult).then_inc(S("f_h"), 1)

                    def hidden_low(f):
                        q = 4 * (f % 4)
                        dve.wait_ge(S("f_hi"), f + 1)
                        tt(FHL[:, q:q + 4, :], HF[:, q:q + 4, :], FHH[:, q:q + 4, :].bitcast(F32), ALU.subtract).then_inc(S("f_lo"), 1)

                    def down(last, h):
                        q = slice(4 * h, 4 * h + 4)
                        dve.wait_ge(S("w_used"), split_half[(0, f"DD{last}")] + 2)
                        tt(hT[:, q, :], hT[:, q, :], PS[:, q, 0:T], ALU.add).then_inc(S("f_acc"), 1)

                    events = {}
                    for f in range(FG):
                        after_half(events, l, f"DU{f}", 1).append((hidden, f))
                        after_half(events, l, f"DU{f}", 1).append((hidden_low, f))
                    for block in DENSE_BLOCKS:
                        for h in range(2):
                            after_half(events, l, f"DD{block[-1]}", 1).append((down, block[-1], h))
                    split_stage(low_half, first_split["dense"], 6 * FG, events)
                    end_stage(dve, "dve")

            dve.wait_ge(S("q_log"), 1)
            idx = MR[:, 96:112].bitcast(U32)
            v(dve.tensor_copy(MR[:, 0:16], PS[:, 0, 0:16]))
            for t in range(2):
                v(dve.max(MR[:, 112 + 8 * t:120 + 8 * t], MR[:, 8 * t:8 * t + 8]))
                v(dve.max_index(idx[:, 8 * t:8 * t + 8], MR[:, 112 + 8 * t:120 + 8 * t], MR[:, 8 * t:8 * t + 8]))
            v(dve.tensor_copy(MR[:, 128:144], idx))
            for t in range(2):
                v(tt(MR[:, 176 + t:177 + t], MR[:, 113 + 8 * t:114 + 8 * t], MR[:, 112 + 8 * t:113 + 8 * t], ALU.subtract))
            dve.memset(small[:, 63:64], 0.0).then_inc(S("q_gap"), 1)
            dve.wait_ge(S("q_exp"), 1)
            v(dve.tensor_scalar(MR[:, 178:180], MR[:, 176:178], 1.0, None, ALU.add))
            v(dve.reciprocal(MR[:, 178:180], MR[:, 178:180]))
            v(tt(MR[:, 180:182], MR[:, 176:178], MR[:, 178:180], ALU.mult))
            for t in range(2):
                sel, gate = MR[:, 16 + 8 * t:24 + 8 * t], MR[:, 32 + 8 * t:40 + 8 * t]
                one, two = MR[:, 48:56], MR[:, 56:64]
                v(dve.tensor_scalar(one, C("iota8"), MR[:, 128 + 8 * t:129 + 8 * t], None, ALU.is_equal))
                v(dve.tensor_scalar(two, C("iota8"), MR[:, 129 + 8 * t:130 + 8 * t], None, ALU.is_equal))
                v(tt(sel, one, two, ALU.add))
                v(dve.tensor_scalar(one, one, MR[:, 178 + t:179 + t], None, ALU.mult))
                v(dve.scalar_tensor_tensor(gate, two, MR[:, 180 + t:181 + t], one, ALU.mult, ALU.add))
            dve.memset(small[:, 63:64], 0.0).then_inc(S("q_sel"), 1)
            dve.wait_ge(S("q_rank"), 1)
            v(dve.memset(MR[:, 64:82], -1.0))
            for t in range(2):
                slot = MR[:, 64 + 9 * t:72 + 9 * t]
                v(dve.scalar_tensor_tensor(slot, PS[:, 5, 8 * t:8 * t + 8], 1.0, MR[:, 16 + 8 * t:24 + 8 * t], ALU.add, ALU.mult))
                v(dve.tensor_scalar(slot, slot, -1.0, None, ALU.add))
            v(dve.tensor_reduce(small[:, 41:42], PS[:, 5, 16:24], AX.X, ALU.max))
            dve.tensor_scalar(small[:, 40:41].bitcast(I32), small[:, 41:42], float(SLOTS), None, ALU.is_gt).then_inc(S("route_flag"), 1)
            dve.wait_ge(S("route_flag"), 1)
            end_stage(dve, "dve")

            slots = MR[:, 64:64 + 2 * (NE + 1)].rearrange("p (t e) -> p t e", t=2)
            gates = MR[:, 32:48].rearrange("p (t e) -> p t e", t=2)

            def v_e(wait_for, ins):
                ins.then_inc(S("e_chain"), 1)
                dve.wait_ge(S("e_chain"), wait_for)

            def expert_low(n, j):
                half = j % 2
                dve.wait_ge(S("w_hi"), n * HALVES + (j + 1 + BASE))
                tt(WL[(BASE + j) % 3][:, 0:lows], ring[(MOE0 + j // 2) % RING][:, 2048 * half:2048 * half + lows],
                   WH[(BASE + j) % 3][:, 0:lows].bitcast(F32), ALU.subtract).then_inc(S("w_lo_dve"), 1)

            def expert_hidden(dve, e, n, run, last):
                steps = 4

                def link_e(i, ins):
                    v_e(n * steps + (i + 1), ins)

                dve.memset(small[:, 59:60], 0.0).then_inc(S("e_free"), 1)
                link_e(0, dve.tensor_copy(MR[:, 164:166], gates[:, :, bass.ds(e, 1)]))
                link_e(1, dve.tensor_copy(MR[:, 160:162], slots[:, :, bass.ds(e, 1)]))
                for t in range(2):
                    ins = dve.tensor_scalar(SEL[:, 2 + t, :], C("iota", 0, SLOTS), MR[:, 160 + t:161 + t], MR[:, 164 + t:165 + t],
                                            ALU.is_equal, ALU.mult)
                ins.then_inc(S("e_selg"), 1)
                link_e(2, dve.tensor_copy(MR[:, 162:164], slots[:, :, bass.ds(e + 1, 1)]))
                dve.wait_ge(S("e_xg"), n + run + 1)
                select_next(S("e_sel"))

                def hidden(f):
                    dve.wait_ge(S("w_used"), used(n, "u", f))
                    dve.wait_ge(S("e_s"), n * FG + (f + 1))
                    tt(MH[:, :], MS[:, :], PS[:, 2 * (f % 2) + 1, :], ALU.mult).then_inc(S("e_h"), 1)

                def hidden_low(f):
                    dve.wait_ge(S("e_hth"), n * FG + (f + 1))
                    tt(HTL[f % 2][:, :], PS[:, 6, :], HTH[f % 2][:, :].bitcast(F32), ALU.subtract).then_inc(S("e_htl"), 1)

                events = {}
                for f in range(FG):
                    at_half(events, "u", f, 1, 2).append((hidden, f))
                    at_half(events, "u", f, 1, 5 if f < FG - 1 else 3).append((hidden_low, f))
                for j in range(3, HALVES):
                    expert_low(n, j)
                    for do, f in events.get(j, []):
                        do(f)
                gathered_low(n + run + 2)
                if not last:
                    for j in range(3):
                        expert_low(n + 1, j)
                dve.wait_ge(S("e_sc"), n + 1)
                halves = lambda x_: x_.rearrange("p (a b) n -> p a b n", b=2)
                for i, b in enumerate((2, 6)):
                    o = halves(hT[:, 4 * i:4 * i + 4, META:T])
                    ins = tt(o, o, PS[:, b:b + 2, :].rearrange("p a (b n) -> p a b n", b=2), ALU.add)
                link_e(3, ins)

            def gathered_low(wait_for):
                dve.wait_ge(S("e_xgh"), wait_for)
                tt(XGL[:, :].rearrange("p (a b) -> p a b", a=2), PS[:, 2:4, :], XGH[:, :].bitcast(F32).rearrange("p (a b) -> p a b", a=2),
                   ALU.subtract).then_inc(S("e_xgl"), 1)

            def select_next(sem):
                for t in range(2):
                    ins = dve.tensor_scalar(SEL[:, t, :], C("iota", 0, SLOTS), MR[:, 162 + t:163 + t], None, ALU.is_equal)
                ins.then_inc(sem, 1)

            def first_select(dve, run):
                if not (isinstance(run, int) and run == 0):
                    ins = dve.tensor_scalar(slots, slots, -float(SLOTS), None, ALU.add)
                    ins.then_inc(S("p_chain"), 1)
                    dve.wait_ge(S("p_chain"), run * 2)
                dve.tensor_copy(MR[:, 162:164], slots[:, :, 0]).then_inc(S("p_chain"), 1)
                dve.wait_ge(S("p_chain"), run * 2 + 1)
                select_next(S("e_sel"))
                for j in range(3):
                    expert_low(run * NE, j)
                gathered_low(run * (NE + 1) + 1)

            for_all_experts(dve, expert_hidden, first_select)
            end_stage(dve, "dve")
            norm(DEPTH, 0, "norm_final").then_inc(S("fin"), 1)

    return nc


def constant_array():
    c = np.zeros((P, NCONST), np.float32)

    def put(name, v):
        o, w = CONST_COLS[name]
        assert v.shape[1] == w
        c[:v.shape[0], o:o + w] = v

    i = np.arange(P)
    row, col = i[:, None], i[None, :]
    head = (row // HD) == (col // HD)
    put("ident", row == col)
    put("ones", np.ones((P, P)))
    put("headones", head)
    put("negsuffix", -1.0 * (row >= col))
    put("negones", -np.ones((P, P)))
    put("negmask", -1e30 * (row >= col))
    put("before", row < col)
    sb = np.ones((P, 432))
    sb[:, 0:P] = row < col
    sb[:, T:T + P] = row < col
    sb[:, 416:432] = (row < col)[:, 0:16]
    put("sbmask", sb)
    rs, cs = row % CH, col % CH
    level = []
    for v in range(6):
        b = 1 << v
        level.append(head & (rs // (2 * b) == cs // (2 * b)) & (rs // b % 2 == 0) & (cs // b % 2 == 1))
    put("level", np.concatenate(level, 1))
    put("strict", head & (rs < cs))
    put("bd", head)
    put("incl", (row % CH) <= np.arange(CH)[None, :])
    put("stack", (row % CH) == np.arange(CH)[None, :])
    put("reset", np.tile((np.arange(TP) % CH != 0)[None], (P, 1)))
    put("iota", np.tile(np.arange(2 * P)[None], (P, 1)))
    put("iota8", np.tile(np.arange(NE)[None], (P, 1)))
    n = np.maximum(LINE_TOP - np.arange(LINE), 0)
    large = 16 + (np.log(np.maximum(n, 1).astype(np.float32) / np.float32(16)) / np.float32(np.log(8.0)) * np.float32(16)).astype(np.int32)
    bucket = np.where(n < 16, n, np.minimum(large, NBUCKET - 1))
    put("bucket", np.arange(NBUCKET)[:, None] == bucket[None])
    return c


def parameter_array(a):
    out = np.zeros((DEPTH, P, NPARAM), np.float32)
    for l in range(DEPTH):
        def put(name, v):
            o, w = PARAM_COLS[name]
            out[l, :v.shape[0], o:o + w] = v

        tiles = lambda v: np.asarray(v).reshape(-1, P).T
        mu = np.asarray(a["tshift_mu"][l])
        b = COL_R
        put("norm_mix", tiles(a["norm_mix"][l]))
        put("norm_ffn", tiles(a["norm_ffn"][l]))
        put("mu_r", tiles(mu[0:512]))
        put("mu_k", tiles(mu[COL_K - b:COL_K - b + 512]))
        put("mu_v", tiles(mu[COL_V - b:COL_V - b + 512]))
        put("mu_wa", np.concatenate([mu[COL_W - b:COL_W - b + 64], mu[COL_A - b:COL_A - b + 64]])[:, None])
        put("mu_g0", mu[COL_G - b:COL_G - b + P][:, None])
        put("mu_g1", mu[COL_G - b + P:COL_G - b + P + 32][:, None])
        for n, k in (("w0", "rwkv_w0"), ("a0", "rwkv_a0"), ("k_k", "rwkv_k_k"), ("k_a", "rwkv_k_a"), ("r_k", "rwkv_r_k"),
                     ("ln_g", "rwkv_ln_g"), ("ln_b", "rwkv_ln_b")):
            put(n, tiles(np.asarray(a[k][l]).reshape(-1)))
        if l:
            put("vres_mu", tiles(a["vres_mu"][l - 1]))
            put("vres_b", tiles(a["vres_b"][l - 1]))
        sinks = np.asarray(a["sinks"][l])
        put("sink", np.repeat(sinks.reshape(4, 2).T, 64, axis=0))
        put("sink_meta", np.repeat(sinks.reshape(2, 4).T, META, axis=0))
        put("norm_final", tiles(a["norm_final"]))
    return out


_PLAIN = ["x", "meta_tokens", "w_in", "w_proj_a", "w_proj_b", "w_proj_c", "w_out", "dense_w_gate", "dense_w_up", "dense_w_down",
          "moe_router", "moe_w_gate", "moe_w_up", "moe_w_down", "rwkv_w2", "rwkv_a2", "rwkv_g2", "vres_w1", "vres_w2", "rel_bias"]


def kernel(**inputs):
    import concourse.bacc as bacc
    from concourse.bass_utils import run_bass_kernel_spmd

    nc = bacc.Bacc("TRN2", target_bir_lowering=False, num_devices=1)
    arrays, args = {}, []
    given = [(n, np.ascontiguousarray(inputs[n])) for n in _PLAIN]
    given += [("consts", constant_array()), ("params", parameter_array(inputs))]
    for name, a in given:
        arrays[f"in_{name}"] = a
        args.append(nc.dram_tensor(f"in_{name}", a.shape, mybir.dt.from_np(a.dtype), kind="ExternalInput").ap())
    args.append(nc.dram_tensor("out_0", (1, SEQ, D), F32, kind="ExternalOutput").ap())
    build_trunk(nc, *args)
    r = run_bass_kernel_spmd(nc, [arrays], core_ids=[0])
    return r.results[0]["out_0"]
```
